# Optimizing a Trainium2 kernel written in Bass

```python
import jax, jax.numpy as jnp
from jax import lax
import numpy as np

D_MODEL = 1024
BATCH = 1
SEQ = 512
DEPTH = 1

HEAD_DIM = 64
ROPE_THETA = 10000.0
RMS_EPS = 1e-6
NEG_BIG = -1e30

SWA_HEADS = 8
SWA_KV_HEADS = 2
SWA_WINDOW = 128
SWA_BLOCK = 128

NSA_HEADS = 8
NSA_KV_HEADS = 2
CMP_LEN = 32
CMP_STRIDE = 16
CMP_HIDDEN = 256
SEL_BLOCK = 64
SEL_TOPN = 16
SEL_QCHUNK = 64
NSA_WINDOW = 512
NSA_BLOCK = 128
NSA_N_GATES = 3

KV_W = HEAD_DIM * SWA_KV_HEADS
NKV_W = HEAD_DIM * NSA_KV_HEADS
SPLIT_SIZES = (
    SWA_HEADS * HEAD_DIM, KV_W, KV_W,
    NSA_HEADS * HEAD_DIM,
    NKV_W, NKV_W, NKV_W, NKV_W, NKV_W, NKV_W,
    NSA_HEADS * NSA_N_GATES,
)
IN_WIDTH = sum(SPLIT_SIZES)
MIX_WIDTH = (SWA_HEADS + NSA_HEADS) * HEAD_DIM

PEER_HEADS = 8
N_KEYS = 128
N_EXPERTS = N_KEYS * N_KEYS
PEER_QDIM = 256
PEER_TOPK = 16
PEER_CHUNK = 128

kernel_name = "hymba_swa_sink_nsa_peer_block"

def rmsnorm(x, g):
    xf = x.astype(jnp.float32)
    y = xf * lax.rsqrt(jnp.mean(xf * xf, axis=-1, keepdims=True) + RMS_EPS)
    return (y * g.astype(jnp.float32)).astype(x.dtype)

def rope(x, positions):
    half = HEAD_DIM // 2
    inv_freq = ROPE_THETA ** (-jnp.arange(half, dtype=jnp.float32) / half)
    ang = positions.astype(jnp.float32)[..., None] * inv_freq
    cos = jnp.cos(ang)[:, :, None, :]
    sin = jnp.sin(ang)[:, :, None, :]
    xf = x.astype(jnp.float32)
    x1, x2 = xf[..., :half], xf[..., half:]
    return jnp.concatenate([x1 * cos - x2 * sin, x2 * cos + x1 * sin], axis=-1).astype(x.dtype)

def banded_gqa_attention(q, k, v, window, block, sinks=None):
    B, T, H, dh = q.shape
    Hkv = k.shape[2]
    G = H // Hkv
    nb = T // block
    nprev = -(-(window - 1) // block)
    span = (nprev + 1) * block
    pad = ((0, 0), (nprev * block, 0), (0, 0), (0, 0))
    kp = jnp.pad(k, pad)
    vp = jnp.pad(v, pad)
    kidx = (jnp.arange(nb) * block)[:, None] + jnp.arange(span)[None, :]
    kb = kp[:, kidx]
    vb = vp[:, kidx]
    qb = q.reshape(B, nb, block, Hkv, G, dh)
    s = jnp.einsum('bnqhgd,bnkhd->bnhgqk', qb, kb).astype(jnp.float32) * (dh ** -0.5)
    qpos = (jnp.arange(nb) * block)[:, None] + jnp.arange(block)[None, :]
    kpos = kidx - nprev * block
    diff = qpos[:, :, None] - kpos[:, None, :]
    mask = (diff >= 0) & (diff < window) & (kpos[:, None, :] >= 0)
    s = jnp.where(mask[None, :, None, None], s, -jnp.inf)
    if sinks is None:
        p = jax.nn.softmax(s, axis=-1)
    else:
        sink = sinks.astype(jnp.float32).reshape(Hkv, G)[None, None, :, :, None, None]
        sink = jnp.broadcast_to(sink, s.shape[:-1] + (1,))
        p = jax.nn.softmax(jnp.concatenate([s, sink], axis=-1), axis=-1)[..., :-1]
    o = jnp.einsum('bnhgqk,bnkhd->bnqhgd', p.astype(v.dtype), vb)
    return o.reshape(B, T, H, dh)

def compress_blocks(kv, pos_emb, w1, w2):
    B, T, Hkv, dh = kv.shape
    nc = (T - CMP_LEN) // CMP_STRIDE + 1
    idx = (jnp.arange(nc) * CMP_STRIDE)[:, None] + jnp.arange(CMP_LEN)[None, :]
    blocks = kv[:, idx] + pos_emb[None, None, :, None, :]
    flat = blocks.transpose(0, 1, 3, 2, 4).reshape(B, nc, Hkv, CMP_LEN * dh)
    return jax.nn.gelu(flat @ w1, approximate=False) @ w2

def nsa_compressed_attention(q5, k_cmp, v_cmp):
    T = q5.shape[1]
    nc = k_cmp.shape[1]
    s = jnp.einsum('bthgd,bchd->bhgtc', q5, k_cmp).astype(jnp.float32) * (HEAD_DIM ** -0.5)
    vis = (jnp.arange(nc) * CMP_STRIDE + CMP_LEN - 1)[None, :] <= jnp.arange(T)[:, None]
    p = jnp.where(vis, jax.nn.softmax(jnp.where(vis, s, NEG_BIG), axis=-1), 0.0)
    o = jnp.einsum('bhgtc,bchd->bthgd', p.astype(v_cmp.dtype), v_cmp)
    return o, p

def nsa_select_blocks(p_cmp, T):
    nc = p_cmp.shape[-1]
    ns = T // SEL_BLOCK
    n_sel = min(SEL_TOPN, ns)
    cstart = jnp.arange(nc) * CMP_STRIDE
    bstart = jnp.arange(ns) * SEL_BLOCK
    lo = jnp.maximum(cstart[:, None], bstart[None, :])
    hi = jnp.minimum(cstart[:, None] + CMP_LEN, bstart[None, :] + SEL_BLOCK)
    overlap = jnp.clip(hi - lo, 0).astype(jnp.float32) / CMP_LEN
    imp = jnp.einsum('bhgtc,cj->bhtj', p_cmp, overlap)
    t = jnp.arange(T)[:, None]
    j = jnp.arange(ns)[None, :]
    cur = t // SEL_BLOCK
    valid = j * SEL_BLOCK <= t
    forced = (j == 0) | (j == cur) | (j == cur - 1)
    score = jnp.where(forced, jnp.inf, jnp.where(valid, imp, -jnp.inf))
    top, idx = lax.top_k(score, n_sel)
    return idx, top > -jnp.inf

def nsa_selected_attention(q5, k_sel, v_sel, sel_idx, sel_valid):
    B, T, Hkv, G, dh = q5.shape
    ns = T // SEL_BLOCK
    n_sel = sel_idx.shape[-1]
    C = SEL_QCHUNK
    nq = T // C
    kb = k_sel.reshape(B, ns, SEL_BLOCK, Hkv, dh).transpose(0, 3, 1, 2, 4)
    vb = v_sel.reshape(B, ns, SEL_BLOCK, Hkv, dh).transpose(0, 3, 1, 2, 4)
    qc = q5.reshape(B, nq, C, Hkv, G, dh).transpose(1, 0, 3, 4, 2, 5)
    ic = sel_idx.reshape(B, Hkv, nq, C, n_sel).transpose(2, 0, 1, 3, 4)
    vc = sel_valid.reshape(B, Hkv, nq, C, n_sel).transpose(2, 0, 1, 3, 4)
    t0 = jnp.arange(nq) * C
    bi = jnp.arange(B)[:, None, None, None]
    hi = jnp.arange(Hkv)[None, :, None, None]

    def step(args):
        q_c, i_c, v_c, start = args
        kg = kb[bi, hi, i_c]
        vg = vb[bi, hi, i_c]
        s = jnp.einsum('bhgqd,bhqnkd->bhgqnk', q_c, kg).astype(jnp.float32) * (dh ** -0.5)
        kpos = i_c[..., None] * SEL_BLOCK + jnp.arange(SEL_BLOCK)
        qpos = start + jnp.arange(C)
        mask = (kpos <= qpos[None, None, :, None, None]) & v_c[..., None]
        s = jnp.where(mask[:, :, None], s, -jnp.inf)
        p = jax.nn.softmax(s.reshape(B, Hkv, G, C, n_sel * SEL_BLOCK), axis=-1)
        p = p.reshape(B, Hkv, G, C, n_sel, SEL_BLOCK)
        return jnp.einsum('bhgqnk,bhqnkd->bqhgd', p.astype(vg.dtype), vg)

    out = lax.map(step, (qc, ic, vc, t0))
    return out.transpose(1, 0, 2, 3, 4, 5).reshape(B, T, Hkv, G, dh)

def peer_ffn(h, w_query, sub_keys_1, sub_keys_2, expert_down, expert_up):
    B, T, D = h.shape
    N = B * T
    ht = h.reshape(N, D)
    q = (ht @ w_query).reshape(N, PEER_HEADS, 2, PEER_QDIM // 2)
    s1 = jnp.einsum('nhd,kd->nhk', q[:, :, 0], sub_keys_1)
    s2 = jnp.einsum('nhd,kd->nhk', q[:, :, 1], sub_keys_2)
    t1, i1 = lax.top_k(s1, PEER_TOPK)
    t2, i2 = lax.top_k(s2, PEER_TOPK)
    cand = (t1[..., :, None] + t2[..., None, :]).reshape(N, PEER_HEADS, PEER_TOPK * PEER_TOPK)
    cidx = (i1[..., :, None] * N_KEYS + i2[..., None, :]).reshape(N, PEER_HEADS, PEER_TOPK * PEER_TOPK)
    sc, pos = lax.top_k(cand, PEER_TOPK)
    eidx = jnp.take_along_axis(cidx, pos, axis=-1)
    gate = jax.nn.softmax(sc.astype(jnp.float32), axis=-1).astype(h.dtype)
    nchunk = N // PEER_CHUNK

    def step(args):
        x_c, e_c, g_c = args
        u = expert_down[e_c]
        a = jax.nn.gelu(jnp.einsum('cd,chkd->chk', x_c, u), approximate=False)
        vv = expert_up[e_c]
        return jnp.einsum('chk,chkd->cd', g_c * a, vv)

    out = lax.map(step, (ht.reshape(nchunk, PEER_CHUNK, D),
                         eidx.reshape(nchunk, PEER_CHUNK, PEER_HEADS, PEER_TOPK),
                         gate.reshape(nchunk, PEER_CHUNK, PEER_HEADS, PEER_TOPK)))
    return out.reshape(B, T, D)

def hybrid_layer(x, positions, norm_attn, w_in, attn_sinks,
                 cmp_k_pos, cmp_k_w1, cmp_k_w2, cmp_v_pos, cmp_v_w1, cmp_v_w2,
                 w_out, norm_ffn, peer_w_query, peer_sub_keys_1, peer_sub_keys_2,
                 peer_expert_down, peer_expert_up):
    B, T, _ = x.shape
    h = rmsnorm(x, norm_attn)
    proj = h @ w_in
    offsets = np.cumsum(SPLIT_SIZES)[:-1].tolist()
    qa, ka, va, qb, kc, vc, ks, vs, kw, vw, gl = jnp.split(proj, offsets, axis=-1)
    hd = lambda t, n: t.reshape(B, T, n, HEAD_DIM)

    qa = rope(hd(qa, SWA_HEADS), positions)
    ka = rope(hd(ka, SWA_KV_HEADS), positions)
    o_a = banded_gqa_attention(qa, ka, hd(va, SWA_KV_HEADS), SWA_WINDOW, SWA_BLOCK, attn_sinks)

    G = NSA_HEADS // NSA_KV_HEADS
    qb = rope(hd(qb, NSA_HEADS), positions)
    q5 = qb.reshape(B, T, NSA_KV_HEADS, G, HEAD_DIM)
    k_cmp = compress_blocks(rope(hd(kc, NSA_KV_HEADS), positions), cmp_k_pos, cmp_k_w1, cmp_k_w2)
    v_cmp = compress_blocks(hd(vc, NSA_KV_HEADS), cmp_v_pos, cmp_v_w1, cmp_v_w2)
    o_cmp, p_cmp = nsa_compressed_attention(q5, k_cmp, v_cmp)
    sel_idx, sel_valid = nsa_select_blocks(p_cmp, T)
    o_sel = nsa_selected_attention(q5, rope(hd(ks, NSA_KV_HEADS), positions),
                                   hd(vs, NSA_KV_HEADS), sel_idx, sel_valid)
    o_win = banded_gqa_attention(qb, rope(hd(kw, NSA_KV_HEADS), positions),
                                 hd(vw, NSA_KV_HEADS), NSA_WINDOW, NSA_BLOCK)
    gates = jax.nn.sigmoid(gl.astype(jnp.float32)).astype(x.dtype).reshape(B, T, NSA_HEADS, NSA_N_GATES)
    o_b = (gates[..., 0:1] * o_cmp.reshape(B, T, NSA_HEADS, HEAD_DIM)
           + gates[..., 1:2] * o_sel.reshape(B, T, NSA_HEADS, HEAD_DIM)
           + gates[..., 2:3] * o_win)

    mixed = jnp.concatenate([o_a.reshape(B, T, -1), o_b.reshape(B, T, -1)], axis=-1)
    x = x + mixed @ w_out
    x = x + peer_ffn(rmsnorm(x, norm_ffn), peer_w_query, peer_sub_keys_1, peer_sub_keys_2,
                     peer_expert_down, peer_expert_up)
    return x

def setup_inputs(seed: int = 0) -> dict:
    key = jax.random.key(seed)
    ks = jax.random.split(key, 20)
    f32 = jnp.float32
    nrm = lambda k, shape, scale: jax.random.normal(k, shape, f32) * scale
    L = DEPTH
    return {
        "x": nrm(ks[0], (BATCH, SEQ, D_MODEL), 1.0),
        "positions": jnp.broadcast_to(jnp.arange(SEQ, dtype=jnp.int32)[None, :], (BATCH, SEQ)),
        "norm_attn": 1.0 + nrm(ks[1], (L, D_MODEL), 0.02),
        "w_in": nrm(ks[2], (L, D_MODEL, IN_WIDTH), D_MODEL ** -0.5),
        "attn_sinks": nrm(ks[3], (L, SWA_HEADS), 0.5),
        "cmp_k_pos": nrm(ks[4], (L, CMP_LEN, HEAD_DIM), 0.1),
        "cmp_k_w1": nrm(ks[5], (L, CMP_LEN * HEAD_DIM, CMP_HIDDEN), (CMP_LEN * HEAD_DIM) ** -0.5),
        "cmp_k_w2": nrm(ks[6], (L, CMP_HIDDEN, HEAD_DIM), CMP_HIDDEN ** -0.5),
        "cmp_v_pos": nrm(ks[7], (L, CMP_LEN, HEAD_DIM), 0.1),
        "cmp_v_w1": nrm(ks[8], (L, CMP_LEN * HEAD_DIM, CMP_HIDDEN), (CMP_LEN * HEAD_DIM) ** -0.5),
        "cmp_v_w2": nrm(ks[9], (L, CMP_HIDDEN, HEAD_DIM), CMP_HIDDEN ** -0.5),
        "w_out": nrm(ks[10], (L, MIX_WIDTH, D_MODEL), MIX_WIDTH ** -0.5),
        "norm_ffn": 1.0 + nrm(ks[11], (L, D_MODEL), 0.02),
        "peer_w_query": nrm(ks[12], (L, D_MODEL, PEER_HEADS * PEER_QDIM), D_MODEL ** -0.5),
        "peer_sub_keys_1": nrm(ks[13], (L, N_KEYS, PEER_QDIM // 2), (PEER_QDIM // 2) ** -0.5),
        "peer_sub_keys_2": nrm(ks[14], (L, N_KEYS, PEER_QDIM // 2), (PEER_QDIM // 2) ** -0.5),
        "peer_expert_down": nrm(ks[15], (L, N_EXPERTS, D_MODEL), D_MODEL ** -0.5),
        "peer_expert_up": nrm(ks[16], (L, N_EXPERTS, D_MODEL), 0.5),
        "norm_f": 1.0 + nrm(ks[17], (D_MODEL,), 0.02),
    }

def reference(x, positions, norm_attn, w_in, attn_sinks, cmp_k_pos, cmp_k_w1, cmp_k_w2,
              cmp_v_pos, cmp_v_w1, cmp_v_w2, w_out, norm_ffn, peer_w_query,
              peer_sub_keys_1, peer_sub_keys_2, peer_expert_down, peer_expert_up, norm_f):
    h = x
    for layer in range(DEPTH):
        h = hybrid_layer(h, positions, norm_attn[layer], w_in[layer], attn_sinks[layer],
                         cmp_k_pos[layer], cmp_k_w1[layer], cmp_k_w2[layer],
                         cmp_v_pos[layer], cmp_v_w1[layer], cmp_v_w2[layer],
                         w_out[layer], norm_ffn[layer], peer_w_query[layer],
                         peer_sub_keys_1[layer], peer_sub_keys_2[layer],
                         peer_expert_down[layer], peer_expert_up[layer])
    return rmsnorm(h, norm_f)


_drawn_inputs = setup_inputs


def setup_inputs(seed=0):
    import zlib

    import numpy as np

    out = dict(_drawn_inputs(seed))
    spreads = {}
    factors = {'norm_attn': 2.812,
     'attn_sinks': 18.427,
     'cmp_k_pos': 4.063,
     'norm_f': 8.254,
     'cmp_v_pos': 3.284,
     'norm_ffn': 3.609}
    for name, (base, spread) in spreads.items():
        noise = np.random.default_rng([zlib.crc32(name.encode()), seed]).standard_normal(out[name].shape)
        drawn = base * np.exp(spread * noise) if base else spread * noise
        out[name] = __import__('jax').numpy.asarray(drawn.astype(out[name].dtype))
    for name, factor in factors.items():
        out[name] = (out[name] * factor).astype(out[name].dtype)
    return out
```

```python
import concourse.bass as bass
from concourse import mybir
from concourse.alu_op_type import AluOpType as ALU
import numpy as np

F32, F32R, BF16 = mybir.dt.float32, mybir.dt.float32r, mybir.dt.bfloat16
U32, I32 = mybir.dt.uint32, mybir.dt.int32
ACT = mybir.ActivationFunctionType
X_AXIS = mybir.AxisListType.X

P = 128
T, D = 512, 1024
KC, TB = D // P, T // P
DH, HALF = 64, 32
HEADS, GROUPS = 8, 2
HPG = HEADS // GROUPS
COLS = 512
N_GATES = 3 * HEADS
CMP_LEN, CMP_STRIDE, CMP_HIDDEN = 32, 16, 256
NC = (T - CMP_LEN) // CMP_STRIDE + 1
CP = NC + 1
PH, NK, TOPK = 8, 128, 16
NEG = -1e30
EPS = 1e-6
TILES_IN, TILES_OUT, TILES_Q = 4, 2, 4
TILES = TILES_IN + TILES_OUT + TILES_Q
GC = 8
NG = NK // GC
GB = 4
NGB = NK // GB
TG = 32
NTG = T // TG
PSTEP = 4
DR = 4

TWO_PI = 2.0 * np.pi
PI_A = 6.28125
PI_B = float(np.float32(np.round((TWO_PI - PI_A) * 2.0 ** 19) / 2.0 ** 19))
PI_C = float(np.float32(TWO_PI - PI_A - PI_B))
ROUND = 1.5 * 2.0 ** 23
PI_CLAMP = float(np.nextafter(np.float32(np.pi), np.float32(0)))

SWA, SEL, WIN = range(3)
UNITS = [(qb, br, h) for qb in range(TB) for br in (SWA, SEL, WIN) for h in range(HEADS)]
K_OF = {SWA: 0, SEL: 2, WIN: 3}
STEP_QB = 3 * HEADS


def width(qb, br):
    return min(qb + 1, 2) * P if br == SWA else (qb + 1) * P


def tile_used(i):
    if i < TILES_IN:
        return "pj_done", TB * (i + 1)
    if i < TILES_IN + TILES_OUT:
        return "wo_ps", TB * (i - TILES_IN + 1)
    return "q_ps", 4 * (i - TILES_IN - TILES_OUT + 1)


def f32(ap):
    return ap.bitcast(F32)


def build(nc, x, pos, params, consts, consts_b, wts, wgate, w1, w2, subkeys, normf, down, up, y):
    at = [16512]

    def size(shape, dt):
        return int(np.prod(shape[1:])) * (2 if dt == BF16 else 4)

    def place(name, shape, dt, offset):
        return nc.alloc_sbuf_tensor_at(name, shape, dt, offset=offset)

    def sb(name, shape, dt=F32):
        t = place(name, shape, dt, at[0])
        at[0] += (size(shape, dt) + 31) // 32 * 32
        return t

    xt = sb("xt", [P, TB, D])
    h_hi = sb("h_hi", [P, KC, T], F32R)
    h_lo = sb("h_lo", [P, KC, T], F32R)
    cst = sb("cst", [P, 432])
    ident = cst[:, 0:P]
    cmp_neg = cst[:, 128:256].rearrange("p (q c) -> p q c", q=TB)
    cmp_vis = cst[:, 256:384].rearrange("p (q c) -> p q c", q=TB)
    inv_freq = cst[:, 384:416]
    iota16 = cst[:, 416:432]
    cstb = sb("cstb", [P, 384], BF16)
    ident_b, mask_b = cstb[:, 0:P], cstb[:, P:384]
    prm = sb("prm", [P, 96])
    g_attn, g_ffn, sinks = prm[:, 0:8], prm[:, 8:16], prm[:, 16:24]
    cmp_pos = prm[:, 32:96].rearrange("p (k l) -> p k l", k=2)
    posi = sb("posi", [P, TB], I32)
    posf = sb("posf", [P, TB])
    ssq = sb("ssq", [P, TB])
    ms = sb("ms", [P, TB])
    rt = sb("rt", [P, TB])
    rstd = sb("rstd", [P, TB])
    nt = sb("nt", [P, TB])
    base = at[0]

    w_raw = [sb(f"w_raw{i}", [P, KC, COLS]) for i in range(2)]
    w_lo = [place(f"w_lo{i}", [P, KC, COLS], F32R, base + i * 16384) for i in range(2)]
    w_hi = [sb(f"w_hi{i}", [P, KC, COLS], F32R) for i in range(2)]
    after_w = at[0]
    xs = sb("xs", [P, TB, D])
    mixed = xs
    qT = sb("qT", [P, 2, HPG, T])
    kT = sb("kT", [P, 4, T])
    vcT = sb("vcT", [P, T])
    vnat = sb("vnat", [P, TB, COLS])
    gates = sb("gates", [P, TB, HEADS, 3])
    gexp = sb("gexp", [P, TB, N_GATES])
    stage = at[0]
    wg_raw = sb("wg_raw", [P, KC, N_GATES])
    wg_lo = place("wg_lo", [P, KC, N_GATES], F32R, stage)
    wg_hi = sb("wg_hi", [P, KC, N_GATES], F32R)
    cos2 = sb("cos2", [P, TB, 2, HALF])
    sin2 = sb("sin2", [P, TB, 2, HALF])
    ang = sb("ang", [P, TB, HALF])
    trn = sb("trn", [P, TB, HALF])
    red = sb("red", [P, TB, HALF])
    red2 = sb("red2", [P, TB, HALF])
    rp_c = [sb(f"rp_c{i}", [P, COLS]) for i in range(2)]
    rp_s = [sb(f"rp_s{i}", [P, COLS]) for i in range(2)]
    roped = [sb(f"roped{i}", [P, COLS]) for i in range(2)]
    end_proj = at[0]
    at[0] = stage
    w1_sb = sb("w1_sb", [P, CMP_LEN, CMP_HIDDEN])
    end_w1 = at[0]
    at[0] = stage
    pr = [sb(f"pr{i}", [P, COLS]) for i in range(3)]
    pt = [sb(f"pt{i}", [P, COLS]) for i in range(2)]
    o_tmp = sb("o_tmp", [P, COLS])
    c_sc = sb("c_sc", [P, HEADS, CP])
    c_pT = sb("c_pT", [P, GROUPS, P])
    assert at[0] <= end_w1
    at[0] = max(end_proj, end_w1)
    cx = [place(f"cx{i}", [P, CMP_LEN, NC], F32, after_w + i * 4096) for i in range(2)]
    hid = [sb(f"hid{i}", [P, GROUPS * 2, CP]) for i in range(2)]
    hrep = place("hrep", [P, GROUPS * 2, 4, CP], F32, after_w + 2 * 4096)
    w2_sb = sb("w2_sb", [P, 2, 2, DH])
    kcT = sb("kcT", [P, CP])
    vbd = sb("vbd", [P, GROUPS, 4, DH])
    nmax = sb("nmax", [P, len(UNITS)])
    rsum = sb("rsum", [P, len(UNITS)])
    nsink = sb("nsink", [P, HEADS])
    es_in = sb("es_in", [P, TB, HEADS])
    es = sb("es", [P, TB, HEADS])
    coef = sb("coef", [P, HEADS])
    c_max = sb("c_max", [P, HEADS])
    c_sum = sb("c_sum", [P, HEADS])
    c_coef = sb("c_coef", [P, HEADS])
    assert at[0] <= 229368, at[0]

    at[0] = after_w + 16384
    q_sb = [sb(f"q_sb{i}", [P, T]) for i in range(2)]
    sk = sb("sk", [P, 2, NK])
    work = [sb(f"work{i}", [P, TB, NK]) for i in range(2)]
    tv = [[sb(f"tv{r}{s}", [P, TB, TOPK]) for s in range(2)] for r in range(2)]
    ti = [[sb(f"ti{r}{s}", [P, TB, TOPK], U32) for s in range(2)] for r in range(2)]
    tif = [[sb(f"tif{r}{s}", [P, TB, TOPK]) for s in range(2)] for r in range(2)]
    cand = sb("cand", [P, TB, TOPK, TOPK])
    candw = sb("candw", [P, TB, TOPK * TOPK])
    posn = sb("posn", [P, TB, TOPK], U32)
    pab = [[sb(f"pab{r}{s}", [P, TB, TOPK], U32) for s in range(2)] for r in range(2)]
    hit = [[sb(f"hit{r}{s}", [P, TB, TOPK, TOPK]) for s in range(2)] for r in range(2)]
    score = sb("score", [P, TB, PH, TOPK])
    key = [sb(f"key{s}", [P, TB, PH, TOPK]) for s in range(2)]
    g_sum = sb("g_sum", [P, TB, PH])
    slots = at[0]
    sl_key = [sb(f"sl_key{s}", [P, T], BF16) for s in range(2)]
    sl_g = [sb(f"sl_g{i}", [P, T], BF16) for i in range(3)]
    sl_r = [sb(f"sl_r{i}", [P, T]) for i in range(2)]
    assert at[0] <= 229368, at[0]

    at[0] = base
    iota_k = sb("iota_k", [P, NK, TG], BF16)
    oh = [[sb(f"oh{r}{i}", [P, NK, TG], BF16) for i in range(2)] for r in range(2)]
    gp = [[sb(f"gp{r}{i}", [P, NK, TG], BF16) for i in range(3)] for r in range(2)]
    ev = [sb(f"ev{i}", [P, NGB, TG, GB]) for i in range(2)]
    assert at[0] <= slots, (at[0], slots)

    at[0] = base
    d_raw = sb("d_raw", [P, DR, KC, P])
    d_lo = place("d_lo", [P, DR, KC, P], F32R, base)
    d_hi = sb("d_hi", [P, 2, KC, P], F32R)
    u_raw = sb("u_raw", [P, DR, D])
    u_hi = sb("u_hi", [P, GC, D], F32R)
    u_lo = sb("u_lo", [P, GC, D], F32R)
    w_e_hi = sb("w_e_hi", [P, GC, T], F32R)
    w_e_lo = sb("w_e_lo", [P, GC, T], F32R)
    g_sb = sb("g_sb", [P, 2, T, GB])
    a_sb = sb("a_sb", [P, 2, T])
    assert at[0] <= 229368, at[0]
    nf = place("nf", [P, D], F32, base)
    junk = place("junk", [P, D], F32, after_w + 16384)

    gates_dram = nc.dram_tensor("gates_dram", (NGB, P, T * GB), F32, kind="Internal").ap()

    bank = [nc.alloc_psum_tensor(f"bank{i}", [P, 512], F32) for i in range(8)]
    sems = {}

    def S(name):
        if name not in sems:
            sems[name] = nc.alloc_semaphore(name)
        return sems[name]

    x_v = x.rearrange("(b p) d -> b p d", p=P)
    y_v = y.rearrange("(b p) d -> b p d", p=P)

    with nc.Block() as block:

        @block.sync
        def _(sp):
            for b in range(TB):
                sp.dma_start(xt[:, b], x_v[b]).then_inc(S(f"x_loaded{b}"), 16)
            sp.dma_start(cst[:], consts).then_inc(S("const_loaded"), 16)
            sp.dma_start(prm[:], params).then_inc(S("const_loaded"), 16)
            sp.dma_start(posi[:], pos).then_inc(S("const_loaded"), 16)
            sp.dma_start(cstb[:], consts_b[:, 0:384]).then_inc(S("const_loaded"), 16)
            sp.dma_start(wg_raw[:], wgate.rearrange("p (k c) -> p k c", k=KC)).then_inc(S("wg_loaded"), 16)
            for i in range(TILES):
                if i >= 2:
                    used, count = tile_used(i - 2)
                    sp.wait_ge(S(used), count)
                sp.dma_start(w_raw[i % 2][:], wts[i].rearrange("p (k c) -> p k c", k=KC))\
                  .then_inc(S(f"w_loaded{i % 2}"), 16)
                if i == TILES_IN + TILES_OUT:
                    sp.wait_ge(S("mixed_done"), 1)
                    sp.dma_start(sk[:], subkeys.rearrange("p (s k) -> p s k", s=2)).then_inc(S("sk_loaded"), 16)
            sp.wait_ge(S("q_ps"), 2 * PH)
            sp.dma_start(iota_k[:], consts_b[:, 384:384 + NK * TG].rearrange("p (k t) -> p k t", t=TG))\
              .then_inc(S("iota_loaded"), 16)
            dst = gates_dram.rearrange("b p t -> p b t")

            def store(i, r):
                sp.wait_ge(S("ev_full"), (i + 1) * (TG // PSTEP))
                sp.dma_start(dst[:, :, bass.ts(i, TG * GB)], ev[r][:].rearrange("p b t k -> p b (t k)"))\
                  .then_inc(S(f"ev_stored{r}"), 16)

            with sp.Fori(0, NTG // 2) as o:
                for r in range(2):
                    store(o * 2 + r, r)
            for r in range(2):
                sp.wait_ge(S(f"ev_stored{r}"), 16 * (NTG // 2))
            sp.wait_ge(S("gate_mm"), NTG * (TG // PSTEP))

            def loads(g, c):
                e = g * GC + c
                first = isinstance(g, int) and e < DR
                if not first:
                    sp.wait_ge(S("pd_done"), e - DR + 1)
                sp.dma_start(d_raw[:, c % DR], down[bass.ts(e, 1)].rearrange("o p (k e) -> p (o k) e", k=KC))\
                  .then_inc(S(f"d_loaded{c % DR}"), 16)
                if not first:
                    sp.wait_ge(S("u_lo_done"), e - DR + 1)
                sp.dma_start(u_raw[:, c % DR], up[bass.ts(e, 1)].rearrange("o p d -> p (o d)"))\
                  .then_inc(S(f"u_loaded{c % DR}"), 16)
                if c % GB == 0:
                    b = c // GB
                    if not (isinstance(g, int) and g == 0):
                        sp.wait_ge(S("w_done"), e - GB)
                    sp.dma_start(g_sb[:, b], gates_dram[bass.ts(g * 2 + b, 1)]
                                 .rearrange("o p (t k) -> p (o t) k", k=GB)).then_inc(S(f"g_loaded{b}"), 16)

            for c in range(GC):
                loads(0, c)
            with sp.Fori(1, NG) as g:
                for c in range(GC):
                    loads(g, c)
            sp.wait_ge(S("acc_done"), NG * 8)
            sp.dma_start(nf[:], normf.partition_broadcast(P).rearrange("p o d -> p (o d)")).then_inc(S("nf_loaded"), 16)
            for b in range(TB):
                sp.wait_ge(S("y_done"), b + 1)
                sp.dma_start(y_v[b], xt[:, b]).then_inc(S("y_stored"), 16)
            sp.wait_ge(S("y_stored"), 16 * TB)

        @block.gpsimd
        def _(pool):
            pool.dma_start(w2_sb[:], w2.rearrange("p (k h d) -> p k h d", k=2, h=2)).then_inc(S("w2_loaded"), 16)
            pool.wait_ge(S("evT"), 13)
            pool.wait_ge(S("pj_done"), 17)
            for kv in range(2):
                if kv == 1:
                    pool.wait_ge(S("hid_done"), 1)
                for half in range(2):
                    pool.dma_start(w1_sb[64 * half:64 * half + 64], w1[kv].rearrange("p (l h) -> p l h", l=CMP_LEN)).then_inc(S("w1_loaded"), 16)
            for hd in range(PH):
                r = hd % 2
                for s in range(2):
                    pool.wait_ge(S("hit_eq"), 2 * hd + s + 1)
                    nc.gpsimd.tensor_tensor(
                        hit[r][s][:], hit[r][s][:],
                        tif[r][s][:].unsqueeze(2).broadcast_to([P, TB, TOPK, TOPK]), ALU.mult)\
                        .then_inc(S("hit_done"), 1)

        @block.scalar
        def _(act):
            def split_w(i):
                act.wait_ge(S(f"w_loaded{i % 2}"), 16 * (i // 2 + 1))
                if i >= 2:
                    used, count = tile_used(i - 2)
                    act.wait_ge(S(used), count)
                nc.scalar.activation(w_hi[i % 2][:], w_raw[i % 2][:], ACT.Copy).then_inc(S("w_hi_done"), 1)

            def rms(n):
                for b in range(TB):
                    if n == 0:
                        act.wait_ge(S(f"x_loaded{b}"), 16)
                    else:
                        act.wait_ge(S("x1_done") if n == 1 else S("acc_done"),
                                    TB + b + 1 if n == 1 else (NG - 1) * 8 + 2 * b + 2)
                    if n * TB + b:
                        act.wait_ge(S("ssq_done"), n * TB + b)
                    squares = junk[:] if n < 2 else a_sb[:].rearrange("p a t -> p (a t)")
                    nc.scalar.activation(squares, xt[:, b], ACT.Square, accum_out=ssq[:, b:b + 1])\
                      .then_inc(S("ssq_done"), 1)
                act.wait_ge(S("ms_done"), n + 1)
                nc.scalar.activation(rt[:], ms[:], ACT.Sqrt).then_inc(S("root_done"), 1)

            def evac_hi(rep, gain):
                for k in range(KC):
                    act.wait_ge(S("hT_ps"), rep * KC + k + 1)
                    nc.scalar.activation(h_hi[:, k], bank[k][:], ACT.Copy,
                                         **({} if gain is None else {"scale": gain[:, k:k + 1]}))\
                      .then_inc(S("h_hi_done"), 1)

            rms(0)
            act.wait_ge(S("wg_loaded"), 16)
            nc.scalar.activation(wg_hi[:], wg_raw[:], ACT.Copy).then_inc(S("wg_hi_done"), 1)
            split_w(0)
            act.wait_ge(S("const_loaded"), 64)
            evac_hi(0, g_attn)
            split_w(1)
            act.wait_ge(S("angles"), 2)
            for i, (dst, src) in enumerate(((sin2, red), (cos2, red2))):
                for half in range(2):
                    nc.scalar.activation(dst[:, :, half], src[:], ACT.Sin,
                                         scale=-1.0 if i == 0 and half == 0 else 1.0).then_inc(S("tables"), 1)

            def evac_T(u):
                n, b = divmod(u, TB)
                act.wait_ge(S("tT_done"), u + 1)
                src = bank[4 + u % 2][:].rearrange("p (j t) -> p j t", j=4)
                if n < 2:
                    nc.scalar.activation(qT[:, n, :, b * P:(b + 1) * P], src, ACT.Copy, scale=DH ** -0.5)\
                      .then_inc(S("evT"), 1)
                else:
                    nc.scalar.activation(kT[:, :, b * P:(b + 1) * P], src, ACT.Copy).then_inc(S("evT"), 1)

            for u in range(16):
                if u >= 1 and u <= 12:
                    evac_T(u - 1)
                if u >= 12:
                    act.wait_ge(S("pj_done"), u + 1)
                    nc.scalar.activation(vnat[:, u - 12], bank[u % 4][:], ACT.Copy).then_inc(S("v_done"), 1)
                if u == 5:
                    split_w(2)
                if u == 9:
                    split_w(3)
            act.wait_ge(S("tT_done"), 13)
            nc.scalar.activation(vcT[:], bank[4][:], ACT.Copy).then_inc(S("evT"), 1)
            act.wait_ge(S("pj_done"), 17)
            nc.scalar.activation(gexp[:], bank[0][:, 0:TB * N_GATES].rearrange("p (b g) -> p b g", b=TB),
                                 ACT.Exp, scale=-1.0).then_inc(S("gexp_done"), 1)
            for kv in range(2):
                act.wait_ge(S("hid_done"), kv + 1)
                if kv == 0:
                    act.wait_ge(S("pads"), 2)
                nc.scalar.activation(hid[kv][:, :, 0:NC],
                                     bank[6 + kv][:, 0:4 * CP].rearrange("p (j c) -> p j c", j=4)[:, :, 0:NC],
                                     ACT.Gelu).then_inc(S("hid_act"), 1)
            act.wait_ge(S("cmp_ps"), 1)
            nc.scalar.activation(kcT[:, 0:NC], bank[4][:, 0:NC], ACT.Copy).then_inc(S("kc_done"), 1)
            split_w(4)
            split_w(5)

            for s in range(len(UNITS) + 12):
                qb, in_qb = divmod(s, STEP_QB)
                if s < len(UNITS):
                    n = width(*UNITS[s][:2])
                    act.wait_ge(S("max_done"), s + 1)
                    if s >= 3:
                        act.wait_ge(S("pT_ps"), s - 2)
                    nc.scalar.activation(pr[s % 3][:, 0:n], bank[s % 3][:, 0:n], ACT.Exp,
                                         bias=nmax[:, s:s + 1], accum_out=rsum[:, s:s + 1])\
                      .then_inc(S("exp_done"), 1)
                    if in_qb == 2:
                        act.wait_ge(S("c_shift"), qb + 1)
                        nc.scalar.activation(c_sc[:, :, 0:NC], c_sc[:, :, 0:NC], ACT.Exp)\
                          .then_inc(S("c_exp"), 1)
                    if in_qb == 7:
                        act.wait_ge(S("c_T"), qb + 1)
                        nc.scalar.activation(c_pT[:], bank[7][:, 256:512].rearrange("p (g t) -> p g t", g=2),
                                             ACT.Copy).then_inc(S("c_pT_done"), 1)
                if 2 <= s < len(UNITS) + 2 and s % 2 == 0:
                    u = s - 2
                    n = width(*UNITS[u][:2])
                    act.wait_ge(S("pT_ps"), u + 1)
                    if u >= 2:
                        act.wait_ge(S("pv_done"), u - 1)
                    nc.scalar.activation(pt[0][:, 0:n], bank[3][:, 0:n], ACT.Copy).then_inc(S("pt_done0"), 1)
                if in_qb == HEADS + 1 and qb < TB:
                    act.wait_ge(S("es_in_done"), qb + 1)
                    nc.scalar.activation(es[:, qb], es_in[:, qb], ACT.Exp).then_inc(S("es_done"), 1)

            evac_hi(1, None)
            split_w(6)
            rms(1)
            evac_hi(2, g_ffn)
            split_w(7)
            for v in range(2 * PH):
                act.wait_ge(S("q_ps"), v + 1)
                if v >= 2:
                    act.wait_ge(S("s_ps"), v - 1)
                nc.scalar.activation(q_sb[v % 2][:], bank[v % 2][:], ACT.Copy).then_inc(S("q_done"), 1)
                if v == 3:
                    split_w(8)
                if v == 7:
                    split_w(9)
            act.wait_ge(S("score_shift"), 1)
            nc.scalar.activation(score[:], score[:], ACT.Exp).then_inc(S("score_exp"), 1)
            def evac_gates(i, r, q):
                n = i * (TG // PSTEP) + q
                act.wait_ge(S("gate_mm"), n + 1)
                if q == 0:
                    wait_slot(i, r)
                src = bank[4 + q % 4][:].rearrange("p (t b k) -> p t b k", t=PSTEP, k=GB)
                dst = ev[r][:, :, q * PSTEP:(q + 1) * PSTEP].rearrange("p b t k -> p t b k")
                nc.scalar.activation(dst, src, ACT.Copy).then_inc(S("ev_full"), 1)

            def wait_slot(i, r):
                if not (isinstance(i, int) and i < 2):
                    act.wait_ge(S(f"ev_stored{r}"), (i - r) * 8)

            for r in range(2):
                for q in range(TG // PSTEP):
                    evac_gates(r, r, q)
            with act.Fori(1, NTG // 2) as o:
                for r in range(2):
                    for q in range(TG // PSTEP):
                        evac_gates(o * 2 + r, r, q)

            def d_high(g, c):
                e = g * GC + c
                act.wait_ge(S(f"d_loaded{c % DR}"), (g * 2 + c // DR + 1) * 16)
                if not (isinstance(g, int) and e < 2):
                    act.wait_ge(S("pd_done"), e - 1)
                nc.scalar.activation(d_hi[:, c % 2], d_raw[:, c % DR], ACT.Copy).then_inc(S("d_hi_done"), 1)

            def group(g, last):
                first = isinstance(g, int) and g == 0
                for c in range(GC):
                    e = g * GC + c
                    act.wait_ge(S(f"u_loaded{c % DR}"), (g * 2 + c // DR + 1) * 16)
                    if c == 0 and not first:
                        act.wait_ge(S("pu_done"), g * 8)
                    nc.scalar.activation(u_hi[:, c], u_raw[:, c % DR], ACT.Copy).then_inc(S("u_hi_done"), 1)
                    act.wait_ge(S("pd_done"), e + 1)
                    if not (first and c < 2):
                        act.wait_ge(S("w_done"), e - 1)
                    nc.scalar.activation(a_sb[:, c % 2], bank[c % 2][:], ACT.Gelu).then_inc(S("gelu_done"), 1)
                    if c < GC - 2:
                        d_high(g, c + 2)
                    elif not last:
                        d_high(g + 1, c + 2 - GC)

            d_high(0, 0)
            d_high(0, 1)
            group(0, False)
            with act.Fori(1, NG - 1) as g:
                group(g, False)
            group(NG - 1, True)
            rms(2)

        @block.vector
        def _(dve):
            done = [0]

            def link(ins):
                done[0] += 1
                ins.then_inc(S("dve_link"), 1)
                dve.wait_ge(S("dve_link"), done[0])

            V = nc.vector

            def split_w(i):
                dve.wait_ge(S("w_hi_done"), i + 1)
                V.tensor_tensor(w_lo[i % 2][:], w_raw[i % 2][:], f32(w_hi[i % 2][:]), ALU.subtract)\
                 .then_inc(S("w_lo_done"), 1)

            def rstd_of(n):
                dve.wait_ge(S("ssq_done"), TB * (n + 1))
                V.tensor_scalar(ms[:], ssq[:], 1.0 / D, EPS, ALU.mult, ALU.add).then_inc(S("ms_done"), 1)
                dve.wait_ge(S("root_done"), n + 1)
                link(V.reciprocal(rstd[:], rt[:]))
                link(V.tensor_tensor(nt[:], rstd[:], rstd[:], ALU.mult))
                link(V.tensor_tensor(nt[:], nt[:], ms[:], ALU.mult))
                link(V.tensor_scalar(nt[:], nt[:], -0.5, 1.5, ALU.mult, ALU.add))
                link(V.tensor_tensor(rstd[:], rstd[:], nt[:], ALU.mult))

            def scale_rows(n):
                for b in range(TB):
                    V.tensor_scalar(xs[:, b], xt[:, b], rstd[:, b:b + 1], None, ALU.mult)\
                     .then_inc(S("xs_done"), 1)

            def evac_lo(rep, gain):
                for k in range(KC):
                    dve.wait_ge(S("h_hi_done"), rep * KC + k + 1)
                    if gain is None:
                        V.tensor_tensor(h_lo[:, k], bank[k][:], f32(h_hi[:, k]), ALU.subtract)\
                         .then_inc(S("h_lo_done"), 1)
                    else:
                        V.scalar_tensor_tensor(h_lo[:, k], bank[k][:], gain[:, k:k + 1], f32(h_hi[:, k]),
                                               ALU.mult, ALU.subtract).then_inc(S("h_lo_done"), 1)

            dve.wait_ge(S("const_loaded"), 64)
            link(V.tensor_copy(posf[:], posi[:]))
            link(V.tensor_tensor(ang[:], posf[:].unsqueeze(2).broadcast_to([P, TB, HALF]),
                                 inv_freq.unsqueeze(1).broadcast_to([P, TB, HALF]), ALU.mult))
            link(V.tensor_scalar(trn[:], ang[:], 1.0 / TWO_PI, ROUND, ALU.mult, ALU.add))
            link(V.tensor_scalar(trn[:], trn[:], ROUND, None, ALU.subtract))
            link(V.scalar_tensor_tensor(red[:], trn[:], -PI_A, ang[:], ALU.mult, ALU.add))
            link(V.scalar_tensor_tensor(red[:], trn[:], -PI_B, red[:], ALU.mult, ALU.add))
            link(V.scalar_tensor_tensor(red[:], trn[:], -PI_C, red[:], ALU.mult, ALU.add))
            link(V.tensor_scalar(red2[:], red[:], np.pi / 2, None, ALU.add))
            link(V.tensor_scalar(trn[:], red2[:], float(np.pi), -TWO_PI, ALU.is_gt, ALU.mult))
            link(V.tensor_tensor(red2[:], red2[:], trn[:], ALU.add))
            for t in (red, red2):
                V.tensor_scalar(t[:], t[:], PI_CLAMP, -PI_CLAMP, ALU.min, ALU.max).then_inc(S("angles"), 1)

            rstd_of(0)
            scale_rows(0)
            dve.wait_ge(S("wg_hi_done"), 1)
            V.tensor_tensor(wg_lo[:], wg_raw[:], f32(wg_hi[:]), ALU.subtract).then_inc(S("wg_lo_done"), 1)
            split_w(0)
            evac_lo(0, g_attn)
            split_w(1)

            dve.wait_ge(S("tables"), 4)
            heads = lambda ap: ap.rearrange("p (h f d) -> p h f d", h=HEADS, f=2)
            for u in range(12):
                b = u % TB
                dve.wait_ge(S("pj_done"), u + 1)
                if u >= 2:
                    dve.wait_ge(S("rope_done"), u - 1)
                ps = heads(bank[u % 4][:])
                c_b = cos2[:, b].rearrange("p f d -> p (f d)").unsqueeze(1).broadcast_to([P, HEADS, DH])
                V.tensor_tensor(rp_c[u % 2][:].rearrange("p (h d) -> p h d", h=HEADS),
                                bank[u % 4][:].rearrange("p (h d) -> p h d", h=HEADS), c_b, ALU.mult)
                for half in range(2):
                    ins = V.tensor_tensor(heads(rp_s[u % 2][:])[:, :, half], ps[:, :, 1 - half],
                                          sin2[:, b, half].unsqueeze(1).broadcast_to([P, HEADS, HALF]), ALU.mult)
                ins.then_inc(S("pj_free"), 1)
                dve.wait_ge(S("pj_free"), u + 1)
                if u >= 2:
                    dve.wait_ge(S("tT_done"), u - 1)
                V.tensor_tensor(roped[u % 2][:], rp_c[u % 2][:], rp_s[u % 2][:], ALU.add).then_inc(S("rope_done"), 1)
                if u == 5:
                    split_w(2)
                if u == 9:
                    split_w(3)
            V.memset(kcT[:], 0.0)
            link(V.memset(vbd[:], 0.0))
            V.memset(hid[0][:], 0.0).then_inc(S("pads"), 1)
            V.memset(hid[1][:], 0.0).then_inc(S("pads"), 1)
            V.tensor_scalar(nsink[:], sinks, -1.0, None, ALU.mult)
            for kv in range(2):
                dve.wait_ge(S("evT"), 12 + kv)
                src = (kT[:, 1] if kv == 0 else vcT[:]).rearrange("p (c l) -> p l c", l=CMP_STRIDE)
                for part in range(2):
                    ls = slice(part * CMP_STRIDE, (part + 1) * CMP_STRIDE)
                    V.tensor_tensor(cx[kv][:, ls], src[:, :, part:part + NC],
                                    cmp_pos[:, kv, ls].unsqueeze(2).broadcast_to([P, CMP_STRIDE, NC]), ALU.add)\
                     .then_inc(S("cx_done"), 1)
            dve.wait_ge(S("gexp_done"), 1)
            link(V.tensor_scalar(gexp[:], gexp[:], 1.0, None, ALU.add))
            link(V.reciprocal(gates[:].rearrange("p b h k -> p b (h k)"), gexp[:]))
            dve.wait_ge(S("hid_act"), 2)
            dve.wait_ge(S("hid_done"), 2)
            V.tensor_copy(hrep[:], hid[1][:].unsqueeze(2).broadcast_to([P, GROUPS * 2, 4, CP]))\
             .then_inc(S("hrep_done"), 1)
            dve.wait_ge(S("cmp_ps"), 2)
            for g in range(GROUPS):
                for j in range(HPG):
                    q = slice(CP * j, CP * j + CP)
                    V.tensor_copy(vbd[q, g, j], bank[5][q, g * DH:(g + 1) * DH]).then_inc(S("vbd_done"), 1)
            split_w(4)
            split_w(5)
            link(V.memset(c_sc[:], 0.0))

            def finish(gi):
                qb, br = gi // 3, gi % 3
                sl = slice(gi * HEADS, (gi + 1) * HEADS)
                o = bank[5 + gi % 2][:].rearrange("p (h d) -> p h d", h=HEADS)
                co = coef[:].unsqueeze(2).broadcast_to([P, HEADS, DH])
                out_a = mixed[:, qb, 0:COLS].rearrange("p (h d) -> p h d", h=HEADS)
                out_b = mixed[:, qb, COLS:2 * COLS]
                dve.wait_ge(S("exp_done"), 8 * gi + 8)
                if gi >= 1:
                    dve.wait_ge(S("o_free"), gi)
                if br == SWA:
                    dve.wait_ge(S("es_done"), qb + 1)
                    link(V.tensor_tensor(coef[:], rsum[:, sl], es[:, qb], ALU.add))
                    link(V.reciprocal(coef[:], coef[:]))
                else:
                    link(V.reciprocal(coef[:], rsum[:, sl]))
                    link(V.tensor_tensor(coef[:], coef[:], gates[:, qb, :, br], ALU.mult))
                dve.wait_ge(S("pv_done"), 8 * gi + 8)
                if br == SWA:
                    V.tensor_tensor(out_a, o, co, ALU.mult).then_inc(S("o_free"), 1)
                else:
                    V.tensor_tensor(o_tmp[:].rearrange("p (h d) -> p h d", h=HEADS), o, co, ALU.mult)\
                     .then_inc(S("o_free"), 1)
                    dve.wait_ge(S("o_free"), gi + 1)
                    dve.wait_ge(S("c_mixed"), qb + 1)
                    link(V.tensor_tensor(out_b, out_b, o_tmp[:], ALU.add))

            for s in range(len(UNITS) + 12):
                qb, in_qb = divmod(s, STEP_QB)
                if s < len(UNITS):
                    _, br, h = UNITS[s]
                    n = width(qb, br)
                    dve.wait_ge(S("s_done"), s + 1)
                    if br == SWA:
                        link(V.tensor_reduce(nmax[:, s:s + 1], bank[s % 3][:, 0:n], X_AXIS, ALU.max, negate=True))
                        V.tensor_tensor(nmax[:, s:s + 1], nmax[:, s:s + 1], nsink[:, h:h + 1], ALU.min)\
                         .then_inc(S("max_done"), 1)
                    else:
                        V.tensor_reduce(nmax[:, s:s + 1], bank[s % 3][:, 0:n], X_AXIS, ALU.max, negate=True)\
                         .then_inc(S("max_done"), 1)
                    if in_qb == 1:
                        dve.wait_ge(S("c_s"), qb + 1)
                        if qb >= 1:
                            dve.wait_ge(S("c_T"), qb)
                        cs = c_sc[:, :, 0:NC]
                        link(V.tensor_tensor(cs, bank[7][:, 0:HEADS * CP].rearrange("p (h c) -> p h c", h=HEADS)[:, :, 0:NC],
                                             cmp_neg[:, qb, 0:NC].unsqueeze(1).broadcast_to([P, HEADS, NC]), ALU.add))
                        link(V.tensor_reduce(c_max[:], cs, X_AXIS, ALU.max))
                        V.tensor_tensor(cs, cs, c_max[:].unsqueeze(2).broadcast_to([P, HEADS, NC]), ALU.subtract)\
                         .then_inc(S("c_shift"), 1)
                    if in_qb == 3:
                        dve.wait_ge(S("c_exp"), qb + 1)
                        V.tensor_tensor(cs, cs, cmp_vis[:, qb, 0:NC].unsqueeze(1).broadcast_to([P, HEADS, NC]), ALU.mult)\
                         .then_inc(S("c_p"), 1)
                        dve.wait_ge(S("c_p"), qb + 1)
                        link(V.tensor_reduce(c_sum[:], cs, X_AXIS, ALU.add))
                        link(V.tensor_scalar(c_sum[:], c_sum[:], 1e-30, None, ALU.max))
                        link(V.reciprocal(c_sum[:], c_sum[:]))
                        if qb >= 1:
                            dve.wait_ge(S("c_mixed"), qb)
                        link(V.tensor_tensor(c_coef[:], c_sum[:], gates[:, qb, :, 0], ALU.mult))
                    if in_qb == 12:
                        dve.wait_ge(S("c_o"), qb + 1)
                        V.tensor_tensor(mixed[:, qb, COLS:2 * COLS].rearrange("p (h d) -> p h d", h=HEADS),
                                        bank[7][:].rearrange("p (h d) -> p h d", h=HEADS),
                                        c_coef[:].unsqueeze(2).broadcast_to([P, HEADS, DH]), ALU.mult)\
                         .then_inc(S("c_mixed"), 1)
                if 2 <= s < len(UNITS) + 2 and s % 2 == 1:
                    u = s - 2
                    n = width(*UNITS[u][:2])
                    dve.wait_ge(S("pT_ps"), u + 1)
                    if u >= 2:
                        dve.wait_ge(S("pv_done"), u - 1)
                    V.tensor_copy(pt[1][:, 0:n], bank[4][:, 0:n]).then_inc(S("pt_done1"), 1)
                if in_qb == HEADS and qb < TB:
                    dve.wait_ge(S("max_done"), s)
                    V.tensor_tensor(es_in[:, qb], sinks, nmax[:, qb * STEP_QB:qb * STEP_QB + HEADS], ALU.add)\
                     .then_inc(S("es_in_done"), 1)
                if s >= 11 and (s - 11) % HEADS == 0 and (s - 11) // HEADS < 3 * TB:
                    finish((s - 11) // HEADS)
            V.tensor_copy(nt[:, 0:1], mixed[:, TB - 1, D - 1:D]).then_inc(S("mixed_done"), 1)
            evac_lo(1, None)
            for n in range(2 * TB):
                half, b = divmod(n, TB)
                dve.wait_ge(S("wo_ps"), n + 1)
                o = xt[:, b, half * COLS:(half + 1) * COLS]
                V.tensor_tensor(o, o, bank[n % 4][:], ALU.add).then_inc(S("x1_done"), 1)
                if n == 3:
                    split_w(6)
            rstd_of(1)
            scale_rows(1)
            evac_lo(2, g_ffn)
            split_w(7)

            LOW = -3.0e38

            def keys_of(hd):
                r = hd % 2
                for s in range(2):
                    dve.wait_ge(S("hit_done"), 2 * hd + s + 1)
                    V.tensor_reduce(key[s][:, :, hd], hit[r][s][:], X_AXIS, ALU.add).then_inc(S("key_done"), 1)

            def top16(vals, idx, src, tmp):
                for b in range(TB):
                    V.max(vals[b][:, 0:8], src[b]).then_inc(S("top_a"), 1)
                top_count[0] += TB
                for b in range(TB):
                    dve.wait_ge(S("top_a"), top_count[0] - TB + b + 1)
                    V.max_index(idx[b][:, 0:8], vals[b][:, 0:8], src[b])
                    V.match_replace(tmp[b], vals[b][:, 0:8], src[b], LOW).then_inc(S("top_b"), 1)
                for b in range(TB):
                    dve.wait_ge(S("top_b"), top_count[0] - TB + b + 1)
                    V.max(vals[b][:, 8:16], tmp[b]).then_inc(S("top_c"), 1)
                for b in range(TB):
                    dve.wait_ge(S("top_c"), top_count[0] - TB + b + 1)
                    last = V.max_index(idx[b][:, 8:16], vals[b][:, 8:16], tmp[b])
                return last

            top_count = [0]
            for hd in range(PH):
                r = hd % 2
                for s in range(2):
                    v = 2 * hd + s
                    dve.wait_ge(S("s_ps"), v + 1)
                    src = bank[2 + v % 4]
                    if v >= 2:
                        dve.wait_ge(S("s_free"), v - 1)
                    if hd >= 2:
                        dve.wait_ge(S("hit_done"), 2 * (hd - 2) + s + 1)
                    top16([tv[r][s][:, b] for b in range(TB)], [ti[r][s][:, b] for b in range(TB)],
                          [src[:, b * NK:(b + 1) * NK] for b in range(TB)],
                          [work[s][:, b] for b in range(TB)]).then_inc(S("s_free"), 1)
                dve.wait_ge(S("s_free"), 2 * hd + 2)
                for b in range(TB):
                    V.tensor_tensor(cand[:, b], tv[r][0][:, b].unsqueeze(2).broadcast_to([P, TOPK, TOPK]),
                                    tv[r][1][:, b].unsqueeze(1).broadcast_to([P, TOPK, TOPK]), ALU.add)\
                     .then_inc(S("cand_done"), 1)
                dve.wait_ge(S("cand_done"), TB * (hd + 1))
                link(top16([score[:, b, hd] for b in range(TB)], [posn[:, b] for b in range(TB)],
                           [cand[:, b].rearrange("p i j -> p (i j)") for b in range(TB)],
                           [candw[:, b] for b in range(TB)]))
                V.tensor_copy(tif[r][0][:], ti[r][0][:])
                V.tensor_copy(tif[r][1][:], ti[r][1][:])
                V.tensor_scalar(pab[r][0][:], posn[:], 4, None, ALU.logical_shift_right)
                link(V.tensor_scalar(pab[r][1][:], posn[:], TOPK - 1, None, ALU.bitwise_and))
                if hd >= 2:
                    dve.wait_ge(S("key_done"), 2 * (hd - 1))
                for s in range(2):
                    V.tensor_tensor(hit[r][s][:].rearrange("p b k r -> p (b k) r"),
                                    pab[r][s][:].rearrange("p b k -> p (b k)").unsqueeze(2)
                                    .broadcast_to([P, TB * TOPK, TOPK]),
                                    iota16.unsqueeze(1).broadcast_to([P, TB * TOPK, TOPK]), ALU.is_equal)\
                     .then_inc(S("hit_eq"), 1)
                if hd >= 1:
                    keys_of(hd - 1)
                if hd == 1:
                    split_w(8)
                if hd == 3:
                    split_w(9)
            link(V.tensor_copy(g_sum[:], score[:, :, :, 0]))
            sv = score[:].rearrange("p b h k -> p (b h) k")
            gv = g_sum[:].rearrange("p b h -> p (b h)").unsqueeze(2).broadcast_to([P, TB * PH, TOPK])
            V.tensor_tensor(sv, sv, gv, ALU.subtract).then_inc(S("score_shift"), 1)
            keys_of(PH - 1)
            dve.wait_ge(S("score_exp"), 1)
            link(V.tensor_reduce(g_sum[:].rearrange("p b h -> p (b h)"), sv, X_AXIS, ALU.add))
            link(V.reciprocal(g_sum[:], g_sum[:]))
            V.tensor_tensor(sv, sv, gv, ALU.mult).then_inc(S("gate_done"), 1)
            dve.wait_ge(S("slot_ps"), 3)
            V.tensor_copy(sl_key[0][:], bank[1][:]).then_inc(S("slot_done"), 1)
            V.tensor_copy(sl_key[1][:], bank[2][:]).then_inc(S("slot_done"), 1)
            link(V.tensor_copy(sl_g[0][:], bank[0][:]))
            link(V.tensor_tensor(sl_r[0][:], bank[0][:], sl_g[0][:], ALU.subtract))
            link(V.tensor_copy(sl_g[1][:], sl_r[0][:]))
            link(V.tensor_tensor(sl_r[1][:], sl_r[0][:], sl_g[1][:], ALU.subtract))
            link(V.tensor_copy(sl_g[2][:], sl_r[1][:]))
            dve.wait_ge(S("iota_loaded"), 16)

            def one_hots(i, r):
                if not (isinstance(i, int) and i < 2):
                    dve.wait_ge(S("gate_mm"), (i - 1) * (TG // PSTEP))
                tok = bass.ts(i, TG)
                cols = lambda t: t[:, tok].unsqueeze(1).broadcast_to([P, NK, TG])
                V.tensor_tensor(oh[r][0][:], iota_k[:], cols(sl_key[0]), ALU.is_equal).then_inc(S("oh_a"), 1)
                V.tensor_tensor(oh[r][1][:], iota_k[:], cols(sl_key[1]), ALU.is_equal)
                dve.wait_ge(S("oh_a"), i + 1)
                for j in range(3):
                    ins = V.tensor_tensor(gp[r][j][:], oh[r][0][:], cols(sl_g[j]), ALU.mult)
                ins.then_inc(S("oh_done"), 1)

            for i in range(2):
                one_hots(i, i)
            with dve.Fori(1, NTG // 2) as o:
                for r in range(2):
                    one_hots(o * 2 + r, r)

            dve.wait_ge(S("gate_mm"), NTG * (TG // PSTEP))
            dve.wait_ge(S("ev_stored0"), 16 * (NTG // 2))
            dve.wait_ge(S("ev_stored1"), 16 * (NTG // 2))

            def d_low(g, c):
                e = g * GC + c
                dve.wait_ge(S("d_hi_done"), e + 1)
                V.tensor_tensor(d_lo[:, c % DR], d_raw[:, c % DR], f32(d_hi[:, c % 2]), ALU.subtract)\
                 .then_inc(S("d_lo_done"), 1)

            def group(g, last):
                for c in range(GC):
                    e, b = g * GC + c, c // GB
                    dve.wait_ge(S("u_hi_done"), e + 1)
                    V.tensor_tensor(u_lo[:, c], u_raw[:, c % DR], f32(u_hi[:, c]), ALU.subtract)\
                     .then_inc(S("u_lo_done"), 1)
                    dve.wait_ge(S("gelu_done"), e + 1)
                    if c % GB == 0:
                        dve.wait_ge(S(f"g_loaded{b}"), 16 * g + 16)
                    V.tensor_tensor(a_sb[:, c % 2], a_sb[:, c % 2], g_sb[:, b, :, c % GB], ALU.mult)\
                     .then_inc(S("w_step"), 1)
                    dve.wait_ge(S("w_step"), 2 * e + 1)
                    V.tensor_copy(w_e_hi[:, c], a_sb[:, c % 2]).then_inc(S("w_step"), 1)
                    dve.wait_ge(S("w_step"), 2 * e + 2)
                    V.tensor_tensor(w_e_lo[:, c], a_sb[:, c % 2], f32(w_e_hi[:, c]), ALU.subtract)\
                     .then_inc(S("w_done"), 1)
                    if c < GC - 2:
                        d_low(g, c + 2)
                    elif not last:
                        d_low(g + 1, c + 2 - GC)
                for n in range(8):
                    dve.wait_ge(S("pu_done"), g * 8 + n + 1)
                    o = xt[:, n // 2, (n % 2) * COLS:(n % 2 + 1) * COLS]
                    V.tensor_tensor(o, o, bank[4 + n % 4][:], ALU.add).then_inc(S("acc_done"), 1)

            d_low(0, 0)
            d_low(0, 1)
            group(0, False)
            with dve.Fori(1, NG - 1) as g:
                group(g, False)
            group(NG - 1, True)
            rstd_of(2)
            dve.wait_ge(S("nf_loaded"), 16)
            for b in range(TB):
                V.scalar_tensor_tensor(xt[:, b], xt[:, b], rstd[:, b:b + 1], nf[:], ALU.mult, ALU.mult)\
                 .then_inc(S("y_done"), 1)

        @block.tensor
        def _(pe):
            def transposes(rep, src):
                for b in range(TB):
                    if rep != 1:
                        pe.wait_ge(S("xs_done"), (rep // 2) * TB + b + 1)
                    for k in range(KC):
                        t = nc.tensor.transpose(bank[k][:, b * P:(b + 1) * P], src[:, b, k * P:(k + 1) * P], ident)
                        if b == TB - 1:
                            t.then_inc(S("hT_ps"), 1)

            def mm3(out, a_hi, a_lo, b_hi, b_lo, n, last):
                for j, (a, b) in enumerate(((a_hi, b_hi), (a_hi, b_lo), (a_lo, b_hi))):
                    m = nc.tensor.matmul(out, a, b, start=(n == 0 and j == 0), stop=(n == last and j == 2))
                return m

            pe.wait_ge(S("const_loaded"), 64)
            transposes(0, xs)

            def rope_T(u):
                pe.wait_ge(S("rope_done"), u + 1)
                if u >= 2:
                    pe.wait_ge(S("evT"), u - 1)
                for j in range(4):
                    t = nc.tensor.transpose(bank[4 + u % 2][:, j * P:(j + 1) * P],
                                            roped[u % 2][:, j * P:(j + 1) * P], ident)
                t.then_inc(S("tT_done"), 1)

            pe.wait_ge(S("h_lo_done"), KC)
            for u in range(16):
                n, b = divmod(u, TB)
                if b == 0:
                    pe.wait_ge(S("w_lo_done"), n + 1)
                if u >= 4:
                    pe.wait_ge(S("pj_free"), u - 3)
                tok = slice(b * P, (b + 1) * P)
                for k in range(KC):
                    m = mm3(bank[u % 4][:], h_hi[:, k, tok], h_lo[:, k, tok],
                            w_hi[n % 2][:, k], w_lo[n % 2][:, k], k, KC - 1)
                m.then_inc(S("pj_done"), 1)
                if 1 <= u <= 12:
                    rope_T(u - 1)
            pe.wait_ge(S("v_done"), 1)
            pe.wait_ge(S("wg_lo_done"), 1)
            for b in range(TB):
                tok = slice(b * P, (b + 1) * P)
                for k in range(KC):
                    m = mm3(bank[0][:, b * N_GATES:(b + 1) * N_GATES], h_hi[:, k, tok], h_lo[:, k, tok],
                            wg_hi[:, k], wg_lo[:, k], k, KC - 1)
            m.then_inc(S("pj_done"), 1)
            pe.wait_ge(S("v_done"), TB)
            pe.wait_ge(S("evT"), 11)
            for b in range(TB):
                t = nc.tensor.transpose(bank[4][:, b * P:(b + 1) * P], vnat[:, b, P:2 * P], ident)
            t.then_inc(S("tT_done"), 1)

            for kv in range(2):
                pe.wait_ge(S("cx_done"), 2 * kv + 2)
                pe.wait_ge(S("w1_loaded"), 32 * (kv + 1))
                for g in range(GROUPS):
                    rows = slice(DH * g, DH * g + DH)
                    for hh in range(2):
                        j = g * 2 + hh
                        for l in range(CMP_LEN):
                            m = nc.tensor.matmul(bank[6 + kv][:, j * CP:j * CP + NC],
                                                 w1_sb[rows, l, hh * P:(hh + 1) * P], cx[kv][rows, l],
                                                 start=(l == 0), stop=(l == CMP_LEN - 1))
                    if g == 0:
                        m.then_inc(S("rows_switch"), 1)
                        pe.wait_ge(S("rows_switch"), kv + 1)
                m.then_inc(S("hid_done"), 1)
            pe.wait_ge(S("hid_act"), 1)
            pe.wait_ge(S("w2_loaded"), 16)
            pe.wait_ge(S("evT"), 13)
            for g in range(GROUPS):
                for hh in range(2):
                    m = nc.tensor.matmul(bank[4][DH * g:DH * g + DH, 0:NC], w2_sb[:, 0, hh],
                                         hid[0][:, g * 2 + hh, 0:NC], start=(hh == 0), stop=(hh == 1))
            m.then_inc(S("cmp_ps"), 1)
            pe.wait_ge(S("hrep_done"), 1)
            for g in range(GROUPS):
                for hh in range(2):
                    m = nc.tensor.matmul(bank[5][:, g * DH:(g + 1) * DH],
                                         hrep[:, g * 2 + hh].rearrange("p j c -> p (j c)"),
                                         w2_sb[:, 1, hh], start=(hh == 0), stop=(hh == 1))
            m.then_inc(S("cmp_ps"), 1)

            pe.wait_ge(S("kc_done"), 1)
            pe.wait_ge(S("vbd_done"), 8)
            pe.wait_ge(S("gexp_done"), 1)
            for s in range(len(UNITS) + 12):
                qb, in_qb = divmod(s, STEP_QB)
                if s < len(UNITS):
                    _, br, h = UNITS[s]
                    g, j = divmod(h, HPG)
                    rows = slice(DH * g, DH * g + DH)
                    if in_qb == 0:
                        if qb >= 1:
                            pe.wait_ge(S("c_mixed"), qb)
                        for hh in range(HEADS):
                            rr = slice(DH * (hh // HPG), DH * (hh // HPG) + DH)
                            m = nc.tensor.matmul(bank[7][:, hh * CP:hh * CP + NC],
                                                 qT[rr, 1, hh % HPG, qb * P:(qb + 1) * P], kcT[rr, 0:NC],
                                                 start=True, stop=True)
                            if hh == HPG - 1:
                                m.then_inc(S("rows_switch"), 1)
                                pe.wait_ge(S("rows_switch"), 2 + qb + 1)
                        m.then_inc(S("c_s"), 1)
                    n = width(qb, br)
                    k0 = (qb + 1) * P - n
                    if s >= 3:
                        pe.wait_ge(S("exp_done"), s - 2)
                    nc.tensor.matmul(bank[s % 3][:, 0:n], qT[rows, 0 if br == SWA else 1, j, qb * P:(qb + 1) * P],
                                     kT[rows, K_OF[br], k0:k0 + n], start=True, stop=False)
                    mw = n if br == SWA else P
                    nc.tensor.matmul(bank[s % 3][:, n - mw:n], ident_b, mask_b[:, 2 * P - mw:2 * P],
                                     start=False, stop=True).then_inc(S("s_done"), 1)
                if 2 <= s < len(UNITS) + 2:
                    u = s - 2
                    n = width(*UNITS[u][:2])
                    pe.wait_ge(S("exp_done"), u + 1)
                    if u >= 2:
                        pe.wait_ge(S(f"pt_done{u % 2}"), u // 2)
                    for kb in range(n // P):
                        t = nc.tensor.transpose(bank[3 + u % 2][:, kb * P:(kb + 1) * P],
                                                pr[u % 3][:, kb * P:(kb + 1) * P], ident)
                    t.then_inc(S("pT_ps"), 1)
                if 3 <= s < len(UNITS) + 3:
                    u = s - 3
                    uq, ub, uh = UNITS[u]
                    n = width(uq, ub)
                    gi = u // HEADS
                    if uh == 0 and gi >= 2:
                        pe.wait_ge(S("o_free"), gi - 1)
                    pe.wait_ge(S(f"pt_done{u % 2}"), u // 2 + 1)
                    v0 = K_OF[ub] * P + (uh // HPG) * DH
                    for kb in range(n // P):
                        tb = uq + 1 - n // P + kb
                        m = nc.tensor.matmul(bank[5 + gi % 2][:, uh * DH:(uh + 1) * DH],
                                             pt[u % 2][:, kb * P:(kb + 1) * P], vnat[:, tb, v0:v0 + DH],
                                             start=(kb == 0), stop=(kb == n // P - 1))
                    m.then_inc(S("pv_done"), 1)
                if s < len(UNITS) and in_qb == 6:
                    pe.wait_ge(S("c_p"), qb + 1)
                    for g in range(GROUPS):
                        t = nc.tensor.transpose(bank[7][:, 256 + g * P:256 + (g + 1) * P],
                                                c_sc[:, g * HPG:(g + 1) * HPG].rearrange("p h c -> p (h c)"), ident)
                    t.then_inc(S("c_T"), 1)
                if s < len(UNITS) and in_qb == 9:
                    pe.wait_ge(S("c_pT_done"), qb + 1)
                    for g in range(GROUPS):
                        m = nc.tensor.matmul(bank[7][:, g * 256:(g + 1) * 256], c_pT[:, g],
                                             vbd[:, g].rearrange("p j d -> p (j d)"), start=True, stop=True)
                    m.then_inc(S("c_o"), 1)

            pe.wait_ge(S("mixed_done"), 1)
            transposes(1, mixed)
            pe.wait_ge(S("h_lo_done"), 2 * KC)
            for n in range(2 * TB):
                half, b = divmod(n, TB)
                i = TILES_IN + half
                if b == 0:
                    pe.wait_ge(S("w_lo_done"), i + 1)
                if n >= 4:
                    pe.wait_ge(S("x1_done"), n - 3)
                tok = slice(b * P, (b + 1) * P)
                for k in range(KC):
                    m = mm3(bank[n % 4][:], h_hi[:, k, tok], h_lo[:, k, tok],
                            w_hi[i % 2][:, k], w_lo[i % 2][:, k], k, KC - 1)
                m.then_inc(S("wo_ps"), 1)
            transposes(2, xs)

            pe.wait_ge(S("h_lo_done"), 3 * KC)
            pe.wait_ge(S("sk_loaded"), 16)

            def key_scores(v):
                if v >= 4:
                    pe.wait_ge(S("s_free"), v - 3)
                pe.wait_ge(S("q_done"), v + 1)
                for b in range(TB):
                    m = nc.tensor.matmul(bank[2 + v % 4][:, b * NK:(b + 1) * NK],
                                         q_sb[v % 2][:, b * P:(b + 1) * P], sk[:, v % 2], start=True, stop=True)
                m.then_inc(S("s_ps"), 1)

            for v in range(2 * PH):
                i = TILES_IN + TILES_OUT + v // 4
                if v % 4 == 0:
                    pe.wait_ge(S("w_lo_done"), i + 1)
                if v >= 2:
                    pe.wait_ge(S("q_done"), v - 1)
                for k in range(KC):
                    c = slice((v % 4) * P, (v % 4 + 1) * P)
                    m = mm3(bank[v % 2][:], w_hi[i % 2][:, k, c], w_lo[i % 2][:, k, c],
                            h_hi[:, k], h_lo[:, k], k, KC - 1)
                m.then_inc(S("q_ps"), 1)
                if v >= 1:
                    key_scores(v - 1)
            key_scores(2 * PH - 1)

            pe.wait_ge(S("gate_done"), 1)
            pe.wait_ge(S("key_done"), 2 * PH)
            for n, src in enumerate((score, key[0], key[1])):
                for b in range(TB):
                    t = nc.tensor.transpose(bank[n][:, b * P:(b + 1) * P],
                                            src[:, b].rearrange("p h k -> p (h k)"), ident)
                t.then_inc(S("slot_ps"), 1)

            def gate_rows(i, r):
                pe.wait_ge(S("oh_done"), i + 1)
                for q in range(TG // PSTEP):
                    n = i * (TG // PSTEP) + q
                    if not (isinstance(n, int) and n < 4):
                        pe.wait_ge(S("ev_full"), n - 3)
                    for tt in range(PSTEP):
                        t = q * PSTEP + tt
                        for j in range(3):
                            m = nc.tensor.matmul(bank[4 + q % 4][:, tt * NK:(tt + 1) * NK], oh[r][1][:, :, t],
                                                 gp[r][j][:, :, t], start=(j == 0), stop=(j == 2))
                    m.then_inc(S("gate_mm"), 1)

            for i in range(2):
                gate_rows(i, i)
            with pe.Fori(1, NTG // 2) as o:
                for r in range(2):
                    gate_rows(o * 2 + r, r)

            pe.wait_ge(S("ev_full"), NTG * (TG // PSTEP))

            def group(g):
                first = isinstance(g, int) and g == 0
                for c in range(GC):
                    e = g * GC + c
                    pe.wait_ge(S("d_lo_done"), e + 1)
                    if not (first and c < 2):
                        pe.wait_ge(S("gelu_done"), e - 1)
                    for k in range(KC):
                        m = mm3(bank[c % 2][:], d_hi[:, c % 2, k], d_lo[:, c % DR, k],
                                h_hi[:, k], h_lo[:, k], k, KC - 1)
                    m.then_inc(S("pd_done"), 1)
                for n in range(8):
                    b, half = divmod(n, 2)
                    if not (first and n < 4):
                        pe.wait_ge(S("acc_done"), g * 8 + n - 3)
                    tok, cols = slice(b * P, (b + 1) * P), slice(half * COLS, (half + 1) * COLS)
                    for c in range(GC):
                        if n == 0:
                            pe.wait_ge(S("u_lo_done"), g * GC + c + 1)
                            pe.wait_ge(S("w_done"), g * GC + c + 1)
                        m = mm3(bank[4 + n % 4][:], w_e_hi[:, c, tok], w_e_lo[:, c, tok],
                                u_hi[:, c, cols], u_lo[:, c, cols], c, GC - 1)
                    m.then_inc(S("pu_done"), 1)

            group(0)
            with pe.Fori(1, NG) as g:
                group(g)


def constants():
    c = np.zeros((P, 432), np.float32)
    c[:, 0:P] = np.eye(P)
    t = np.arange(T).reshape(TB, P).T
    vis = np.zeros((P, TB, CP), np.float32)
    vis[:, :, :NC] = (np.arange(NC) * CMP_STRIDE + CMP_LEN - 1)[None, None] <= t[:, :, None]
    c[:, 128:256] = np.where(vis > 0, 0.0, NEG).reshape(P, -1)
    c[:, 256:384] = vis.reshape(P, -1)
    c[:, 384:416] = np.float32(10000.0) ** (-np.arange(HALF, dtype=np.float32) / np.float32(HALF))
    c[:, 416:432] = np.arange(TOPK)
    b = np.zeros((P, 384 + NK * TG), np.dtype("bfloat16"))
    b[:, 0:P] = np.eye(P)
    q, k = np.arange(P)[:, None], np.arange(P)[None]
    b[:, P:2 * P] = np.where(k > q, 0.0, NEG)
    b[:, 2 * P:3 * P] = np.where(k <= q, 0.0, NEG)
    b[:, 384:] = np.repeat(np.arange(NK), TG)[None]
    return c, b


def kernel(x, positions, norm_attn, w_in, attn_sinks, cmp_k_pos, cmp_k_w1, cmp_k_w2, cmp_v_pos, cmp_v_w1,
           cmp_v_w2, w_out, norm_ffn, peer_w_query, peer_sub_keys_1, peer_sub_keys_2, peer_expert_down,
           peer_expert_up, norm_f):
    import concourse.bacc as bacc
    from concourse.bass_utils import run_bass_kernel_spmd

    a = lambda v: np.asarray(v)[0]
    kw = HEADS // HPG * DH
    w = a(w_in)
    sizes = [HEADS * DH, kw, kw, HEADS * DH] + [kw] * 6 + [N_GATES]
    qa, ka, va, qb, kc, vc, ks, vs, kw_, vw, gl = np.split(w, np.cumsum(sizes)[:-1], axis=1)
    pairs = lambda q: q.reshape(D, GROUPS, HPG, DH).transpose(0, 2, 1, 3).reshape(D, HEADS * DH)
    tiles = [pairs(qa), pairs(qb), np.concatenate([ka, kc, ks, kw_], 1), np.concatenate([va, vc, vs, vw], 1)]
    for m in (a(w_out), a(peer_w_query)):
        tiles += [m[:, c:c + COLS] for c in range(0, m.shape[1], COLS)]
    chunked = lambda m: m.reshape(KC, P, -1).transpose(1, 0, 2).reshape(P, -1)
    params = np.zeros((P, 96), np.float32)
    params[:, 0:8] = a(norm_attn).reshape(KC, P).T
    params[:, 8:16] = a(norm_ffn).reshape(KC, P).T
    params[:, 16:24] = a(attn_sinks)[None]
    for n, e in enumerate((a(cmp_k_pos), a(cmp_v_pos))):
        params[:, 32 + 32 * n:64 + 32 * n] = np.concatenate([e.T, e.T], 0)
    w1 = lambda m: a(m).reshape(CMP_LEN, DH, CMP_HIDDEN).transpose(1, 0, 2).reshape(DH, -1)
    w2 = lambda m: a(m).reshape(2, P, DH).transpose(1, 0, 2).reshape(P, -1)
    c, b = constants()
    arrays = {
        "x_in": a(x), "pos": np.asarray(positions)[0].reshape(TB, P).T, "params": params, "consts": c, "consts_b": b,
        "wts": np.stack([chunked(t) for t in tiles]), "wgate": chunked(gl),
        "w1": np.stack([w1(cmp_k_w1), w1(cmp_v_w1)]), "w2": np.concatenate([w2(cmp_k_w2), w2(cmp_v_w2)], 1),
        "subkeys": np.concatenate([a(peer_sub_keys_1).T, a(peer_sub_keys_2).T], 1),
        "normf": np.asarray(norm_f).reshape(1, D),
        "down": a(peer_expert_down).reshape(NK, P, KC, P).transpose(0, 3, 2, 1).reshape(NK, P, KC * P),
        "up": a(peer_expert_up).reshape(NK, P, D),
    }
    arrays = {k: np.ascontiguousarray(v) for k, v in arrays.items()}
    nc = bacc.Bacc("TRN2", target_bir_lowering=False, num_devices=1)
    ins = [nc.dram_tensor(k, v.shape, mybir.dt.from_np(v.dtype), kind="ExternalInput").ap() for k, v in arrays.items()]
    y = nc.dram_tensor("y", (T, D), F32, kind="ExternalOutput").ap()
    build(nc, *ins, y)
    r = run_bass_kernel_spmd(nc, [arrays], core_ids=[0])
    return r.results[0]["y"].reshape(1, T, D)
```

```python
import concourse.bass as bass
from concourse import mybir
from concourse.alu_op_type import AluOpType as ALU
import numpy as np

F32, F32R, BF16 = mybir.dt.float32, mybir.dt.float32r, mybir.dt.bfloat16
U32, I32 = mybir.dt.uint32, mybir.dt.int32
ACT = mybir.ActivationFunctionType
X_AXIS = mybir.AxisListType.X

P = 128
T, D = 512, 1024
KC, TB = D // P, T // P
DH, HALF = 64, 32
HEADS, GROUPS = 8, 2
HPG = HEADS // GROUPS
COLS = 512
N_GATES = 3 * HEADS
CMP_LEN, CMP_STRIDE, CMP_HIDDEN = 32, 16, 256
NC = (T - CMP_LEN) // CMP_STRIDE + 1
LP = CMP_LEN // 2
CP = NC + 1
PH, NK, TOPK = 8, 128, 16
NEG = -1e30
EPS = 1e-6
TILES_IN, TILES_OUT, TILES_Q = 4, 2, 4
TILES = TILES_IN + TILES_OUT + TILES_Q
GC = 8
NG = NK // GC
GB = 4
NGB = NK // GB
TG = 32
NTG = T // TG
PSTEP = 4
DR = 4
E_REST = 2 * PH
E_GATES = E_REST + 8
E_LAST = E_GATES + NTG
NE = E_LAST + 8
POOL_KEYS = {4: 0, 6: 1, 9: 2, 11: 3, 14: 4, 16: 5, 20: 6}
NSUB = NE // GB
G0 = NE // GC

TWO_PI = 2.0 * np.pi
PI_A = 6.28125
PI_B = float(np.float32(np.round((TWO_PI - PI_A) * 2.0 ** 19) / 2.0 ** 19))
PI_C = float(np.float32(TWO_PI - PI_A - PI_B))
ROUND = 1.5 * 2.0 ** 23
PI_CLAMP = float(np.nextafter(np.float32(np.pi), np.float32(0)))

SWA, SEL, WIN = range(3)
UNITS = [(qb, br, h) for qb in range(TB) for br in (SWA, SEL, WIN) for h in range(HEADS)]
K_OF = {SWA: 0, SEL: 2, WIN: 3}
STEP_QB = 3 * HEADS


def width(qb, br):
    return min(qb + 1, 2) * P if br == SWA else (qb + 1) * P


def tile_used(i):
    if i < TILES_IN:
        return "pj_done", TB * (i + 1)
    if i < TILES_IN + TILES_OUT:
        return "wo_ps", TB * (i - TILES_IN + 1)
    return "q_ps", 4 * (i - TILES_IN - TILES_OUT + 1)


def banks_before(g):
    return (g - G0) * 8 + NSUB * 8


def f32(ap):
    return ap.bitcast(F32)


def build(nc, x, pos, params, consts, consts_b, wts, wgate, w1, w2, subkeys, normf, down, up, y):
    at = [16512]

    def size(shape, dt):
        return int(np.prod(shape[1:])) * (2 if dt == BF16 else 4)

    def place(name, shape, dt, offset):
        return nc.alloc_sbuf_tensor_at(name, shape, dt, offset=offset)

    def sb(name, shape, dt=F32):
        t = place(name, shape, dt, at[0])
        at[0] += (size(shape, dt) + 31) // 32 * 32
        return t

    xt = sb("xt", [P, TB, D])
    h_hi = sb("h_hi", [P, KC, T], F32R)
    h_lo = sb("h_lo", [P, KC, T], F32R)
    cst = sb("cst", [P, 432])
    ident = cst[:, 0:P]
    cmp_neg = cst[:, 128:256].rearrange("p (q c) -> p q c", q=TB)
    cmp_vis = cst[:, 256:384].rearrange("p (q c) -> p q c", q=TB)
    inv_freq = cst[:, 384:416]
    iota16 = cst[:, 416:432]
    cstb = sb("cstb", [P, 384], BF16)
    ident_b, mask_b = cstb[:, 0:P], cstb[:, P:384]
    prm = sb("prm", [P, 96])
    g_attn, g_ffn, sinks = prm[:, 0:8], prm[:, 8:16], prm[:, 16:24]
    cmp_pos = prm[:, 32:96].rearrange("p (k l) -> p k l", k=2)
    posi = sb("posi", [P, TB], I32)
    posf = sb("posf", [P, TB])
    ssq = sb("ssq", [P, TB])
    ms = sb("ms", [P, TB])
    rt = sb("rt", [P, TB])
    rstd = sb("rstd", [P, TB])
    nt = sb("nt", [P, TB])
    base = at[0]

    w_raw = [sb(f"w_raw{i}", [P, KC, COLS]) for i in range(2)]
    w_lo = [place(f"w_lo{i}", [P, KC, COLS], F32R, base + i * 16384) for i in range(2)]
    w_hi = [sb(f"w_hi{i}", [P, KC, COLS], F32R) for i in range(2)]
    after_w = at[0]
    xs = sb("xs", [P, TB, D])
    mixed = xs
    qT = sb("qT", [P, 2, HPG, T])
    kT = sb("kT", [P, 4, T])
    vcT = sb("vcT", [P, T])
    vnat = sb("vnat", [P, TB, COLS])
    gates = sb("gates", [P, TB, HEADS, 3])
    gexp = sb("gexp", [P, TB, N_GATES])
    stage = at[0]
    cos2 = sb("cos2", [P, TB, 2, HALF])
    sin2 = sb("sin2", [P, TB, 2, HALF])
    ang = sb("ang", [P, TB, HALF])
    trn = sb("trn", [P, TB, HALF])
    red = sb("red", [P, TB, HALF])
    red2 = sb("red2", [P, TB, HALF])
    scratch = at[0]
    rp_c = [sb(f"rp_c{i}", [P, COLS]) for i in range(2)]
    rp_s = [sb(f"rp_s{i}", [P, COLS]) for i in range(2)]
    roped = [sb(f"roped{i}", [P, COLS]) for i in range(2)]
    wg_at = at[0]
    wg_raw = sb("wg_raw", [P, KC, N_GATES])
    wg_lo = place("wg_lo", [P, KC, N_GATES], F32R, wg_at)
    wg_hi = sb("wg_hi", [P, KC, N_GATES], F32R)
    w1_sb = [place("w1_k", [P, LP, CMP_HIDDEN], F32, after_w), sb("w1_v", [P, LP, CMP_HIDDEN])]
    cx = [place(f"cx{i}", [P, LP, GROUPS, NC], F32, scratch + i * 4096) for i in range(2)]
    hrep = place("hrep", [P, GROUPS * 2, 4, CP], F32, scratch + 2 * 4096)
    end_proj = at[0]
    at[0] = stage
    pr = [sb(f"pr{i}", [P, COLS]) for i in range(3)]
    pt = [sb(f"pt{i}", [P, COLS]) for i in range(2)]
    o_tmp = sb("o_tmp", [P, COLS])
    c_sc = sb("c_sc", [P, HEADS, CP])
    c_pT = sb("c_pT", [P, GROUPS, P])
    assert at[0] <= end_proj
    at[0] = end_proj
    hid = [sb(f"hid{i}", [P, GROUPS * 2, CP]) for i in range(2)]
    w2_sb = sb("w2_sb", [P, 2, 2, DH])
    kcT = sb("kcT", [P, CP])
    vbd = sb("vbd", [P, GROUPS, 4, DH])
    nmax = sb("nmax", [P, len(UNITS)])
    rsum = sb("rsum", [P, len(UNITS)])
    nsink = sb("nsink", [P, HEADS])
    es_in = sb("es_in", [P, TB, HEADS])
    es = sb("es", [P, TB, HEADS])
    coef = sb("coef", [P, HEADS])
    c_max = sb("c_max", [P, HEADS])
    c_sum = sb("c_sum", [P, HEADS])
    c_coef = sb("c_coef", [P, HEADS])
    assert at[0] <= 229368, at[0]

    at[0] = after_w + 16384
    q_sb = [sb(f"q_sb{i}", [P, T]) for i in range(2)]
    sk = sb("sk", [P, 2, NK])
    work = [sb(f"work{i}", [P, TB, NK]) for i in range(2)]
    tv = [[sb(f"tv{r}{s}", [P, TB, TOPK]) for s in range(2)] for r in range(2)]
    ti = [[sb(f"ti{r}{s}", [P, TB, TOPK], U32) for s in range(2)] for r in range(2)]
    tif = [[sb(f"tif{r}{s}", [P, TB, TOPK]) for s in range(2)] for r in range(2)]
    cand = sb("cand", [P, TB, TOPK, TOPK])
    candw = sb("candw", [P, TB, TOPK * TOPK])
    posn = sb("posn", [P, TB, TOPK], U32)
    pab = [[sb(f"pab{r}{s}", [P, TB, TOPK], U32) for s in range(2)] for r in range(2)]
    hit = [[sb(f"hit{r}{s}", [P, TB, TOPK, TOPK]) for s in range(2)] for r in range(2)]
    score = sb("score", [P, TB, PH, TOPK])
    key = [sb(f"key{s}", [P, TB, PH, TOPK]) for s in range(2)]
    g_sum = sb("g_sum", [P, TB, PH])
    slots = at[0]
    sl_key = [sb(f"sl_key{s}", [P, T], BF16) for s in range(2)]
    sl_g = [sb(f"sl_g{i}", [P, T], BF16) for i in range(3)]
    sl_r = [sb(f"sl_r{i}", [P, T]) for i in range(2)]
    assert at[0] <= 229368, at[0]

    tail = (229368 - 5 * 4096) // 32 * 32
    assert at[0] <= tail, (at[0], tail)
    at[0] = tail
    f_raw = [sb(f"f_raw{i}", [P, KC, P]) for i in range(2)]
    f_lo = [place(f"f_lo{i}", [P, KC, P], F32R, tail + i * 4096) for i in range(2)]
    f_hi = [sb(f"f_hi{i}", [P, KC, P], F32R) for i in range(2)]
    f_act = [sb(f"f_act{i}", [P, T]) for i in range(2)]

    at[0] = base
    iota_k = sb("iota_k", [P, NK, TG], BF16)
    oh = [[sb(f"oh{r}{i}", [P, NK, TG], BF16) for i in range(2)] for r in range(2)]
    gp = [[sb(f"gp{r}{i}", [P, NK, TG], BF16) for i in range(3)] for r in range(2)]
    ev = [sb(f"ev{i}", [P, NGB, TG, GB]) for i in range(2)]
    assert at[0] <= slots, (at[0], slots)

    at[0] = base
    d_raw = sb("d_raw", [P, DR, KC, P])
    d_lo = place("d_lo", [P, DR, KC, P], F32R, base)
    d_hi = sb("d_hi", [P, 2, KC, P], F32R)
    u_raw = sb("u_raw", [P, DR, D])
    u_hi = sb("u_hi", [P, GC, D], F32R)
    u_lo = sb("u_lo", [P, GC, D], F32R)
    w_e_hi = sb("w_e_hi", [P, GC, T], F32R)
    w_e_lo = sb("w_e_lo", [P, GC, T], F32R)
    a_early = place("a_early", [P, GC, T], F32, base)
    g_early = place("g_early", [P, T, GB], F32, base + DR * D * 4)
    g_sb = sb("g_sb", [P, 2, T, GB])
    a_sb = sb("a_sb", [P, 2, T])
    assert at[0] <= 229368, at[0]
    nf = place("nf", [P, D], F32, base)
    junk = place("junk", [P, D], F32, after_w + 16384)

    gates_dram = nc.dram_tensor("gates_dram", (NGB, P, T * GB), F32, kind="Internal").ap()

    act_dram = nc.dram_tensor("act_dram", (NE, P, T), F32, kind="Internal").ap()

    bank = [nc.alloc_psum_tensor(f"bank{i}", [P, 512], F32) for i in range(8)]
    sems = {}

    def S(name):
        if name not in sems:
            sems[name] = nc.alloc_semaphore(name)
        return sems[name]

    x_v = x.rearrange("(b p) d -> b p d", p=P)
    y_v = y.rearrange("(b p) d -> b p d", p=P)

    with nc.Block() as block:

        @block.sync
        def _(sp):
            for b in range(TB):
                sp.dma_start(xt[:, b], x_v[b]).then_inc(S(f"x_loaded{b}"), 16)
            sp.dma_start(cst[:], consts).then_inc(S("const_loaded"), 16)
            sp.dma_start(prm[:], params).then_inc(S("const_loaded"), 16)
            sp.dma_start(posi[:], pos).then_inc(S("const_loaded"), 16)
            sp.dma_start(cstb[:], consts_b[:, 0:384]).then_inc(S("const_loaded"), 16)
            sp.dma_start(wg_raw[:], wgate.rearrange("p (k c) -> p k c", k=KC)).then_inc(S("wg_loaded"), 16)
            def early_down(f, r):
                if not (isinstance(f, int) and f < 2):
                    sp.wait_ge(S("f_ps"), f - 1)
                sp.dma_start(f_raw[r][:], down[bass.ts(f, 1)].rearrange("o p (k e) -> p (o k) e", k=KC))\
                    .then_inc(S(f"f_loaded{r}"), 16)

            def early_store(f, r):
                sp.wait_ge(S("f_gelu"), f + 1)
                sp.dma_start(act_dram[bass.ts(f, 1)].rearrange("o p t -> p (o t)"), f_act[r][:])\
                  .then_inc(S(f"f_stored{r}"), 16)

            for i in range(TILES_IN + TILES_OUT + 2):
                if i >= 2:
                    used, count = tile_used(i - 2)
                    sp.wait_ge(S(used), count)
                sp.dma_start(w_raw[i % 2][:], wts[i].rearrange("p (k c) -> p k c", k=KC))\
                  .then_inc(S(f"w_loaded{i % 2}"), 16)
                if i == TILES_IN + TILES_OUT:
                    sp.wait_ge(S("mixed_done"), 1)
                    sp.dma_start(sk[:], subkeys.rearrange("p (s k) -> p s k", s=2)).then_inc(S("sk_loaded"), 16)
            for f in range(E_GATES + 1):
                if f == 0:
                    sp.wait_ge(S("mixed_done"), 1)
                early_down(f, f % 2)
                if f >= 2:
                    early_store(f - 2, f % 2)
                if f in (4, 8):
                    i = TILES - 2 + (f == 8)
                    used, count = tile_used(i - 2)
                    sp.wait_ge(S(used), count)
                    sp.dma_start(w_raw[i % 2][:], wts[i].rearrange("p (k c) -> p k c", k=KC))\
                      .then_inc(S(f"w_loaded{i % 2}"), 16)
                if f == E_REST + 1:
                    sp.wait_ge(S("q_ps"), 2 * PH)
                    sp.dma_start(iota_k[:], consts_b[:, 384:384 + NK * TG].rearrange("p (k t) -> p k t", t=TG))\
                      .then_inc(S("iota_loaded"), 16)
            dst = gates_dram.rearrange("b p t -> p b t")

            def store(i, r):
                sp.wait_ge(S("ev_full"), (i + 1) * (TG // PSTEP))
                sp.dma_start(dst[:, :, bass.ts(i, TG * GB)], ev[r][:].rearrange("p b t k -> p b (t k)"))\
                  .then_inc(S(f"ev_stored{r}"), 16)

            with sp.Fori(0, NTG // 2) as o:
                for r in range(2):
                    i = o * 2 + r
                    early_down(i + E_GATES + 1, 1 - r)
                    early_store(i + E_GATES - 1, 1 - r)
                    store(i, r)

            def early_up(n, c):
                if n >= 1:
                    sp.wait_ge(S("u_lo_done"), (n - 1) * GB + c + 1)
                sp.dma_start(u_raw[:, c], up[n * GB + c]).then_inc(S(f"us_loaded{c}"), 16)

            def early_acts(n):
                h = slice(n % 2 * GB, n % 2 * GB + GB)
                if n >= 2:
                    sp.wait_ge(S("w_done"), (n - 1) * GB)
                sp.dma_start(a_early[:, h], act_dram[n * GB:(n + 1) * GB].rearrange("e p t -> p e t"))\
                  .then_inc(S(f"as_loaded{n % 2}"), 16)
                if n == 0:
                    for r in range(2):
                        sp.wait_ge(S(f"ev_stored{r}"), 16 * (NTG // 2))
                else:
                    sp.wait_ge(S("w_done"), n * GB)
                sp.dma_start(g_early[:], gates_dram[n].rearrange("p (t k) -> p t k", k=GB))\
                  .then_inc(S("gs_loaded"), 16)

            sp.wait_ge(S("gate_mm"), NTG * (TG // PSTEP))
            for n in range(2):
                for c in range(GB):
                    f = E_LAST + n * GB + c
                    if f + 1 < NE:
                        early_down(f + 1, (f + 1) % 2)
                    early_store(f - 1, (f - 1) % 2)
                    early_up(n, c)
                    if c == 1:
                        if n == 0:
                            for r in range(2):
                                sp.wait_ge(S(f"f_stored{r}"), 16 * (E_GATES // 2))
                        early_acts(n)
            early_store(NE - 1, 1)
            for r in range(2):
                sp.wait_ge(S(f"f_stored{r}"), 16 * (NE // 2))
            for n in range(2, NSUB):
                for c in range(GB):
                    early_up(n, c)
                early_acts(n)
            sp.wait_ge(S("w_done"), NE)

            def loads(g, c):
                e = g * GC + c
                if not (isinstance(g, int) and e < NE + DR):
                    sp.wait_ge(S("pd_done"), e - NE - DR + 1)
                sp.dma_start(d_raw[:, c % DR], down[bass.ts(e, 1)].rearrange("o p (k e) -> p (o k) e", k=KC))\
                  .then_inc(S(f"d_loaded{c % DR}"), 16)
                sp.wait_ge(S("u_lo_done"), e - DR + 1)
                sp.dma_start(u_raw[:, c % DR], up[bass.ts(e, 1)].rearrange("o p d -> p (o d)"))\
                  .then_inc(S(f"u_loaded{c % DR}"), 16)
                if c % GB == 0:
                    b = c // GB
                    sp.wait_ge(S("w_done"), e - GB)
                    sp.dma_start(g_sb[:, b], gates_dram[bass.ts(g * 2 + b, 1)]
                                 .rearrange("o p (t k) -> p (o t) k", k=GB)).then_inc(S(f"g_loaded{b}"), 16)

            for c in range(GC):
                loads(G0, c)
            with sp.Fori(G0 + 1, NG) as g:
                for c in range(GC):
                    loads(g, c)
            sp.wait_ge(S("acc_done"), banks_before(NG))
            sp.dma_start(nf[:], normf.partition_broadcast(P).rearrange("p o d -> p (o d)")).then_inc(S("nf_loaded"), 16)
            for b in range(TB):
                sp.wait_ge(S("y_done"), b + 1)
                sp.dma_start(y_v[b], xt[:, b]).then_inc(S("y_stored"), 16)
            sp.wait_ge(S("y_stored"), 16 * TB)

        @block.gpsimd
        def _(pool):
            pool.dma_start(w2_sb[:], w2.rearrange("p (k h d) -> p k h d", k=2, h=2)).then_inc(S("w2_loaded"), 16)
            pool.dma_start(w1_sb[1][:], w1[1].rearrange("p (l h) -> p l h", l=LP)).then_inc(S("w1v_loaded"), 16)
            pool.wait_ge(S("hT_ps"), KC)
            pool.dma_start(w1_sb[0][:], w1[0].rearrange("p (l h) -> p l h", l=LP)).then_inc(S("w1k_loaded"), 16)
            def early_low(f, r):
                pool.wait_ge(S("f_hi_done"), f + 1)
                nc.gpsimd.tensor_tensor(f_lo[r][:], f_raw[r][:], f32(f_hi[r][:]), ALU.subtract)\
                    .then_inc(S("f_lo_done"), 1)

            def chosen_keys(hd):
                r = hd % 2
                for s in range(2):
                    pool.wait_ge(S("hit_eq"), 2 * hd + s + 1)
                    nc.gpsimd.tensor_tensor(
                        hit[r][s][:], hit[r][s][:],
                        tif[r][s][:].unsqueeze(2).broadcast_to([P, TB, TOPK, TOPK]), ALU.mult)\
                        .then_inc(S("hit_done"), 1)

            for f in range(E_GATES):
                early_low(f, f % 2)
                if f in POOL_KEYS:
                    chosen_keys(POOL_KEYS[f])
            chosen_keys(PH - 1)
            with pool.Fori(0, NTG // 2) as o:
                for r in range(2):
                    early_low(o * 2 + r + E_GATES, r)
            for f in range(E_LAST, NE):
                early_low(f, f % 2)

        @block.scalar
        def _(act):
            def split_w(i):
                act.wait_ge(S(f"w_loaded{i % 2}"), 16 * (i // 2 + 1))
                if i >= 2:
                    used, count = tile_used(i - 2)
                    act.wait_ge(S(used), count)
                nc.scalar.activation(w_hi[i % 2][:], w_raw[i % 2][:], ACT.Copy).then_inc(S("w_hi_done"), 1)

            def rms(n):
                for b in range(TB):
                    if n == 0:
                        act.wait_ge(S(f"x_loaded{b}"), 16)
                    else:
                        act.wait_ge(S("x1_done") if n == 1 else S("acc_done"),
                                    TB + b + 1 if n == 1 else banks_before(NG - 1) + 2 * b + 2)
                    if n * TB + b:
                        act.wait_ge(S("ssq_done"), n * TB + b)
                    squares = junk[:] if n < 2 else a_sb[:].rearrange("p a t -> p (a t)")
                    nc.scalar.activation(squares, xt[:, b], ACT.Square, accum_out=ssq[:, b:b + 1])\
                      .then_inc(S("ssq_done"), 1)
                act.wait_ge(S("ms_done"), n + 1)
                nc.scalar.activation(rt[:], ms[:], ACT.Sqrt).then_inc(S("root_done"), 1)

            def evac_hi(rep, gain):
                for k in range(KC):
                    act.wait_ge(S("hT_ps"), rep * KC + k + 1)
                    nc.scalar.activation(h_hi[:, k], bank[k][:], ACT.Copy,
                                         **({} if gain is None else {"scale": gain[:, k:k + 1]}))\
                      .then_inc(S("h_hi_done"), 1)

            rms(0)
            act.wait_ge(S("wg_loaded"), 16)
            nc.scalar.activation(wg_hi[:], wg_raw[:], ACT.Copy).then_inc(S("wg_hi_done"), 1)
            split_w(0)
            act.wait_ge(S("const_loaded"), 64)
            evac_hi(0, g_attn)
            split_w(1)
            act.wait_ge(S("angles"), 2)
            for i, (dst, src) in enumerate(((sin2, red), (cos2, red2))):
                for half in range(2):
                    nc.scalar.activation(dst[:, :, half], src[:], ACT.Sin,
                                         scale=-1.0 if i == 0 and half == 0 else 1.0).then_inc(S("tables"), 1)

            def evac_T(u):
                n, b = divmod(u, TB)
                act.wait_ge(S("tT_done"), u + 1)
                src = bank[4 + u % 2][:].rearrange("p (j t) -> p j t", j=4)
                if n < 2:
                    nc.scalar.activation(qT[:, n, :, b * P:(b + 1) * P], src, ACT.Copy, scale=DH ** -0.5)\
                      .then_inc(S("evT"), 1)
                else:
                    nc.scalar.activation(kT[:, :, b * P:(b + 1) * P], src, ACT.Copy).then_inc(S("evT"), 1)

            for u in range(16):
                if u >= 1 and u <= 12:
                    evac_T(u - 1)
                if u >= 12:
                    act.wait_ge(S("pj_done"), u + 1)
                    nc.scalar.activation(vnat[:, u - 12], bank[u % 4][:], ACT.Copy).then_inc(S("v_done"), 1)
                if u == 5:
                    split_w(2)
                if u == 9:
                    split_w(3)
            act.wait_ge(S("tT_done"), 13)
            nc.scalar.activation(vcT[:], bank[4][:], ACT.Copy).then_inc(S("evT"), 1)
            act.wait_ge(S("pj_done"), 17)
            nc.scalar.activation(gexp[:], bank[0][:, 0:TB * N_GATES].rearrange("p (b g) -> p b g", b=TB),
                                 ACT.Exp, scale=-1.0).then_inc(S("gexp_done"), 1)
            for kv in range(2):
                act.wait_ge(S("hid_done"), kv + 1)
                if kv == 0:
                    act.wait_ge(S("pads"), 2)
                nc.scalar.activation(hid[kv][:, :, 0:NC],
                                     bank[6 + kv][:, 0:4 * NC].rearrange("p (j c) -> p j c", j=4),
                                     ACT.Gelu).then_inc(S("hid_act"), 1)
            act.wait_ge(S("cmp_ps"), 1)
            nc.scalar.activation(kcT[:, 0:NC], bank[4][:, 0:NC], ACT.Copy).then_inc(S("kc_done"), 1)
            split_w(4)
            split_w(5)

            for s in range(len(UNITS) + 12):
                qb, in_qb = divmod(s, STEP_QB)
                if s < len(UNITS):
                    n = width(*UNITS[s][:2])
                    act.wait_ge(S("max_done"), s + 1)
                    if s >= 3:
                        act.wait_ge(S("pT_ps"), s - 2)
                    nc.scalar.activation(pr[s % 3][:, 0:n], bank[s % 3][:, 0:n], ACT.Exp,
                                         bias=nmax[:, s:s + 1], accum_out=rsum[:, s:s + 1])\
                      .then_inc(S("exp_done"), 1)
                    if in_qb == 2:
                        act.wait_ge(S("c_shift"), qb + 1)
                        nc.scalar.activation(c_sc[:, :, 0:NC], c_sc[:, :, 0:NC], ACT.Exp)\
                          .then_inc(S("c_exp"), 1)
                    if in_qb == 7:
                        act.wait_ge(S("c_T"), qb + 1)
                        nc.scalar.activation(c_pT[:], bank[7][:, 256:512].rearrange("p (g t) -> p g t", g=2),
                                             ACT.Copy).then_inc(S("c_pT_done"), 1)
                if 2 <= s < len(UNITS) + 2 and s % 2 == 0:
                    u = s - 2
                    n = width(*UNITS[u][:2])
                    act.wait_ge(S("pT_ps"), u + 1)
                    if u >= 2:
                        act.wait_ge(S("pv_done"), u - 1)
                    nc.scalar.activation(pt[0][:, 0:n], bank[3][:, 0:n], ACT.Copy).then_inc(S("pt_done0"), 1)
                if in_qb == HEADS + 1 and qb < TB:
                    act.wait_ge(S("es_in_done"), qb + 1)
                    nc.scalar.activation(es[:, qb], es_in[:, qb], ACT.Exp).then_inc(S("es_done"), 1)

            evac_hi(1, None)
            split_w(6)
            rms(1)
            evac_hi(2, g_ffn)
            split_w(7)
            def early_high(f, r):
                act.wait_ge(S(f"f_loaded{r}"), (f - r) * 8 + 16)
                nc.scalar.activation(f_hi[r][:], f_raw[r][:], ACT.Copy).then_inc(S("f_hi_done"), 1)

            def early_gelu(f, r):
                act.wait_ge(S("f_ps"), f + 1)
                if not (isinstance(f, int) and f < 2):
                    act.wait_ge(S(f"f_stored{r}"), (f - r) * 8)
                nc.scalar.activation(f_act[r][:], bank[6 + r][:], ACT.Gelu).then_inc(S("f_gelu"), 1)

            for v in range(2 * PH):
                if v >= 1:
                    early_gelu(v - 1, (v - 1) % 2)
                early_high(v, v % 2)
                act.wait_ge(S("q_ps"), v + 1)
                if v >= 2:
                    act.wait_ge(S("s_ps"), v - 1)
                nc.scalar.activation(q_sb[v % 2][:], bank[v % 2][:], ACT.Copy).then_inc(S("q_done"), 1)
                if v == 3:
                    split_w(8)
                if v == 7:
                    split_w(9)
            for f in range(E_REST, E_GATES):
                early_gelu(f - 1, (f - 1) % 2)
                early_high(f, f % 2)
            act.wait_ge(S("score_shift"), 1)
            nc.scalar.activation(score[:], score[:], ACT.Exp).then_inc(S("score_exp"), 1)
            def evac_gates(i, r, q):
                n = i * (TG // PSTEP) + q
                act.wait_ge(S("gate_mm"), n + 1)
                if q == 0:
                    wait_slot(i, r)
                src = bank[2 + q % 4][:].rearrange("p (t b k) -> p t b k", t=PSTEP, k=GB)
                dst = ev[r][:, :, q * PSTEP:(q + 1) * PSTEP].rearrange("p b t k -> p t b k")
                nc.scalar.activation(dst, src, ACT.Copy).then_inc(S("ev_full"), 1)

            def wait_slot(i, r):
                if not (isinstance(i, int) and i < 2):
                    act.wait_ge(S(f"ev_stored{r}"), (i - r) * 8)

            def gate_step(i, r):
                f = i + E_GATES
                early_gelu(f - 1, 1 - r)
                early_high(f, r)
                for q in range(TG // PSTEP):
                    evac_gates(i, r, q)

            for i in range(2):
                gate_step(i, i)
            with act.Fori(1, NTG // 2) as o:
                for r in range(2):
                    gate_step(o * 2 + r, r)

            def early_u_high(n, c):
                act.wait_ge(S(f"us_loaded{c}"), 16 * (n + 1))
                if n >= 2:
                    act.wait_ge(S("pu_done"), 8 * (n - 1))
                nc.scalar.activation(u_hi[:, n % 2 * GB + c], u_raw[:, c], ACT.Copy).then_inc(S("u_hi_done"), 1)

            for f in range(E_LAST, NE):
                early_gelu(f - 1, (f - 1) % 2)
                early_high(f, f % 2)
                early_u_high((f - E_LAST) // GB, f % GB)
            early_gelu(NE - 1, 1)
            for n in range(2, NSUB):
                for c in range(GB):
                    early_u_high(n, c)

            def d_high(g, c):
                e = g * GC + c
                act.wait_ge(S(f"d_loaded{c % DR}"), ((g - G0) * 2 + c // DR + 1) * 16)
                if not (isinstance(g, int) and e < NE + 2):
                    act.wait_ge(S("pd_done"), e - NE - 1)
                nc.scalar.activation(d_hi[:, c % 2], d_raw[:, c % DR], ACT.Copy).then_inc(S("d_hi_done"), 1)

            def group(g, last):
                for c in range(GC):
                    e = g * GC + c
                    act.wait_ge(S(f"u_loaded{c % DR}"), ((g - G0) * 2 + c // DR + 1) * 16)
                    if c == 0:
                        act.wait_ge(S("pu_done"), banks_before(g))
                    nc.scalar.activation(u_hi[:, c], u_raw[:, c % DR], ACT.Copy).then_inc(S("u_hi_done"), 1)
                    act.wait_ge(S("pd_done"), e - NE + 1)
                    act.wait_ge(S("w_done"), e - 1)
                    nc.scalar.activation(a_sb[:, c % 2], bank[c % 2][:], ACT.Gelu).then_inc(S("gelu_done"), 1)
                    if c < GC - 2:
                        d_high(g, c + 2)
                    elif not last:
                        d_high(g + 1, c + 2 - GC)

            d_high(G0, 0)
            d_high(G0, 1)
            group(G0, False)
            with act.Fori(G0 + 1, NG - 1) as g:
                group(g, False)
            group(NG - 1, True)
            rms(2)

        @block.vector
        def _(dve):
            done = [0]

            def link(ins):
                done[0] += 1
                ins.then_inc(S("dve_link"), 1)
                dve.wait_ge(S("dve_link"), done[0])

            V = nc.vector

            def split_w(i):
                dve.wait_ge(S("w_hi_done"), i + 1)
                V.tensor_tensor(w_lo[i % 2][:], w_raw[i % 2][:], f32(w_hi[i % 2][:]), ALU.subtract)\
                 .then_inc(S("w_lo_done"), 1)

            def rstd_of(n):
                dve.wait_ge(S("ssq_done"), TB * (n + 1))
                V.tensor_scalar(ms[:], ssq[:], 1.0 / D, EPS, ALU.mult, ALU.add).then_inc(S("ms_done"), 1)
                dve.wait_ge(S("root_done"), n + 1)
                link(V.reciprocal(rstd[:], rt[:]))
                link(V.tensor_tensor(nt[:], rstd[:], rstd[:], ALU.mult))
                link(V.tensor_tensor(nt[:], nt[:], ms[:], ALU.mult))
                link(V.tensor_scalar(nt[:], nt[:], -0.5, 1.5, ALU.mult, ALU.add))
                link(V.tensor_tensor(rstd[:], rstd[:], nt[:], ALU.mult))

            def scale_rows(n):
                for b in range(TB):
                    V.tensor_scalar(xs[:, b], xt[:, b], rstd[:, b:b + 1], None, ALU.mult)\
                     .then_inc(S("xs_done"), 1)

            def evac_lo(rep, gain):
                for k in range(KC):
                    dve.wait_ge(S("h_hi_done"), rep * KC + k + 1)
                    if gain is None:
                        V.tensor_tensor(h_lo[:, k], bank[k][:], f32(h_hi[:, k]), ALU.subtract)\
                         .then_inc(S("h_lo_done"), 1)
                    else:
                        V.scalar_tensor_tensor(h_lo[:, k], bank[k][:], gain[:, k:k + 1], f32(h_hi[:, k]),
                                               ALU.mult, ALU.subtract).then_inc(S("h_lo_done"), 1)

            dve.wait_ge(S("const_loaded"), 64)
            link(V.tensor_copy(posf[:], posi[:]))
            link(V.tensor_tensor(ang[:], posf[:].unsqueeze(2).broadcast_to([P, TB, HALF]),
                                 inv_freq.unsqueeze(1).broadcast_to([P, TB, HALF]), ALU.mult))
            link(V.tensor_scalar(trn[:], ang[:], 1.0 / TWO_PI, ROUND, ALU.mult, ALU.add))
            link(V.tensor_scalar(trn[:], trn[:], ROUND, None, ALU.subtract))
            link(V.scalar_tensor_tensor(red[:], trn[:], -PI_A, ang[:], ALU.mult, ALU.add))
            link(V.scalar_tensor_tensor(red[:], trn[:], -PI_B, red[:], ALU.mult, ALU.add))
            link(V.scalar_tensor_tensor(red[:], trn[:], -PI_C, red[:], ALU.mult, ALU.add))
            link(V.tensor_scalar(red2[:], red[:], np.pi / 2, None, ALU.add))
            link(V.tensor_scalar(trn[:], red2[:], float(np.pi), -TWO_PI, ALU.is_gt, ALU.mult))
            link(V.tensor_tensor(red2[:], red2[:], trn[:], ALU.add))
            for t in (red, red2):
                V.tensor_scalar(t[:], t[:], PI_CLAMP, -PI_CLAMP, ALU.min, ALU.max).then_inc(S("angles"), 1)

            rstd_of(0)
            scale_rows(0)
            dve.wait_ge(S("wg_hi_done"), 1)
            V.tensor_tensor(wg_lo[:], wg_raw[:], f32(wg_hi[:]), ALU.subtract).then_inc(S("wg_lo_done"), 1)
            split_w(0)
            evac_lo(0, g_attn)
            split_w(1)

            dve.wait_ge(S("tables"), 4)
            heads = lambda ap: ap.rearrange("p (h f d) -> p h f d", h=HEADS, f=2)
            for u in range(12):
                b = u % TB
                dve.wait_ge(S("pj_done"), u + 1)
                if u >= 2:
                    dve.wait_ge(S("rope_done"), u - 1)
                ps = heads(bank[u % 4][:])
                c_b = cos2[:, b].rearrange("p f d -> p (f d)").unsqueeze(1).broadcast_to([P, HEADS, DH])
                V.tensor_tensor(rp_c[u % 2][:].rearrange("p (h d) -> p h d", h=HEADS),
                                bank[u % 4][:].rearrange("p (h d) -> p h d", h=HEADS), c_b, ALU.mult)
                for half in range(2):
                    ins = V.tensor_tensor(heads(rp_s[u % 2][:])[:, :, half], ps[:, :, 1 - half],
                                          sin2[:, b, half].unsqueeze(1).broadcast_to([P, HEADS, HALF]), ALU.mult)
                ins.then_inc(S("pj_free"), 1)
                dve.wait_ge(S("pj_free"), u + 1)
                if u >= 2:
                    dve.wait_ge(S("tT_done"), u - 1)
                V.tensor_tensor(roped[u % 2][:], rp_c[u % 2][:], rp_s[u % 2][:], ALU.add).then_inc(S("rope_done"), 1)
                if u == 5:
                    split_w(2)
                if u == 9:
                    split_w(3)
            V.memset(kcT[:], 0.0)
            link(V.memset(vbd[:], 0.0))
            V.memset(hid[0][:], 0.0).then_inc(S("pads"), 1)
            V.memset(hid[1][:], 0.0).then_inc(S("pads"), 1)
            V.tensor_scalar(nsink[:], sinks, -1.0, None, ALU.mult)
            for kv in range(2):
                dve.wait_ge(S("evT"), 12 + kv)
                src = (kT[:, 1] if kv == 0 else vcT[:]).rearrange("p (c l f) -> p l f c", l=CMP_STRIDE // 2, f=2)
                emb = cmp_pos[:, kv].rearrange("p (l f) -> p l f", f=2)
                for g in range(GROUPS):
                    rows = slice(DH * g, DH * g + DH)
                    for par in range(2):
                        for part in range(2):
                            ls = slice(part * LP // 2, (part + 1) * LP // 2)
                            V.tensor_tensor(cx[kv][DH * par:DH * par + DH, ls, g],
                                            src[rows, :, par, part:part + NC],
                                            emb[rows, ls, par].unsqueeze(2).broadcast_to([DH, LP // 2, NC]),
                                            ALU.add).then_inc(S("cx_done"), 1)
            dve.wait_ge(S("gexp_done"), 1)
            link(V.tensor_scalar(gexp[:], gexp[:], 1.0, None, ALU.add))
            link(V.reciprocal(gates[:].rearrange("p b h k -> p b (h k)"), gexp[:]))
            dve.wait_ge(S("hid_act"), 2)
            dve.wait_ge(S("hid_done"), 2)
            V.tensor_copy(hrep[:], hid[1][:].unsqueeze(2).broadcast_to([P, GROUPS * 2, 4, CP]))\
             .then_inc(S("hrep_done"), 1)
            dve.wait_ge(S("cmp_ps"), 2)
            for g in range(GROUPS):
                for j in range(HPG):
                    q = slice(CP * j, CP * j + CP)
                    V.tensor_copy(vbd[q, g, j], bank[5][q, g * DH:(g + 1) * DH]).then_inc(S("vbd_done"), 1)
            split_w(4)
            split_w(5)
            link(V.memset(c_sc[:], 0.0))

            def finish(gi):
                qb, br = gi // 3, gi % 3
                sl = slice(gi * HEADS, (gi + 1) * HEADS)
                o = bank[5 + gi % 2][:].rearrange("p (h d) -> p h d", h=HEADS)
                co = coef[:].unsqueeze(2).broadcast_to([P, HEADS, DH])
                out_a = mixed[:, qb, 0:COLS].rearrange("p (h d) -> p h d", h=HEADS)
                out_b = mixed[:, qb, COLS:2 * COLS]
                dve.wait_ge(S("exp_done"), 8 * gi + 8)
                if gi >= 1:
                    dve.wait_ge(S("o_free"), gi)
                if br == SWA:
                    dve.wait_ge(S("es_done"), qb + 1)
                    link(V.tensor_tensor(coef[:], rsum[:, sl], es[:, qb], ALU.add))
                    link(V.reciprocal(coef[:], coef[:]))
                else:
                    link(V.reciprocal(coef[:], rsum[:, sl]))
                    link(V.tensor_tensor(coef[:], coef[:], gates[:, qb, :, br], ALU.mult))
                dve.wait_ge(S("pv_done"), 8 * gi + 8)
                if br == SWA:
                    V.tensor_tensor(out_a, o, co, ALU.mult).then_inc(S("o_free"), 1)
                else:
                    V.tensor_tensor(o_tmp[:].rearrange("p (h d) -> p h d", h=HEADS), o, co, ALU.mult)\
                     .then_inc(S("o_free"), 1)
                    dve.wait_ge(S("o_free"), gi + 1)
                    dve.wait_ge(S("c_mixed"), qb + 1)
                    link(V.tensor_tensor(out_b, out_b, o_tmp[:], ALU.add))

            for s in range(len(UNITS) + 12):
                qb, in_qb = divmod(s, STEP_QB)
                if s < len(UNITS):
                    _, br, h = UNITS[s]
                    n = width(qb, br)
                    dve.wait_ge(S("s_done"), s + 1)
                    if br == SWA:
                        link(V.tensor_reduce(nmax[:, s:s + 1], bank[s % 3][:, 0:n], X_AXIS, ALU.max, negate=True))
                        V.tensor_tensor(nmax[:, s:s + 1], nmax[:, s:s + 1], nsink[:, h:h + 1], ALU.min)\
                         .then_inc(S("max_done"), 1)
                    else:
                        V.tensor_reduce(nmax[:, s:s + 1], bank[s % 3][:, 0:n], X_AXIS, ALU.max, negate=True)\
                         .then_inc(S("max_done"), 1)
                    if in_qb == 1:
                        dve.wait_ge(S("c_s"), qb + 1)
                        if qb >= 1:
                            dve.wait_ge(S("c_T"), qb)
                        cs = c_sc[:, :, 0:NC]
                        link(V.tensor_tensor(cs, bank[7][:, 0:HEADS * CP].rearrange("p (h c) -> p h c", h=HEADS)[:, :, 0:NC],
                                             cmp_neg[:, qb, 0:NC].unsqueeze(1).broadcast_to([P, HEADS, NC]), ALU.add))
                        link(V.tensor_reduce(c_max[:], cs, X_AXIS, ALU.max))
                        V.tensor_tensor(cs, cs, c_max[:].unsqueeze(2).broadcast_to([P, HEADS, NC]), ALU.subtract)\
                         .then_inc(S("c_shift"), 1)
                    if in_qb == 3:
                        dve.wait_ge(S("c_exp"), qb + 1)
                        V.tensor_tensor(cs, cs, cmp_vis[:, qb, 0:NC].unsqueeze(1).broadcast_to([P, HEADS, NC]), ALU.mult)\
                         .then_inc(S("c_p"), 1)
                        dve.wait_ge(S("c_p"), qb + 1)
                        link(V.tensor_reduce(c_sum[:], cs, X_AXIS, ALU.add))
                        link(V.tensor_scalar(c_sum[:], c_sum[:], 1e-30, None, ALU.max))
                        link(V.reciprocal(c_sum[:], c_sum[:]))
                        if qb >= 1:
                            dve.wait_ge(S("c_mixed"), qb)
                        link(V.tensor_tensor(c_coef[:], c_sum[:], gates[:, qb, :, 0], ALU.mult))
                    if in_qb == 12:
                        dve.wait_ge(S("c_o"), qb + 1)
                        V.tensor_tensor(mixed[:, qb, COLS:2 * COLS].rearrange("p (h d) -> p h d", h=HEADS),
                                        bank[7][:].rearrange("p (h d) -> p h d", h=HEADS),
                                        c_coef[:].unsqueeze(2).broadcast_to([P, HEADS, DH]), ALU.mult)\
                         .then_inc(S("c_mixed"), 1)
                if 2 <= s < len(UNITS) + 2 and s % 2 == 1:
                    u = s - 2
                    n = width(*UNITS[u][:2])
                    dve.wait_ge(S("pT_ps"), u + 1)
                    if u >= 2:
                        dve.wait_ge(S("pv_done"), u - 1)
                    V.tensor_copy(pt[1][:, 0:n], bank[4][:, 0:n]).then_inc(S("pt_done1"), 1)
                if in_qb == HEADS and qb < TB:
                    dve.wait_ge(S("max_done"), s)
                    V.tensor_tensor(es_in[:, qb], sinks, nmax[:, qb * STEP_QB:qb * STEP_QB + HEADS], ALU.add)\
                     .then_inc(S("es_in_done"), 1)
                if s >= 11 and (s - 11) % HEADS == 0 and (s - 11) // HEADS < 3 * TB:
                    finish((s - 11) // HEADS)
            V.tensor_copy(nt[:, 0:1], mixed[:, TB - 1, D - 1:D]).then_inc(S("mixed_done"), 1)
            evac_lo(1, None)
            for n in range(2 * TB):
                half, b = divmod(n, TB)
                dve.wait_ge(S("wo_ps"), n + 1)
                o = xt[:, b, half * COLS:(half + 1) * COLS]
                V.tensor_tensor(o, o, bank[n % 4][:], ALU.add).then_inc(S("x1_done"), 1)
                if n == 3:
                    split_w(6)
            rstd_of(1)
            scale_rows(1)
            evac_lo(2, g_ffn)
            split_w(7)

            LOW = -3.0e38

            def keys_of(hd):
                r = hd % 2
                for s in range(2):
                    dve.wait_ge(S("hit_done"), 2 * hd + s + 1)
                    V.tensor_reduce(key[s][:, :, hd], hit[r][s][:], X_AXIS, ALU.add).then_inc(S("key_done"), 1)

            def top16(vals, idx, src, tmp):
                for b in range(TB):
                    V.max(vals[b][:, 0:8], src[b]).then_inc(S("top_a"), 1)
                top_count[0] += TB
                for b in range(TB):
                    dve.wait_ge(S("top_a"), top_count[0] - TB + b + 1)
                    V.max_index(idx[b][:, 0:8], vals[b][:, 0:8], src[b])
                    V.match_replace(tmp[b], vals[b][:, 0:8], src[b], LOW).then_inc(S("top_b"), 1)
                for b in range(TB):
                    dve.wait_ge(S("top_b"), top_count[0] - TB + b + 1)
                    V.max(vals[b][:, 8:16], tmp[b]).then_inc(S("top_c"), 1)
                for b in range(TB):
                    dve.wait_ge(S("top_c"), top_count[0] - TB + b + 1)
                    last = V.max_index(idx[b][:, 8:16], vals[b][:, 8:16], tmp[b])
                return last

            top_count = [0]
            for hd in range(PH):
                r = hd % 2
                for s in range(2):
                    v = 2 * hd + s
                    dve.wait_ge(S("s_ps"), v + 1)
                    src = bank[2 + v % 4]
                    if v >= 2:
                        dve.wait_ge(S("s_free"), v - 1)
                    if hd >= 2:
                        dve.wait_ge(S("hit_done"), 2 * (hd - 2) + s + 1)
                    top16([tv[r][s][:, b] for b in range(TB)], [ti[r][s][:, b] for b in range(TB)],
                          [src[:, b * NK:(b + 1) * NK] for b in range(TB)],
                          [work[s][:, b] for b in range(TB)]).then_inc(S("s_free"), 1)
                dve.wait_ge(S("s_free"), 2 * hd + 2)
                for b in range(TB):
                    V.tensor_tensor(cand[:, b], tv[r][0][:, b].unsqueeze(2).broadcast_to([P, TOPK, TOPK]),
                                    tv[r][1][:, b].unsqueeze(1).broadcast_to([P, TOPK, TOPK]), ALU.add)\
                     .then_inc(S("cand_done"), 1)
                dve.wait_ge(S("cand_done"), TB * (hd + 1))
                link(top16([score[:, b, hd] for b in range(TB)], [posn[:, b] for b in range(TB)],
                           [cand[:, b].rearrange("p i j -> p (i j)") for b in range(TB)],
                           [candw[:, b] for b in range(TB)]))
                V.tensor_copy(tif[r][0][:], ti[r][0][:])
                V.tensor_copy(tif[r][1][:], ti[r][1][:])
                V.tensor_scalar(pab[r][0][:], posn[:], 4, None, ALU.logical_shift_right)
                link(V.tensor_scalar(pab[r][1][:], posn[:], TOPK - 1, None, ALU.bitwise_and))
                if hd >= 2:
                    dve.wait_ge(S("key_done"), 2 * (hd - 1))
                for s in range(2):
                    V.tensor_tensor(hit[r][s][:].rearrange("p b k r -> p (b k) r"),
                                    pab[r][s][:].rearrange("p b k -> p (b k)").unsqueeze(2)
                                    .broadcast_to([P, TB * TOPK, TOPK]),
                                    iota16.unsqueeze(1).broadcast_to([P, TB * TOPK, TOPK]), ALU.is_equal)\
                     .then_inc(S("hit_eq"), 1)
                if hd >= 1:
                    keys_of(hd - 1)
                if hd == 1:
                    split_w(8)
                if hd == 3:
                    split_w(9)
            link(V.tensor_copy(g_sum[:], score[:, :, :, 0]))
            sv = score[:].rearrange("p b h k -> p (b h) k")
            gv = g_sum[:].rearrange("p b h -> p (b h)").unsqueeze(2).broadcast_to([P, TB * PH, TOPK])
            V.tensor_tensor(sv, sv, gv, ALU.subtract).then_inc(S("score_shift"), 1)
            keys_of(PH - 1)
            dve.wait_ge(S("score_exp"), 1)
            link(V.tensor_reduce(g_sum[:].rearrange("p b h -> p (b h)"), sv, X_AXIS, ALU.add))
            link(V.reciprocal(g_sum[:], g_sum[:]))
            V.tensor_tensor(sv, sv, gv, ALU.mult).then_inc(S("gate_done"), 1)
            dve.wait_ge(S("slot_ps"), 3)
            V.tensor_copy(sl_key[0][:], bank[1][:]).then_inc(S("slot_done"), 1)
            V.tensor_copy(sl_key[1][:], bank[2][:]).then_inc(S("slot_done"), 1)
            link(V.tensor_copy(sl_g[0][:], bank[0][:]))
            link(V.tensor_tensor(sl_r[0][:], bank[0][:], sl_g[0][:], ALU.subtract))
            link(V.tensor_copy(sl_g[1][:], sl_r[0][:]))
            link(V.tensor_tensor(sl_r[1][:], sl_r[0][:], sl_g[1][:], ALU.subtract))
            link(V.tensor_copy(sl_g[2][:], sl_r[1][:]))
            dve.wait_ge(S("iota_loaded"), 16)

            def one_hots(i, r):
                if not (isinstance(i, int) and i < 2):
                    dve.wait_ge(S("gate_mm"), (i - 1) * (TG // PSTEP))
                tok = bass.ts(i, TG)
                cols = lambda t: t[:, tok].unsqueeze(1).broadcast_to([P, NK, TG])
                V.tensor_tensor(oh[r][0][:], iota_k[:], cols(sl_key[0]), ALU.is_equal).then_inc(S("oh_a"), 1)
                V.tensor_tensor(oh[r][1][:], iota_k[:], cols(sl_key[1]), ALU.is_equal)
                dve.wait_ge(S("oh_a"), i + 1)
                for j in range(3):
                    ins = V.tensor_tensor(gp[r][j][:], oh[r][0][:], cols(sl_g[j]), ALU.mult)
                ins.then_inc(S("oh_done"), 1)

            for i in range(2):
                one_hots(i, i)
            with dve.Fori(1, NTG // 2) as o:
                for r in range(2):
                    one_hots(o * 2 + r, r)

            def accumulate(before, n):
                dve.wait_ge(S("pu_done"), before + n + 1)
                o = xt[:, n // 2, (n % 2) * COLS:(n % 2 + 1) * COLS]
                V.tensor_tensor(o, o, bank[4 + n % 4][:], ALU.add).then_inc(S("acc_done"), 1)

            def early_u_low(n, c):
                e, j = n * GB + c, n % 2 * GB + c
                dve.wait_ge(S("u_hi_done"), e + 1)
                V.tensor_tensor(u_lo[:, j], u_raw[:, c], f32(u_hi[:, j]), ALU.subtract).then_inc(S("u_lo_done"), 1)

            def early_weights(n, c):
                e, j = n * GB + c, n % 2 * GB + c
                dve.wait_ge(S("gs_loaded"), 16 * (n + 1))
                dve.wait_ge(S(f"as_loaded{n % 2}"), 16 * (n // 2 + 1))
                V.tensor_tensor(a_early[:, j], a_early[:, j], g_early[:, :, c], ALU.mult).then_inc(S("w_step"), 1)
                dve.wait_ge(S("w_step"), 2 * e + 1)
                V.tensor_copy(w_e_hi[:, j], a_early[:, j]).then_inc(S("w_step"), 1)
                dve.wait_ge(S("w_step"), 2 * e + 2)
                V.tensor_tensor(w_e_lo[:, j], a_early[:, j], f32(w_e_hi[:, j]), ALU.subtract).then_inc(S("w_done"), 1)

            def d_low(g, c):
                e = (g - G0) * GC + c
                dve.wait_ge(S("d_hi_done"), e + 1)
                V.tensor_tensor(d_lo[:, c % DR], d_raw[:, c % DR], f32(d_hi[:, c % 2]), ALU.subtract)\
                 .then_inc(S("d_lo_done"), 1)

            def group(g, last):
                for c in range(GC):
                    e, b = g * GC + c, c // GB
                    dve.wait_ge(S("u_hi_done"), e + 1)
                    V.tensor_tensor(u_lo[:, c], u_raw[:, c % DR], f32(u_hi[:, c]), ALU.subtract)\
                     .then_inc(S("u_lo_done"), 1)
                    dve.wait_ge(S("gelu_done"), e - NE + 1)
                    if c % GB == 0:
                        dve.wait_ge(S(f"g_loaded{b}"), 16 * (g - G0) + 16)
                    V.tensor_tensor(a_sb[:, c % 2], a_sb[:, c % 2], g_sb[:, b, :, c % GB], ALU.mult)\
                     .then_inc(S("w_step"), 1)
                    dve.wait_ge(S("w_step"), 2 * e + 1)
                    V.tensor_copy(w_e_hi[:, c], a_sb[:, c % 2]).then_inc(S("w_step"), 1)
                    dve.wait_ge(S("w_step"), 2 * e + 2)
                    V.tensor_tensor(w_e_lo[:, c], a_sb[:, c % 2], f32(w_e_hi[:, c]), ALU.subtract)\
                     .then_inc(S("w_done"), 1)
                    if c < GC - 2:
                        d_low(g, c + 2)
                    elif not last:
                        d_low(g + 1, c + 2 - GC)
                for n in range(8):
                    accumulate(banks_before(g), n)

            for c in range(GB):
                early_u_low(0, c)
            for c in range(GB):
                early_weights(0, c)
            for n in range(NSUB):
                for c in range(GB):
                    if n + 1 < NSUB:
                        early_u_low(n + 1, c)
                for c in range(GB):
                    if n + 1 < NSUB:
                        early_weights(n + 1, c)
                    elif c < 2:
                        d_low(G0, c)
                    accumulate(8 * n, 2 * c)
                    accumulate(8 * n, 2 * c + 1)
            group(G0, False)
            with dve.Fori(G0 + 1, NG - 1) as g:
                group(g, False)
            group(NG - 1, True)
            rstd_of(2)
            dve.wait_ge(S("nf_loaded"), 16)
            for b in range(TB):
                V.scalar_tensor_tensor(xt[:, b], xt[:, b], rstd[:, b:b + 1], nf[:], ALU.mult, ALU.mult)\
                 .then_inc(S("y_done"), 1)

        @block.tensor
        def _(pe):
            def transposes(rep, src):
                for b in range(TB):
                    if rep != 1:
                        pe.wait_ge(S("xs_done"), (rep // 2) * TB + b + 1)
                    for k in range(KC):
                        t = nc.tensor.transpose(bank[k][:, b * P:(b + 1) * P], src[:, b, k * P:(k + 1) * P], ident)
                        if b == TB - 1:
                            t.then_inc(S("hT_ps"), 1)

            def mm3(out, a_hi, a_lo, b_hi, b_lo, n, last):
                for j, (a, b) in enumerate(((a_hi, b_hi), (a_hi, b_lo), (a_lo, b_hi))):
                    m = nc.tensor.matmul(out, a, b, start=(n == 0 and j == 0), stop=(n == last and j == 2))
                return m

            pe.wait_ge(S("const_loaded"), 64)
            transposes(0, xs)

            def rope_T(u):
                pe.wait_ge(S("rope_done"), u + 1)
                if u >= 2:
                    pe.wait_ge(S("evT"), u - 1)
                for j in range(4):
                    t = nc.tensor.transpose(bank[4 + u % 2][:, j * P:(j + 1) * P],
                                            roped[u % 2][:, j * P:(j + 1) * P], ident)
                t.then_inc(S("tT_done"), 1)

            pe.wait_ge(S("h_lo_done"), KC)
            for u in range(16):
                n, b = divmod(u, TB)
                if b == 0:
                    pe.wait_ge(S("w_lo_done"), n + 1)
                if u >= 4:
                    pe.wait_ge(S("pj_free"), u - 3)
                tok = slice(b * P, (b + 1) * P)
                for k in range(KC):
                    m = mm3(bank[u % 4][:], h_hi[:, k, tok], h_lo[:, k, tok],
                            w_hi[n % 2][:, k], w_lo[n % 2][:, k], k, KC - 1)
                m.then_inc(S("pj_done"), 1)
                if 1 <= u <= 12:
                    rope_T(u - 1)
            pe.wait_ge(S("v_done"), 1)
            pe.wait_ge(S("wg_lo_done"), 1)
            for b in range(TB):
                tok = slice(b * P, (b + 1) * P)
                for k in range(KC):
                    m = mm3(bank[0][:, b * N_GATES:(b + 1) * N_GATES], h_hi[:, k, tok], h_lo[:, k, tok],
                            wg_hi[:, k], wg_lo[:, k], k, KC - 1)
            m.then_inc(S("pj_done"), 1)
            pe.wait_ge(S("v_done"), TB)
            pe.wait_ge(S("evT"), 11)
            for b in range(TB):
                t = nc.tensor.transpose(bank[4][:, b * P:(b + 1) * P], vnat[:, b, P:2 * P], ident)
            t.then_inc(S("tT_done"), 1)

            for kv in range(2):
                pe.wait_ge(S("cx_done"), 8 * (kv + 1))
                pe.wait_ge(S("w1v_loaded" if kv else "w1k_loaded"), 16)
                for hh in range(2):
                    for l in range(LP):
                        m = nc.tensor.matmul(bank[6 + kv][:, hh * 2 * NC:(hh + 1) * 2 * NC],
                                             w1_sb[kv][:, l, hh * P:(hh + 1) * P],
                                             cx[kv][:, l].rearrange("p g c -> p (g c)"),
                                             start=(l == 0), stop=(l == LP - 1))
                m.then_inc(S("hid_done"), 1)
            pe.wait_ge(S("hid_act"), 1)
            pe.wait_ge(S("w2_loaded"), 16)
            pe.wait_ge(S("evT"), 13)
            for g in range(GROUPS):
                for hh in range(2):
                    m = nc.tensor.matmul(bank[4][DH * g:DH * g + DH, 0:NC], w2_sb[:, 0, hh],
                                         hid[0][:, hh * 2 + g, 0:NC], start=(hh == 0), stop=(hh == 1))
            m.then_inc(S("cmp_ps"), 1)
            pe.wait_ge(S("hrep_done"), 1)
            for g in range(GROUPS):
                for hh in range(2):
                    m = nc.tensor.matmul(bank[5][:, g * DH:(g + 1) * DH],
                                         hrep[:, hh * 2 + g].rearrange("p j c -> p (j c)"),
                                         w2_sb[:, 1, hh], start=(hh == 0), stop=(hh == 1))
            m.then_inc(S("cmp_ps"), 1)

            pe.wait_ge(S("kc_done"), 1)
            pe.wait_ge(S("vbd_done"), 8)
            pe.wait_ge(S("gexp_done"), 1)
            for s in range(len(UNITS) + 12):
                qb, in_qb = divmod(s, STEP_QB)
                if s < len(UNITS):
                    _, br, h = UNITS[s]
                    g, j = divmod(h, HPG)
                    rows = slice(DH * g, DH * g + DH)
                    if in_qb == 0:
                        if qb >= 1:
                            pe.wait_ge(S("c_mixed"), qb)
                        for hh in range(HEADS):
                            rr = slice(DH * (hh // HPG), DH * (hh // HPG) + DH)
                            m = nc.tensor.matmul(bank[7][:, hh * CP:hh * CP + NC],
                                                 qT[rr, 1, hh % HPG, qb * P:(qb + 1) * P], kcT[rr, 0:NC],
                                                 start=True, stop=True)
                            if hh == HPG - 1:
                                m.then_inc(S("rows_switch"), 1)
                                pe.wait_ge(S("rows_switch"), qb + 1)
                        m.then_inc(S("c_s"), 1)
                    n = width(qb, br)
                    k0 = (qb + 1) * P - n
                    if s >= 3:
                        pe.wait_ge(S("exp_done"), s - 2)
                    nc.tensor.matmul(bank[s % 3][:, 0:n], qT[rows, 0 if br == SWA else 1, j, qb * P:(qb + 1) * P],
                                     kT[rows, K_OF[br], k0:k0 + n], start=True, stop=False)
                    mw = n if br == SWA else P
                    nc.tensor.matmul(bank[s % 3][:, n - mw:n], ident_b, mask_b[:, 2 * P - mw:2 * P],
                                     start=False, stop=True).then_inc(S("s_done"), 1)
                if 2 <= s < len(UNITS) + 2:
                    u = s - 2
                    n = width(*UNITS[u][:2])
                    pe.wait_ge(S("exp_done"), u + 1)
                    if u >= 2:
                        pe.wait_ge(S(f"pt_done{u % 2}"), u // 2)
                    for kb in range(n // P):
                        t = nc.tensor.transpose(bank[3 + u % 2][:, kb * P:(kb + 1) * P],
                                                pr[u % 3][:, kb * P:(kb + 1) * P], ident)
                    t.then_inc(S("pT_ps"), 1)
                if 3 <= s < len(UNITS) + 3:
                    u = s - 3
                    uq, ub, uh = UNITS[u]
                    n = width(uq, ub)
                    gi = u // HEADS
                    if uh == 0 and gi >= 2:
                        pe.wait_ge(S("o_free"), gi - 1)
                    pe.wait_ge(S(f"pt_done{u % 2}"), u // 2 + 1)
                    v0 = K_OF[ub] * P + (uh // HPG) * DH
                    for kb in range(n // P):
                        tb = uq + 1 - n // P + kb
                        m = nc.tensor.matmul(bank[5 + gi % 2][:, uh * DH:(uh + 1) * DH],
                                             pt[u % 2][:, kb * P:(kb + 1) * P], vnat[:, tb, v0:v0 + DH],
                                             start=(kb == 0), stop=(kb == n // P - 1))
                    m.then_inc(S("pv_done"), 1)
                if s < len(UNITS) and in_qb == 6:
                    pe.wait_ge(S("c_p"), qb + 1)
                    for g in range(GROUPS):
                        t = nc.tensor.transpose(bank[7][:, 256 + g * P:256 + (g + 1) * P],
                                                c_sc[:, g * HPG:(g + 1) * HPG].rearrange("p h c -> p (h c)"), ident)
                    t.then_inc(S("c_T"), 1)
                if s < len(UNITS) and in_qb == 9:
                    pe.wait_ge(S("c_pT_done"), qb + 1)
                    for g in range(GROUPS):
                        m = nc.tensor.matmul(bank[7][:, g * 256:(g + 1) * 256], c_pT[:, g],
                                             vbd[:, g].rearrange("p j d -> p (j d)"), start=True, stop=True)
                    m.then_inc(S("c_o"), 1)

            pe.wait_ge(S("mixed_done"), 1)
            transposes(1, mixed)
            pe.wait_ge(S("h_lo_done"), 2 * KC)
            for n in range(2 * TB):
                half, b = divmod(n, TB)
                i = TILES_IN + half
                if b == 0:
                    pe.wait_ge(S("w_lo_done"), i + 1)
                if n >= 4:
                    pe.wait_ge(S("x1_done"), n - 3)
                tok = slice(b * P, (b + 1) * P)
                for k in range(KC):
                    m = mm3(bank[n % 4][:], h_hi[:, k, tok], h_lo[:, k, tok],
                            w_hi[i % 2][:, k], w_lo[i % 2][:, k], k, KC - 1)
                m.then_inc(S("wo_ps"), 1)
            transposes(2, xs)

            pe.wait_ge(S("h_lo_done"), 3 * KC)
            pe.wait_ge(S("sk_loaded"), 16)

            def early_score(f, r):
                pe.wait_ge(S("f_lo_done"), f + 1)
                if not (isinstance(f, int) and f < 2):
                    pe.wait_ge(S("f_gelu"), f - 1)
                for k in range(KC):
                    m = mm3(bank[6 + r][:], f_hi[r][:, k], f_lo[r][:, k], h_hi[:, k], h_lo[:, k], k, KC - 1)
                m.then_inc(S("f_ps"), 1)

            def key_scores(v):
                if v >= 4:
                    pe.wait_ge(S("s_free"), v - 3)
                pe.wait_ge(S("q_done"), v + 1)
                for b in range(TB):
                    m = nc.tensor.matmul(bank[2 + v % 4][:, b * NK:(b + 1) * NK],
                                         q_sb[v % 2][:, b * P:(b + 1) * P], sk[:, v % 2], start=True, stop=True)
                m.then_inc(S("s_ps"), 1)

            for v in range(2 * PH):
                i = TILES_IN + TILES_OUT + v // 4
                if v % 4 == 0:
                    pe.wait_ge(S("w_lo_done"), i + 1)
                if v >= 2:
                    pe.wait_ge(S("q_done"), v - 1)
                for k in range(KC):
                    c = slice((v % 4) * P, (v % 4 + 1) * P)
                    m = mm3(bank[v % 2][:], w_hi[i % 2][:, k, c], w_lo[i % 2][:, k, c],
                            h_hi[:, k], h_lo[:, k], k, KC - 1)
                m.then_inc(S("q_ps"), 1)
                if v >= 1:
                    key_scores(v - 1)
                early_score(v, v % 2)
            key_scores(2 * PH - 1)
            for f in range(E_REST, E_GATES):
                early_score(f, f % 2)

            pe.wait_ge(S("gate_done"), 1)
            pe.wait_ge(S("key_done"), 2 * PH)
            for n, src in enumerate((score, key[0], key[1])):
                for b in range(TB):
                    t = nc.tensor.transpose(bank[n][:, b * P:(b + 1) * P],
                                            src[:, b].rearrange("p h k -> p (h k)"), ident)
                t.then_inc(S("slot_ps"), 1)

            def gate_rows(i, r):
                pe.wait_ge(S("oh_done"), i + 1)
                for q in range(TG // PSTEP):
                    n = i * (TG // PSTEP) + q
                    if not (isinstance(n, int) and n < 4):
                        pe.wait_ge(S("ev_full"), n - 3)
                    for tt in range(PSTEP):
                        t = q * PSTEP + tt
                        for j in range(3):
                            m = nc.tensor.matmul(bank[2 + q % 4][:, tt * NK:(tt + 1) * NK], oh[r][1][:, :, t],
                                                 gp[r][j][:, :, t], start=(j == 0), stop=(j == 2))
                    m.then_inc(S("gate_mm"), 1)

            for i in range(2):
                gate_rows(i, i)
                early_score(i + E_GATES, i)
            with pe.Fori(1, NTG // 2) as o:
                for r in range(2):
                    gate_rows(o * 2 + r, r)
                    early_score(o * 2 + r + E_GATES, r)
            for f in range(E_LAST, NE):
                early_score(f, f % 2)

            pe.wait_ge(S("ev_full"), NTG * (TG // PSTEP))

            def early_group(n, half):
                for j in range(8):
                    b, side = divmod(j, 2)
                    if not (isinstance(n, int) and n == 0 and j < 4):
                        pe.wait_ge(S("acc_done"), n * 8 + j - 3)
                    elif j == 2:
                        pe.wait_ge(S("f_gelu"), NE)
                    tok, cols = slice(b * P, (b + 1) * P), slice(side * COLS, (side + 1) * COLS)
                    for c in range(GB):
                        if j == 0:
                            pe.wait_ge(S("w_done"), n * GB + c + 1)
                        e = half * GB + c
                        m = mm3(bank[4 + j % 4][:], w_e_hi[:, e, tok], w_e_lo[:, e, tok],
                                u_hi[:, e, cols], u_lo[:, e, cols], c, GB - 1)
                    m.then_inc(S("pu_done"), 1)

            for n in range(2):
                early_group(n, n)
            with pe.Fori(1, NSUB // 2) as o:
                for r in range(2):
                    early_group(o * 2 + r, r)

            def group(g):
                first = isinstance(g, int) and g == G0
                for c in range(GC):
                    e = (g - G0) * GC + c
                    pe.wait_ge(S("d_lo_done"), e + 1)
                    if not (first and c < 2):
                        pe.wait_ge(S("gelu_done"), e - 1)
                    for k in range(KC):
                        m = mm3(bank[c % 2][:], d_hi[:, c % 2, k], d_lo[:, c % DR, k],
                                h_hi[:, k], h_lo[:, k], k, KC - 1)
                    m.then_inc(S("pd_done"), 1)
                for n in range(8):
                    b, half = divmod(n, 2)
                    pe.wait_ge(S("acc_done"), banks_before(g) + n - 3)
                    tok, cols = slice(b * P, (b + 1) * P), slice(half * COLS, (half + 1) * COLS)
                    for c in range(GC):
                        if n == 0:
                            pe.wait_ge(S("u_lo_done"), g * GC + c + 1)
                            pe.wait_ge(S("w_done"), g * GC + c + 1)
                        m = mm3(bank[4 + n % 4][:], w_e_hi[:, c, tok], w_e_lo[:, c, tok],
                                u_hi[:, c, cols], u_lo[:, c, cols], c, GC - 1)
                    m.then_inc(S("pu_done"), 1)

            group(G0)
            with pe.Fori(G0 + 1, NG) as g:
                group(g)


def constants():
    c = np.zeros((P, 432), np.float32)
    c[:, 0:P] = np.eye(P)
    t = np.arange(T).reshape(TB, P).T
    vis = np.zeros((P, TB, CP), np.float32)
    vis[:, :, :NC] = (np.arange(NC) * CMP_STRIDE + CMP_LEN - 1)[None, None] <= t[:, :, None]
    c[:, 128:256] = np.where(vis > 0, 0.0, NEG).reshape(P, -1)
    c[:, 256:384] = vis.reshape(P, -1)
    c[:, 384:416] = np.float32(10000.0) ** (-np.arange(HALF, dtype=np.float32) / np.float32(HALF))
    c[:, 416:432] = np.arange(TOPK)
    b = np.zeros((P, 384 + NK * TG), np.dtype("bfloat16"))
    b[:, 0:P] = np.eye(P)
    q, k = np.arange(P)[:, None], np.arange(P)[None]
    b[:, P:2 * P] = np.where(k > q, 0.0, NEG)
    b[:, 2 * P:3 * P] = np.where(k <= q, 0.0, NEG)
    b[:, 384:] = np.repeat(np.arange(NK), TG)[None]
    return c, b


def kernel(x, positions, norm_attn, w_in, attn_sinks, cmp_k_pos, cmp_k_w1, cmp_k_w2, cmp_v_pos, cmp_v_w1,
           cmp_v_w2, w_out, norm_ffn, peer_w_query, peer_sub_keys_1, peer_sub_keys_2, peer_expert_down,
           peer_expert_up, norm_f):
    import concourse.bacc as bacc
    from concourse.bass_utils import run_bass_kernel_spmd

    a = lambda v: np.asarray(v)[0]
    kw = HEADS // HPG * DH
    w = a(w_in)
    sizes = [HEADS * DH, kw, kw, HEADS * DH] + [kw] * 6 + [N_GATES]
    qa, ka, va, qb, kc, vc, ks, vs, kw_, vw, gl = np.split(w, np.cumsum(sizes)[:-1], axis=1)
    pairs = lambda q: q.reshape(D, GROUPS, HPG, DH).transpose(0, 2, 1, 3).reshape(D, HEADS * DH)
    tiles = [pairs(qa), pairs(qb), np.concatenate([ka, kc, ks, kw_], 1), np.concatenate([va, vc, vs, vw], 1)]
    for m in (a(w_out), a(peer_w_query)):
        tiles += [m[:, c:c + COLS] for c in range(0, m.shape[1], COLS)]
    chunked = lambda m: m.reshape(KC, P, -1).transpose(1, 0, 2).reshape(P, -1)
    params = np.zeros((P, 96), np.float32)
    params[:, 0:8] = a(norm_attn).reshape(KC, P).T
    params[:, 8:16] = a(norm_ffn).reshape(KC, P).T
    params[:, 16:24] = a(attn_sinks)[None]
    for n, e in enumerate((a(cmp_k_pos), a(cmp_v_pos))):
        params[:, 32 + 32 * n:64 + 32 * n] = np.concatenate([e.T, e.T], 0)
    w1 = lambda m: a(m).reshape(LP, P, CMP_HIDDEN).transpose(1, 0, 2).reshape(P, -1)
    w2 = lambda m: a(m).reshape(2, P, DH).transpose(1, 0, 2).reshape(P, -1)
    c, b = constants()
    arrays = {
        "x_in": a(x), "pos": np.asarray(positions)[0].reshape(TB, P).T, "params": params, "consts": c, "consts_b": b,
        "wts": np.stack([chunked(t) for t in tiles]), "wgate": chunked(gl),
        "w1": np.stack([w1(cmp_k_w1), w1(cmp_v_w1)]), "w2": np.concatenate([w2(cmp_k_w2), w2(cmp_v_w2)], 1),
        "subkeys": np.concatenate([a(peer_sub_keys_1).T, a(peer_sub_keys_2).T], 1),
        "normf": np.asarray(norm_f).reshape(1, D),
        "down": a(peer_expert_down).reshape(NK, P, KC, P).transpose(0, 3, 2, 1).reshape(NK, P, KC * P),
        "up": a(peer_expert_up).reshape(NK, P, D),
    }
    arrays = {k: np.ascontiguousarray(v) for k, v in arrays.items()}
    nc = bacc.Bacc("TRN2", target_bir_lowering=False, num_devices=1)
    ins = [nc.dram_tensor(k, v.shape, mybir.dt.from_np(v.dtype), kind="ExternalInput").ap() for k, v in arrays.items()]
    y = nc.dram_tensor("y", (T, D), F32, kind="ExternalOutput").ap()
    build(nc, *ins, y)
    r = run_bass_kernel_spmd(nc, [arrays], core_ids=[0])
    return r.results[0]["y"].reshape(1, T, D)
```

```python
import concourse.bass as bass
from concourse import mybir
from concourse.alu_op_type import AluOpType as ALU
import numpy as np

F32, F32R, BF16 = mybir.dt.float32, mybir.dt.float32r, mybir.dt.bfloat16
U32, I32 = mybir.dt.uint32, mybir.dt.int32
ACT = mybir.ActivationFunctionType
X_AXIS = mybir.AxisListType.X

P = 128
T, D = 512, 1024
KC, TB = D // P, T // P
DH, HALF = 64, 32
HEADS, GROUPS = 8, 2
HPG = HEADS // GROUPS
COLS = 512
N_GATES = 3 * HEADS
CMP_LEN, CMP_STRIDE, CMP_HIDDEN = 32, 16, 256
NC = (T - CMP_LEN) // CMP_STRIDE + 1
LP = CMP_LEN // 2
CP = NC + 1
PH, NK, TOPK = 8, 128, 16
NEG = -1e30
EPS = 1e-6
TILES_IN, TILES_OUT, TILES_Q = 4, 2, 4
TILES = TILES_IN + TILES_OUT + TILES_Q
GC = 8
NG = NK // GC
GB = 4
NGB = NK // GB
TG = 32
NTG = T // TG
PSTEP = 4
DR = 4
E_REST = 2 * PH
E_SLOTS = E_REST + 6
E_GATES = E_REST + 10
E_LAST = E_GATES + NTG
NE = E_LAST + 6
POOL_KEYS = {4: 0, 6: 1, 9: 2, 11: 3, 13: 4, 15: 5, 18: 6, 20: 7}
NSUB = NE // GB
G0 = NE // GC

TWO_PI = 2.0 * np.pi
PI_A = 6.28125
PI_B = float(np.float32(np.round((TWO_PI - PI_A) * 2.0 ** 19) / 2.0 ** 19))
PI_C = float(np.float32(TWO_PI - PI_A - PI_B))
ROUND = 1.5 * 2.0 ** 23
PI_CLAMP = float(np.nextafter(np.float32(np.pi), np.float32(0)))

SWA, SEL, WIN = range(3)
UNITS = [(qb, br, h) for qb in range(TB) for br in (SWA, SEL, WIN) for h in range(HEADS)]
K_OF = {SWA: 0, SEL: 2, WIN: 3}
STEP_QB = 3 * HEADS


def width(qb, br):
    return min(qb + 1, 2) * P if br == SWA else (qb + 1) * P


def tile_used(i):
    if i < TILES_IN:
        return "pj_done", TB * (i + 1)
    if i < TILES_IN + TILES_OUT:
        return "wo_ps", TB * (i - TILES_IN + 1)
    return "q_ps", 4 * (i - TILES_IN - TILES_OUT + 1)


def banks_before(g):
    return (g - G0) * 8 + NSUB * 8


def f32(ap):
    return ap.bitcast(F32)


def build(nc, x, pos, params, consts, consts_b, wts, wgate, w1, w2, subkeys, normf, down, up, y):
    at = [16512]

    def size(shape, dt):
        return int(np.prod(shape[1:])) * (2 if dt == BF16 else 4)

    def place(name, shape, dt, offset):
        return nc.alloc_sbuf_tensor_at(name, shape, dt, offset=offset)

    def sb(name, shape, dt=F32):
        t = place(name, shape, dt, at[0])
        at[0] += (size(shape, dt) + 31) // 32 * 32
        return t

    xt = sb("xt", [P, TB, D])
    h_hi = sb("h_hi", [P, KC, T], F32R)
    h_lo = sb("h_lo", [P, KC, T], F32R)
    cst = sb("cst", [P, 432])
    ident = cst[:, 0:P]
    cmp_neg = cst[:, 128:256].rearrange("p (q c) -> p q c", q=TB)
    cmp_vis = cst[:, 256:384].rearrange("p (q c) -> p q c", q=TB)
    inv_freq = cst[:, 384:416]
    iota16 = cst[:, 416:432]
    cstb = sb("cstb", [P, 384], BF16)
    ident_b, mask_b = cstb[:, 0:P], cstb[:, P:384]
    prm = sb("prm", [P, 96])
    g_attn, g_ffn, sinks = prm[:, 0:8], prm[:, 8:16], prm[:, 16:24]
    cmp_pos = prm[:, 32:96].rearrange("p (k l) -> p k l", k=2)
    posi = sb("posi", [P, TB], I32)
    posf = sb("posf", [P, TB])
    ssq = sb("ssq", [P, TB])
    ms = sb("ms", [P, TB])
    rt = sb("rt", [P, TB])
    rstd = sb("rstd", [P, TB])
    nt = sb("nt", [P, TB])
    base = at[0]

    w_raw = [sb(f"w_raw{i}", [P, KC, COLS]) for i in range(2)]
    w_lo = [place(f"w_lo{i}", [P, KC, COLS], F32R, base + i * 16384) for i in range(2)]
    w_hi = [sb(f"w_hi{i}", [P, KC, COLS], F32R) for i in range(2)]
    q_g1 = place("q_g1", [P, 2, HPG, T], F32, base + 16384)
    after_w = at[0]
    xs = sb("xs", [P, TB, D])
    mixed = xs
    qT = sb("qT", [P, 2, HPG, T])
    kT = sb("kT", [P, 4, T])
    vcT = sb("vcT", [P, T])
    vnat = sb("vnat", [P, TB, COLS])
    gates = sb("gates", [P, TB, HEADS, 3])
    gexp = sb("gexp", [P, TB, N_GATES])
    stage = at[0]
    cos2 = sb("cos2", [P, TB, 2, HALF])
    sin2 = sb("sin2", [P, TB, 2, HALF])
    ang = sb("ang", [P, TB, HALF])
    trn = sb("trn", [P, TB, HALF])
    red = sb("red", [P, TB, HALF])
    red2 = sb("red2", [P, TB, HALF])
    scratch = at[0]
    rp_c = [sb(f"rp_c{i}", [P, COLS]) for i in range(2)]
    rp_s = [sb(f"rp_s{i}", [P, COLS]) for i in range(2)]
    roped = [sb(f"roped{i}", [P, COLS]) for i in range(2)]
    wg_at = at[0]
    wg_raw = sb("wg_raw", [P, KC, N_GATES])
    wg_lo = place("wg_lo", [P, KC, N_GATES], F32R, wg_at)
    wg_hi = sb("wg_hi", [P, KC, N_GATES], F32R)
    w1_sb = [place("w1_k", [P, LP, CMP_HIDDEN], F32, after_w), sb("w1_v", [P, LP, CMP_HIDDEN])]
    cx = [place(f"cx{i}", [P, LP, GROUPS, NC], F32, scratch + i * 4096) for i in range(2)]
    hrep = place("hrep", [P, GROUPS * 2, 4, CP], F32, scratch + 2 * 4096)
    gexp_T = place("gexp_T", [N_GATES, T], F32, scratch + 10 * 1024)
    end_proj = at[0]
    at[0] = stage
    pr = [sb(f"pr{i}", [P, COLS]) for i in range(3)]
    pt = [sb(f"pt{i}", [P, COLS]) for i in range(3)]
    o_tmp = sb("o_tmp", [P, COLS])
    c_sc = sb("c_sc", [P, TB, HEADS, CP])
    c_pT = sb("c_pT", [P, GROUPS, P])
    assert at[0] <= end_proj
    at[0] = end_proj
    hid_T = [sb(f"hid_T{i}", [GROUPS * NC, CMP_HIDDEN]) for i in range(2)]
    hid = sb("hid", [P, GROUPS * 2, CP])
    w2_sb = sb("w2_sb", [P, 2, 2, DH])
    kcT = sb("kcT", [P, GROUPS, CP])
    vbd = sb("vbd", [P, GROUPS, 4, DH])
    nmax = sb("nmax", [P, len(UNITS)])
    rsum = sb("rsum", [P, len(UNITS)])
    nsink = sb("nsink", [P, HEADS])
    es_in = sb("es_in", [P, TB, HEADS])
    es = sb("es", [P, TB, HEADS])
    coef = sb("coef", [P, HEADS])
    c_max = sb("c_max", [P, TB, HEADS])
    c_sum = sb("c_sum", [P, TB, HEADS])
    c_coef = sb("c_coef", [P, TB, HEADS])
    assert at[0] <= 229368, at[0]

    at[0] = after_w
    cand = sb("cand", [P, TB, TOPK, TOPK])
    candw = sb("candw", [P, TB, TOPK * TOPK])
    hit_0 = [sb(f"hit0{s}", [P, TB, TOPK, TOPK]) for s in range(2)]
    assert at[0] == after_w + 16384
    q_sb = [sb(f"q_sb{i}", [P, T]) for i in range(2)]
    sk = sb("sk", [P, 2, NK])
    work = [sb(f"work{i}", [P, TB, NK]) for i in range(2)]
    tv = [[sb(f"tv{r}{s}", [P, TB, TOPK]) for s in range(2)] for r in range(2)]
    ti = [[sb(f"ti{r}{s}", [P, TB, TOPK], U32) for s in range(2)] for r in range(2)]
    tif = [[sb(f"tif{r}{s}", [P, TB, TOPK]) for s in range(2)] for r in range(2)]
    posn = sb("posn", [P, TB, TOPK], U32)
    pab = [[sb(f"pab{r}{s}", [P, TB, TOPK], U32) for s in range(2)] for r in range(2)]
    hit = [hit_0, [sb(f"hit1{s}", [P, TB, TOPK, TOPK]) for s in range(2)]]
    sl_r = [sb(f"sl_r{i}", [P, T]) for i in range(2)]
    score = sb("score", [P, TB, PH, TOPK])
    key = [sb(f"key{s}", [P, TB, PH, TOPK]) for s in range(2)]
    g_sum = sb("g_sum", [P, TB, PH])
    at[0] = slots = max(at[0], base + 11 * NK * TG * 2 + 2 * NGB * TG * GB * 4)
    sl_key = [sb(f"sl_key{s}", [P, T], BF16) for s in range(2)]
    sl_g = [sb(f"sl_g{i}", [P, T], BF16) for i in range(3)]
    assert at[0] <= 229368, at[0]

    tail = (229368 - 7 * 4096) // 32 * 32
    assert at[0] <= tail, (at[0], tail)
    at[0] = tail
    f_raw = [sb(f"f_raw{i}", [P, KC, P]) for i in range(2)]
    f_lo = [sb(f"f_lo{i}", [P, KC, P], F32R) for i in range(2)]
    f_hi = [sb(f"f_hi{i}", [P, KC, P], F32R) for i in range(2)]
    f_act = [sb(f"f_act{i}", [P, T]) for i in range(2)]

    at[0] = base
    iota_k = sb("iota_k", [P, NK, TG], BF16)
    oh = [[sb(f"oh{r}{i}", [P, NK, TG], BF16) for i in range(2)] for r in range(2)]
    gp = [[sb(f"gp{r}{i}", [P, NK, TG], BF16) for i in range(3)] for r in range(2)]
    ev = [sb(f"ev{i}", [P, NGB, TG, GB]) for i in range(2)]
    assert at[0] <= slots, (at[0], slots)

    at[0] = base
    d_raw = sb("d_raw", [P, DR, KC, P])
    d_lo = place("d_lo", [P, DR, KC, P], F32R, base)
    d_hi = sb("d_hi", [P, 2, KC, P], F32R)
    u_raw = sb("u_raw", [P, DR, D])
    u_hi = sb("u_hi", [P, GC, D], F32R)
    u_lo = sb("u_lo", [P, GC, D], F32R)
    w_e_hi = sb("w_e_hi", [P, GC, T], F32R)
    w_e_lo = sb("w_e_lo", [P, GC, T], F32R)
    a_early = place("a_early", [P, GC, T], F32, base)
    g_early = place("g_early", [P, T, GB], F32, base + DR * D * 4)
    g_sb = sb("g_sb", [P, 2, T, GB])
    a_sb = sb("a_sb", [P, 2, T])
    assert at[0] <= 229368, at[0]
    nf = place("nf", [P, D], F32, base)
    junk = place("junk", [P, D], F32, after_w + 16384)

    gates_dram = nc.dram_tensor("gates_dram", (P, NTG, NGB, TG * GB), F32, kind="Internal").ap()

    act_dram = nc.dram_tensor("act_dram", (NE, P, T), F32, kind="Internal").ap()

    bank = [nc.alloc_psum_tensor(f"bank{i}", [P, 512], F32) for i in range(8)]
    sems = {}

    def S(name):
        if name not in sems:
            sems[name] = nc.alloc_semaphore(name)
        return sems[name]

    x_v = x.rearrange("(b p) d -> b p d", p=P)
    y_v = y.rearrange("(b p) d -> b p d", p=P)

    with nc.Block() as block:

        @block.sync
        def _(sp):
            for b in range(TB):
                sp.dma_start(xt[:, b], x_v[b]).then_inc(S(f"x_loaded{b}"), 16)
                if b == 0:
                    sp.dma_start(cst[:], consts).then_inc(S("cst_loaded"), 16)
            sp.dma_start(prm[:], params).then_inc(S("const_loaded"), 16)
            sp.dma_start(posi[:], pos).then_inc(S("const_loaded"), 16)
            sp.dma_start(cstb[:], consts_b[:, 0:384]).then_inc(S("const_loaded"), 16)
            sp.dma_start(wg_raw[:], wgate.rearrange("p (k c) -> p k c", k=KC)).then_inc(S("wg_loaded"), 16)
            def early_down(f, r):
                if not (isinstance(f, int) and f < 2):
                    sp.wait_ge(S("f_lo_done"), f - 1)
                sp.dma_start(f_raw[r][:], down[bass.ts(f, 1)].rearrange("o p (k e) -> p (o k) e", k=KC))\
                    .then_inc(S(f"f_loaded{r}"), 16)

            for i in range(TILES_IN + TILES_OUT + 2):
                if i >= 2:
                    used, count = tile_used(i - 2)
                    sp.wait_ge(S(used), count)
                if i == TILES_IN + 1:
                    sp.wait_ge(S("s_done"), len(UNITS))
                w_i = wts[i].rearrange("p (k c) -> p k c", k=KC)
                if i == 0:
                    sp.dma_start(w_raw[0][:, 0:KC // 2], w_i[:, 0:KC // 2]).then_inc(S("w0_loaded"), 16)
                    sp.dma_start(w_raw[0][:, KC // 2:], w_i[:, KC // 2:]).then_inc(S("w_loaded0"), 16)
                else:
                    sp.dma_start(w_raw[i % 2][:], w_i).then_inc(S(f"w_loaded{i % 2}"), 16)
                if i == TILES_IN + TILES_OUT:
                    sp.wait_ge(S("mixed_done"), 1)
                    sp.dma_start(sk[:], subkeys.rearrange("p (s k) -> p s k", s=2)).then_inc(S("sk_loaded"), 16)
            for f in range(E_GATES + 1):
                if f == 0:
                    sp.wait_ge(S("mixed_done"), 1)
                early_down(f, f % 2)
                if f in (4, 8):
                    i = TILES - 2 + (f == 8)
                    used, count = tile_used(i - 2)
                    sp.wait_ge(S(used), count)
                    sp.dma_start(w_raw[i % 2][:], wts[i].rearrange("p (k c) -> p k c", k=KC))\
                      .then_inc(S(f"w_loaded{i % 2}"), 16)
                if f == E_REST + 1:
                    sp.wait_ge(S("q_ps"), 2 * PH)
                    sp.dma_start(iota_k[:], consts_b[:, 384:384 + NK * TG].rearrange("p (k t) -> p k t", t=TG))\
                      .then_inc(S("iota_loaded"), 16)
            with sp.Fori(0, NTG // 2) as o:
                for r in range(2):
                    i = o * 2 + r
                    early_down(i + E_GATES + 1, 1 - r)

            def early_up(n, c):
                if n >= 1:
                    sp.wait_ge(S("u_lo_done"), (n - 1) * GB + c + 1)
                sp.dma_start(u_raw[:, c], up[n * GB + c]).then_inc(S(f"us_loaded{c}"), 16)

            def early_acts(n):
                h = slice(n % 2 * GB, n % 2 * GB + GB)
                if n >= 2:
                    sp.wait_ge(S("w_done"), (n - 1) * GB)
                sp.dma_start(a_early[:, h], act_dram[n * GB:(n + 1) * GB].rearrange("e p t -> p e t"))\
                  .then_inc(S(f"as_loaded{n % 2}"), 16)
                if n == 0:
                    for r in range(2):
                        sp.wait_ge(S(f"ev_stored{r}"), 16 * (NTG // 2))
                else:
                    sp.wait_ge(S("w_done"), n * GB)
                sp.dma_start(g_early[:].rearrange("p (i t) k -> p i (t k)", i=NTG), gates_dram[:, :, n])\
                  .then_inc(S("gs_loaded"), 16)

            sp.wait_ge(S("gate_mm"), NTG * (TG // PSTEP))
            for n in range(2):
                for c in range(GB):
                    f = E_LAST + n * GB + c
                    if f + 1 < NE:
                        early_down(f + 1, (f + 1) % 2)
                    early_up(n, c)
                    if c == GB - 1:
                        if n == 0:
                            for r in range(2):
                                sp.wait_ge(S(f"f_stored{r}"), 16 * (E_GATES // 2))
                        early_acts(n)
            for r in range(2):
                sp.wait_ge(S(f"f_stored{r}"), 16 * (NE // 2))
            for n in range(2, NSUB):
                for c in range(GB):
                    early_up(n, c)
                early_acts(n)
            sp.wait_ge(S("w_done"), NE)

            def loads(g, c):
                e = g * GC + c
                if not (isinstance(g, int) and e < NE + DR):
                    sp.wait_ge(S("pd_done"), e - NE - DR + 1)
                sp.dma_start(d_raw[:, c % DR], down[bass.ts(e, 1)].rearrange("o p (k e) -> p (o k) e", k=KC))\
                  .then_inc(S(f"d_loaded{c % DR}"), 16)
                sp.wait_ge(S("u_lo_done"), e - DR + 1)
                sp.dma_start(u_raw[:, c % DR], up[bass.ts(e, 1)].rearrange("o p d -> p (o d)"))\
                  .then_inc(S(f"u_loaded{c % DR}"), 16)
                if c % GB == 0:
                    b = c // GB
                    sp.wait_ge(S("w_done"), e - GB)
                    sp.dma_start(g_sb[:, b].rearrange("p (i t) k -> p i (t k)", i=NTG),
                                 gates_dram[:, :, bass.ts(g * 2 + b, 1)].rearrange("p i o x -> p i (o x)"))\
                      .then_inc(S(f"g_loaded{b}"), 16)

            for c in range(GC):
                loads(G0, c)
            with sp.Fori(G0 + 1, NG) as g:
                for c in range(GC):
                    loads(g, c)
            sp.wait_ge(S("pd_done"), NK - NE)
            sp.dma_start(nf[:], normf.partition_broadcast(P).rearrange("p o d -> p (o d)")).then_inc(S("nf_loaded"), 16)
            for b in range(TB):
                sp.wait_ge(S("y_done"), b + 1)
                sp.dma_start(y_v[b], xt[:, b]).then_inc(S("y_stored"), 16)
            sp.wait_ge(S("y_stored"), 16 * TB)

        @block.gpsimd
        def _(pool):
            pool.dma_start(w2_sb[:], w2.rearrange("p (k h d) -> p k h d", k=2, h=2)).then_inc(S("w2_loaded"), 16)
            pool.wait_ge(S("w_hi_done"), 1)
            pool.dma_start(w1_sb[1][:], w1[1].rearrange("p (l h) -> p l h", l=LP)).then_inc(S("w1v_loaded"), 16)
            pool.wait_ge(S("hT_ps"), KC)
            pool.dma_start(w1_sb[0][:], w1[0].rearrange("p (l h) -> p l h", l=LP)).then_inc(S("w1k_loaded"), 16)
            pool.wait_ge(S("pj_done"), 4 * TB)
            nc.gpsimd.memset(q_g1[0:DH], 0.0).then_inc(S("q_zeroed"), 1)
            pool.wait_ge(S("q_moved"), 1)
            nc.gpsimd.memset(qT[DH:P, 0], 0.0).then_inc(S("q_zeroed"), 1)
            pool.wait_ge(S("c_s"), 1)
            nc.gpsimd.memset(qT[DH:P, 1], 0.0).then_inc(S("q_zeroed"), 1)

            def early_low(f, r):
                pool.wait_ge(S("f_hi_done"), f + 1)
                nc.gpsimd.tensor_tensor(f_lo[r][:], f_raw[r][:], f32(f_hi[r][:]), ALU.subtract)\
                    .then_inc(S("f_lo_done"), 1)

            def chosen_keys(hd):
                r = hd % 2
                for s in range(2):
                    pool.wait_ge(S("hit_eq"), 2 * hd + s + 1)
                    nc.gpsimd.tensor_tensor(
                        hit[r][s][:], hit[r][s][:],
                        tif[r][s][:].unsqueeze(2).broadcast_to([P, TB, TOPK, TOPK]), ALU.mult)\
                        .then_inc(S("hit_done"), 1)

            def w_low(i, part):
                k = slice(part * 3, min(part * 3 + 3, KC))
                if i < 8:
                    pool.wait_ge(S("w_hi_done"), i + 1)
                else:
                    pool.wait_ge(S("w_part_hi"), (i - 8) * 3 + part + 1)
                ins = nc.gpsimd.tensor_tensor(w_lo[i % 2][:, k], w_raw[i % 2][:, k], f32(w_hi[i % 2][:, k]),
                                              ALU.subtract)
                ins.then_inc(S("w_part_lo"), 1)

            for part in range(3):
                w_low(6, part)
            for f in range(E_GATES):
                early_low(f, f % 2)
                if f // 4 < 3 and f % 4 > 0:
                    w_low(7 + f // 4, f % 4 - 1)
                if f in POOL_KEYS:
                    chosen_keys(POOL_KEYS[f])
            with pool.Fori(0, NTG // 2) as o:
                for r in range(2):
                    early_low(o * 2 + r + E_GATES, r)
            for f in range(E_LAST, NE):
                early_low(f, f % 2)

        @block.scalar
        def _(act):
            def split_w(i):
                act.wait_ge(S(f"w_loaded{i % 2}"), 16 * (i // 2 + 1))
                if i >= 2:
                    used, count = tile_used(i - 2)
                    act.wait_ge(S(used), count)
                nc.scalar.activation(w_hi[i % 2][:], w_raw[i % 2][:], ACT.Copy).then_inc(S("w_hi_done"), 1)

            def split_w_part(i, part):
                k = slice(part * 3, min(part * 3 + 3, KC))
                if part == 0:
                    act.wait_ge(S(f"w_loaded{i % 2}"), 16 * (i // 2 + 1))
                    used, count = tile_used(i - 2)
                    act.wait_ge(S(used), count)
                nc.scalar.activation(w_hi[i % 2][:, k], w_raw[i % 2][:, k], ACT.Copy).then_inc(S("w_part_hi"), 1)

            def rms(n):
                for b in range(TB):
                    i = n * TB + b
                    if n == 0:
                        act.wait_ge(S(f"x_loaded{b}"), 16)
                    else:
                        act.wait_ge(S("x1_done") if n == 1 else S("acc_done"),
                                    TB + b + 1 if n == 1 else banks_before(NG - 1) + 2 * b + 2)
                    if i:
                        act.wait_ge(S("ssq_done"), i)
                    squares = junk[:] if n < 2 else a_sb[:].rearrange("p a t -> p (a t)")
                    nc.scalar.activation(squares, xt[:, b], ACT.Square, accum_out=ssq[:, b:b + 1])\
                      .then_inc(S("ssq_done"), 1)
                    act.wait_ge(S("ms_done"), i + 1)
                    nc.scalar.activation(rt[:, b:b + 1], ms[:, b:b + 1], ACT.Sqrt).then_inc(S("root_done"), 1)
                    if n == 1 and b == 1:
                        split_w(6)

            def evac_hi(rep, gain):
                for k in range(KC):
                    if rep == 0 and k == KC // 2:
                        act.wait_ge(S("w_loaded0"), 16)
                        nc.scalar.activation(w_hi[0][:, k:], w_raw[0][:, k:], ACT.Copy).then_inc(S("w_hi_done"), 1)
                    act.wait_ge(S("hT_ps"), rep * KC + k + 1)
                    nc.scalar.activation(h_hi[:, k], bank[k][:], ACT.Copy,
                                         **({} if gain is None else {"scale": gain[:, k:k + 1]}))\
                      .then_inc(S("h_hi_done"), 1)

            rms(0)
            act.wait_ge(S("wg_loaded"), 16)
            nc.scalar.activation(wg_hi[:], wg_raw[:], ACT.Copy).then_inc(S("wg_hi_done"), 1)
            act.wait_ge(S("w0_loaded"), 16)
            nc.scalar.activation(w_hi[0][:, 0:KC // 2], w_raw[0][:, 0:KC // 2], ACT.Copy).then_inc(S("w0_hi_done"), 1)
            act.wait_ge(S("const_loaded"), 48)
            evac_hi(0, g_attn)
            split_w(1)
            act.wait_ge(S("angles"), 2)
            for i, (dst, src) in enumerate(((sin2, red), (cos2, red2))):
                for half in range(2):
                    nc.scalar.activation(dst[:, :, half], src[:], ACT.Sin,
                                         scale=-1.0 if i == 0 and half == 0 else 1.0).then_inc(S("tables"), 1)

            def evac_T(u):
                n, b = divmod(u, TB)
                act.wait_ge(S("tT_done"), u + 1)
                src = bank[4 + u % 2][:].rearrange("p (j t) -> p j t", j=4)
                if n < 2:
                    nc.scalar.activation(qT[:, n, :, b * P:(b + 1) * P], src, ACT.Copy, scale=DH ** -0.5)\
                      .then_inc(S("evT"), 1)
                else:
                    nc.scalar.activation(kT[:, :, b * P:(b + 1) * P], src, ACT.Copy).then_inc(S("evT"), 1)

            for u in range(16):
                if u >= 1 and u <= 12:
                    evac_T(u - 1)
                if u >= 12:
                    act.wait_ge(S("pj_done"), u + 1)
                    nc.scalar.activation(vnat[:, u - 12], bank[u % 4][:], ACT.Copy).then_inc(S("v_done"), 1)
                if u == 5:
                    split_w(2)
                if u == 9:
                    split_w(3)
            act.wait_ge(S("tT_done"), 13)
            nc.scalar.activation(vcT[:], bank[4][:], ACT.Copy).then_inc(S("evT"), 1)
            act.wait_ge(S("pj_done"), 17)
            nc.scalar.activation(gexp_T[:], bank[0][0:N_GATES], ACT.Exp, scale=-1.0).then_inc(S("gexp_done"), 1)
            act.wait_ge(S("evT"), 12)
            nc.scalar.activation(q_g1[DH:P], qT[DH:P], ACT.Copy).then_inc(S("q_moved"), 1)
            split_w(4)
            for kv in range(2):
                act.wait_ge(S("hid_done"), kv + 1)
                nc.scalar.activation(hid_T[kv][:], bank[6 + kv][0:GROUPS * NC, 0:CMP_HIDDEN], ACT.Gelu)\
                  .then_inc(S("hid_act"), 1)
            act.wait_ge(S("cmp_ps"), 1)
            for g in range(GROUPS):
                rows = slice(DH * g, DH * g + DH)
                nc.scalar.activation(kcT[rows, g, 0:NC], bank[4][rows, 0:NC], ACT.Copy).then_inc(S("kc_done"), 1)

            for s in range(len(UNITS) + 12):
                qb, in_qb = divmod(s, STEP_QB)
                if s < len(UNITS):
                    n = width(*UNITS[s][:2])
                    act.wait_ge(S("max_done"), s + 1)
                    if s >= 3:
                        act.wait_ge(S("pT_ps"), s - 2)
                    nc.scalar.activation(pr[s % 3][:, 0:n], bank[s % 3][:, 0:n], ACT.Exp,
                                         bias=nmax[:, s:s + 1], accum_out=rsum[:, s:s + 1])\
                      .then_inc(S("exp_done"), 1)
                    if s == 5:
                        act.wait_ge(S("c_shift"), 1)
                        cs = c_sc[:].rearrange("p q h c -> p (q h) c")[:, :, 0:NC]
                        nc.scalar.activation(cs, cs, ACT.Exp).then_inc(S("c_exp"), 1)
                    if in_qb == 11:
                        act.wait_ge(S("c_T"), qb + 1)
                        nc.scalar.activation(c_pT[:], bank[7][:, 256:512].rearrange("p (g t) -> p g t", g=2),
                                             ACT.Copy).then_inc(S("c_pT_done"), 1)
                if 2 <= s < len(UNITS) + 2 and s % 2 == 0:
                    u = s - 2
                    n = width(*UNITS[u][:2])
                    act.wait_ge(S("pT_ps"), u + 1)
                    if u >= 3:
                        act.wait_ge(S("pv_done"), u - 2)
                        act.wait_ge(S("pt_done1"), (u - 3) // 2 + 1)
                    nc.scalar.activation(pt[u % 3][:, 0:n], bank[3][:, 0:n], ACT.Copy).then_inc(S("pt_done0"), 1)
                if in_qb == HEADS + 1 and qb < TB:
                    act.wait_ge(S("es_in_done"), qb + 1)
                    nc.scalar.activation(es[:, qb], es_in[:, qb], ACT.Exp).then_inc(S("es_done"), 1)

            evac_hi(1, None)
            split_w(5)
            rms(1)
            evac_hi(2, g_ffn)
            def early_high(f, r):
                act.wait_ge(S(f"f_loaded{r}"), (f - r) * 8 + 16)
                if not (isinstance(f, int) and f < 2):
                    act.wait_ge(S("f_ps"), f - 1)
                nc.scalar.activation(f_hi[r][:], f_raw[r][:], ACT.Copy).then_inc(S("f_hi_done"), 1)

            def early_gelu(f, r):
                act.wait_ge(S("f_ps"), f + 1)
                if not (isinstance(f, int) and f < 2):
                    act.wait_ge(S(f"f_stored{r}"), (f - r) * 8)
                nc.scalar.activation(f_act[r][:], bank[6 + r][:], ACT.Gelu).then_inc(S("f_gelu"), 1)
                act.wait_ge(S("f_gelu"), f + 1)
                act.dma_start(act_dram[bass.ts(f, 1)].rearrange("o p t -> p (o t)"), f_act[r][:])\
                   .then_inc(S(f"f_stored{r}"), 16)

            for v in range(2 * PH):
                early_high(v, v % 2)
                if v >= 1:
                    early_gelu(v - 1, (v - 1) % 2)
                act.wait_ge(S("q_ps"), v + 1)
                if v >= 2:
                    act.wait_ge(S("s_ps"), v - 1)
                nc.scalar.activation(q_sb[v % 2][:], bank[v % 2][:], ACT.Copy).then_inc(S("q_done"), 1)
                if v == 0:
                    split_w(7)
                if 4 <= v < 7:
                    split_w_part(8, v - 4)
                if 8 <= v < 11:
                    split_w_part(9, v - 8)
            for f in range(E_REST, E_GATES):
                early_high(f, f % 2)
                early_gelu(f - 1, (f - 1) % 2)
                if f == E_SLOTS - 1:
                    act.wait_ge(S("score_shift"), 1)
                    nc.scalar.activation(score[:], score[:], ACT.Exp).then_inc(S("score_exp"), 1)
            def evac_gates(i, r, q):
                n = i * (TG // PSTEP) + q
                act.wait_ge(S("gate_mm"), n + 1)
                if q == 0:
                    wait_slot(i, r)
                src = bank[2 + q % 4][:].rearrange("p (t b k) -> p t b k", t=PSTEP, k=GB)
                dst = ev[r][:, :, q * PSTEP:(q + 1) * PSTEP].rearrange("p b t k -> p t b k")
                nc.scalar.activation(dst, src, ACT.Copy).then_inc(S("ev_full"), 1)

            def wait_slot(i, r):
                if not (isinstance(i, int) and i < 2):
                    act.wait_ge(S(f"ev_stored{r}"), (i - r) * 8)

            def gate_step(i, r):
                f = i + E_GATES
                early_high(f, r)
                early_gelu(f - 1, 1 - r)
                for q in range(TG // PSTEP):
                    evac_gates(i, r, q)
                act.wait_ge(S("ev_full"), (i + 1) * (TG // PSTEP))
                act.dma_start(gates_dram[:, bass.ts(i, 1)].rearrange("p o b x -> p (o b) x"),
                              ev[r][:].rearrange("p b t k -> p b (t k)"))\
                   .then_inc(S(f"ev_stored{r}"), 16)

            for i in range(2):
                gate_step(i, i)
            with act.Fori(1, NTG // 2) as o:
                for r in range(2):
                    gate_step(o * 2 + r, r)

            def early_u_high(n, c):
                act.wait_ge(S(f"us_loaded{c}"), 16 * (n + 1))
                if n >= 2:
                    act.wait_ge(S("pu_done"), 8 * (n - 1))
                nc.scalar.activation(u_hi[:, n % 2 * GB + c], u_raw[:, c], ACT.Copy).then_inc(S("u_hi_done"), 1)

            for n in range(2):
                for c in range(GB):
                    f = E_LAST + n * GB + c
                    if f < NE:
                        early_high(f, f % 2)
                    if f <= NE:
                        early_gelu(f - 1, (f - 1) % 2)
                    early_u_high(n, c)
            for n in range(2, NSUB):
                for c in range(GB):
                    early_u_high(n, c)

            def d_high(g, c):
                e = g * GC + c
                act.wait_ge(S(f"d_loaded{c % DR}"), ((g - G0) * 2 + c // DR + 1) * 16)
                if not (isinstance(g, int) and e < NE + 2):
                    act.wait_ge(S("pd_done"), e - NE - 1)
                nc.scalar.activation(d_hi[:, c % 2], d_raw[:, c % DR], ACT.Copy).then_inc(S("d_hi_done"), 1)

            def group(g, last):
                for c in range(GC):
                    e = g * GC + c
                    act.wait_ge(S(f"u_loaded{c % DR}"), ((g - G0) * 2 + c // DR + 1) * 16)
                    if c == 0:
                        act.wait_ge(S("pu_done"), banks_before(g))
                    nc.scalar.activation(u_hi[:, c], u_raw[:, c % DR], ACT.Copy).then_inc(S("u_hi_done"), 1)
                    act.wait_ge(S("pd_done"), e - NE + 1)
                    act.wait_ge(S("w_done"), e - 1)
                    nc.scalar.activation(a_sb[:, c % 2], bank[c % 2][:], ACT.Gelu).then_inc(S("gelu_done"), 1)
                    if c < GC - 2:
                        d_high(g, c + 2)
                    elif not last:
                        d_high(g + 1, c + 2 - GC)

            d_high(G0, 0)
            d_high(G0, 1)
            group(G0, False)
            with act.Fori(G0 + 1, NG - 1) as g:
                group(g, False)
            group(NG - 1, True)
            rms(2)

        @block.vector
        def _(dve):
            done = [0]

            def link(ins):
                done[0] += 1
                ins.then_inc(S("dve_link"), 1)
                dve.wait_ge(S("dve_link"), done[0])

            V = nc.vector

            def split_w(i):
                dve.wait_ge(S("w_hi_done"), i + 1)
                V.tensor_tensor(w_lo[i % 2][:], w_raw[i % 2][:], f32(w_hi[i % 2][:]), ALU.subtract)\
                 .then_inc(S("w_lo_done"), 1)

            def rstd_of(n, b):
                i = n * TB + b
                c = slice(b, b + 1)
                dve.wait_ge(S("ssq_done"), i + 1)
                V.tensor_scalar(ms[:, c], ssq[:, c], 1.0 / D, EPS, ALU.mult, ALU.add).then_inc(S("ms_done"), 1)
                dve.wait_ge(S("root_done"), i + 1)
                link(V.reciprocal(rstd[:, c], rt[:, c]))
                link(V.tensor_tensor(nt[:, c], rstd[:, c], rstd[:, c], ALU.mult))
                link(V.tensor_tensor(nt[:, c], nt[:, c], ms[:, c], ALU.mult))
                link(V.tensor_scalar(nt[:, c], nt[:, c], -0.5, 1.5, ALU.mult, ALU.add))
                link(V.tensor_tensor(rstd[:, c], rstd[:, c], nt[:, c], ALU.mult))

            def scale_rows(n, b):
                rstd_of(n, b)
                V.tensor_scalar(xs[:, b], xt[:, b], rstd[:, b:b + 1], None, ALU.mult).then_inc(S("xs_done"), 1)

            def final_rows(b):
                rstd_of(2, b)
                if b == 0:
                    dve.wait_ge(S("nf_loaded"), 16)
                V.scalar_tensor_tensor(xt[:, b], xt[:, b], rstd[:, b:b + 1], nf[:], ALU.mult, ALU.mult)\
                 .then_inc(S("y_done"), 1)

            def evac_lo(rep, gain):
                for k in range(KC):
                    if rep == 0 and k == KC // 2:
                        dve.wait_ge(S("w_hi_done"), 1)
                        V.tensor_tensor(w_lo[0][:, k:], w_raw[0][:, k:], f32(w_hi[0][:, k:]), ALU.subtract)\
                         .then_inc(S("w_lo_done"), 1)
                    dve.wait_ge(S("h_hi_done"), rep * KC + k + 1)
                    if gain is None:
                        V.tensor_tensor(h_lo[:, k], bank[k][:], f32(h_hi[:, k]), ALU.subtract)\
                         .then_inc(S("h_lo_done"), 1)
                    else:
                        V.scalar_tensor_tensor(h_lo[:, k], bank[k][:], gain[:, k:k + 1], f32(h_hi[:, k]),
                                               ALU.mult, ALU.subtract).then_inc(S("h_lo_done"), 1)

            for b in range(TB):
                scale_rows(0, b)
            dve.wait_ge(S("wg_hi_done"), 1)
            V.tensor_tensor(wg_lo[:], wg_raw[:], f32(wg_hi[:]), ALU.subtract).then_inc(S("wg_lo_done"), 1)
            dve.wait_ge(S("w0_hi_done"), 1)
            half = slice(0, KC // 2)
            V.tensor_tensor(w_lo[0][:, half], w_raw[0][:, half], f32(w_hi[0][:, half]), ALU.subtract)\
             .then_inc(S("w0_lo_done"), 1)
            evac_lo(0, g_attn)

            dve.wait_ge(S("const_loaded"), 48)
            link(V.tensor_copy(posf[:], posi[:]))
            link(V.tensor_tensor(ang[:], posf[:].unsqueeze(2).broadcast_to([P, TB, HALF]),
                                 inv_freq.unsqueeze(1).broadcast_to([P, TB, HALF]), ALU.mult))
            link(V.tensor_scalar(trn[:], ang[:], 1.0 / TWO_PI, ROUND, ALU.mult, ALU.add))
            link(V.tensor_scalar(trn[:], trn[:], ROUND, None, ALU.subtract))
            link(V.scalar_tensor_tensor(red[:], trn[:], -PI_A, ang[:], ALU.mult, ALU.add))
            link(V.scalar_tensor_tensor(red[:], trn[:], -PI_B, red[:], ALU.mult, ALU.add))
            link(V.scalar_tensor_tensor(red[:], trn[:], -PI_C, red[:], ALU.mult, ALU.add))
            link(V.tensor_scalar(red2[:], red[:], np.pi / 2, None, ALU.add))
            link(V.tensor_scalar(trn[:], red2[:], float(np.pi), -TWO_PI, ALU.is_gt, ALU.mult))
            link(V.tensor_tensor(red2[:], red2[:], trn[:], ALU.add))
            for t in (red, red2):
                V.tensor_scalar(t[:], t[:], PI_CLAMP, -PI_CLAMP, ALU.min, ALU.max).then_inc(S("angles"), 1)


            dve.wait_ge(S("tables"), 4)
            heads = lambda ap: ap.rearrange("p (h f d) -> p h f d", h=HEADS, f=2)
            for u in range(12):
                b = u % TB
                dve.wait_ge(S("pj_done"), u + 1)
                if u >= 2:
                    dve.wait_ge(S("rope_done"), u - 1)
                ps = heads(bank[u % 4][:])
                c_b = cos2[:, b].rearrange("p f d -> p (f d)").unsqueeze(1).broadcast_to([P, HEADS, DH])
                V.tensor_tensor(rp_c[u % 2][:].rearrange("p (h d) -> p h d", h=HEADS),
                                bank[u % 4][:].rearrange("p (h d) -> p h d", h=HEADS), c_b, ALU.mult)
                for half in range(2):
                    ins = V.tensor_tensor(heads(rp_s[u % 2][:])[:, :, half], ps[:, :, 1 - half],
                                          sin2[:, b, half].unsqueeze(1).broadcast_to([P, HEADS, HALF]), ALU.mult)
                ins.then_inc(S("pj_free"), 1)
                dve.wait_ge(S("pj_free"), u + 1)
                if u >= 2:
                    dve.wait_ge(S("tT_done"), u - 1)
                V.tensor_tensor(roped[u % 2][:], rp_c[u % 2][:], rp_s[u % 2][:], ALU.add).then_inc(S("rope_done"), 1)
                if u == 1:
                    split_w(1)
                if u == 5:
                    split_w(2)
                if u == 9:
                    split_w(3)
            V.memset(kcT[:], 0.0)
            link(V.memset(vbd[:], 0.0))
            V.tensor_scalar(nsink[:], sinks, -1.0, None, ALU.mult)
            for kv in range(2):
                dve.wait_ge(S("evT"), 12 + kv)
                src = (kT[:, 1] if kv == 0 else vcT[:]).rearrange("p (c l f) -> p l f c", l=CMP_STRIDE // 2, f=2)
                emb = cmp_pos[:, kv].rearrange("p (l f) -> p l f", f=2)
                for g in range(GROUPS):
                    rows = slice(DH * g, DH * g + DH)
                    for par in range(2):
                        for part in range(2):
                            ls = slice(part * LP // 2, (part + 1) * LP // 2)
                            V.tensor_tensor(cx[kv][DH * par:DH * par + DH, ls, g],
                                            src[rows, :, par, part:part + NC],
                                            emb[rows, ls, par].unsqueeze(2).broadcast_to([DH, LP // 2, NC]),
                                            ALU.add).then_inc(S("cx_done"), 1)
            link(V.memset(hrep[:], 0.0))
            dve.wait_ge(S("gates_T"), 1)
            link(V.tensor_scalar(gexp[:], bank[1][:, 0:TB * N_GATES].rearrange("p (b g) -> p b g", b=TB),
                                 1.0, None, ALU.add))
            V.reciprocal(gates[:].rearrange("p b h k -> p b (h k)"), gexp[:]).then_inc(S("gates_ready"), 1)
            dve.wait_ge(S("gates_ready"), 1)
            split_w(4)
            four = lambda ap: ap[:, 0:4 * NC].rearrange("p (j c) -> p j c", j=4)
            dve.wait_ge(S("hid_ps"), 1)
            V.tensor_copy(hid[:, :, 0:NC], four(bank[2])).then_inc(S("hid_T_done"), 1)
            dve.wait_ge(S("hid_ps"), 2)
            V.tensor_copy(hrep[:, :, :, 0:NC], four(bank[3]).unsqueeze(2).broadcast_to([P, GROUPS * 2, 4, NC]))\
             .then_inc(S("hrep_done"), 1)
            dve.wait_ge(S("cmp_ps"), 2)
            for g in range(GROUPS):
                for j in range(HPG):
                    q = slice(CP * j, CP * j + CP)
                    V.tensor_copy(vbd[q, g, j], bank[5][q, g * DH:(g + 1) * DH]).then_inc(S("vbd_done"), 1)
            link(V.memset(c_sc[:], 0.0))

            def finish(gi):
                qb, br = gi // 3, gi % 3
                sl = slice(gi * HEADS, (gi + 1) * HEADS)
                o = bank[5 + gi % 2][:].rearrange("p (h d) -> p h d", h=HEADS)
                co = coef[:].unsqueeze(2).broadcast_to([P, HEADS, DH])
                out_a = mixed[:, qb, 0:COLS].rearrange("p (h d) -> p h d", h=HEADS)
                out_b = mixed[:, qb, COLS:2 * COLS]
                dve.wait_ge(S("exp_done"), 8 * gi + 8)
                if gi >= 1:
                    dve.wait_ge(S("o_free"), gi)
                if br == SWA:
                    dve.wait_ge(S("es_done"), qb + 1)
                    link(V.tensor_tensor(coef[:], rsum[:, sl], es[:, qb], ALU.add))
                    link(V.reciprocal(coef[:], coef[:]))
                else:
                    link(V.reciprocal(coef[:], rsum[:, sl]))
                    link(V.tensor_tensor(coef[:], coef[:], gates[:, qb, :, br], ALU.mult))
                dve.wait_ge(S("pv_done"), 8 * gi + 8)
                if br == SWA:
                    V.tensor_tensor(out_a, o, co, ALU.mult).then_inc(S("o_free"), 1)
                else:
                    V.tensor_tensor(o_tmp[:].rearrange("p (h d) -> p h d", h=HEADS), o, co, ALU.mult)\
                     .then_inc(S("o_free"), 1)
                    dve.wait_ge(S("o_free"), gi + 1)
                    dve.wait_ge(S("c_mixed"), qb + 1)
                    link(V.tensor_tensor(out_b, out_b, o_tmp[:], ALU.add))

            for s in range(len(UNITS) + 12):
                qb, in_qb = divmod(s, STEP_QB)
                if s < len(UNITS):
                    _, br, h = UNITS[s]
                    n = width(qb, br)
                    dve.wait_ge(S("s_done"), s + 1)
                    if br == SWA:
                        link(V.tensor_reduce(nmax[:, s:s + 1], bank[s % 3][:, 0:n], X_AXIS, ALU.max, negate=True))
                        V.tensor_tensor(nmax[:, s:s + 1], nmax[:, s:s + 1], nsink[:, h:h + 1], ALU.min)\
                         .then_inc(S("max_done"), 1)
                    else:
                        V.tensor_reduce(nmax[:, s:s + 1], bank[s % 3][:, 0:n], X_AXIS, ALU.max, negate=True)\
                         .then_inc(S("max_done"), 1)
                    if s in (1, 2):
                        dve.wait_ge(S("c_s"), 1)
                        for q in range(2 * s - 2, 2 * s):
                            V.tensor_tensor(
                                c_sc[:, q, :, 0:NC].rearrange("p (g j) c -> p g j c", g=GROUPS),
                                bank[6 + q // 2][:, q % 2 * 256:(q % 2 + 1) * 256]
                                .rearrange("p (j g c) -> p g j c", j=HPG, g=GROUPS)[:, :, :, 0:NC],
                                cmp_neg[:, q, 0:NC].unsqueeze(1).unsqueeze(1).broadcast_to([P, GROUPS, HPG, NC]),
                                ALU.add).then_inc(S("c_masked"), 1)
                    if s == 3:
                        cs = c_sc[:].rearrange("p q h c -> p (q h) c")[:, :, 0:NC]
                        over = lambda ap: ap[:].rearrange("p q h -> p (q h)").unsqueeze(2).broadcast_to([P, TB * HEADS, NC])
                        dve.wait_ge(S("c_masked"), TB)
                        link(V.tensor_reduce(c_max[:].rearrange("p q h -> p (q h)"), cs, X_AXIS, ALU.max))
                    if s == 4:
                        V.tensor_tensor(cs, cs, over(c_max), ALU.subtract).then_inc(S("c_shift"), 1)
                    if s in (7, 8):
                        dve.wait_ge(S("c_exp"), 1)
                        for q in range(2 * s - 14, 2 * s - 12):
                            c_q = c_sc[:, q, :, 0:NC]
                            V.tensor_tensor(c_q, c_q, cmp_vis[:, q, 0:NC].unsqueeze(1).broadcast_to([P, HEADS, NC]),
                                            ALU.mult).then_inc(S("c_p"), 1)
                    if s == 9:
                        dve.wait_ge(S("c_p"), TB)
                        link(V.tensor_reduce(c_sum[:].rearrange("p q h -> p (q h)"), cs, X_AXIS, ALU.add))
                        link(V.tensor_scalar(c_sum[:], c_sum[:], 1e-30, None, ALU.max))
                        link(V.reciprocal(c_sum[:], c_sum[:]))
                        link(V.tensor_tensor(c_coef[:], c_sum[:], gates[:, :, :, 0], ALU.mult))
                    if in_qb == 16:
                        dve.wait_ge(S("c_o"), qb + 1)
                        V.tensor_tensor(mixed[:, qb, COLS:2 * COLS].rearrange("p (h d) -> p h d", h=HEADS),
                                        bank[7][:].rearrange("p (h d) -> p h d", h=HEADS),
                                        c_coef[:, qb].unsqueeze(2).broadcast_to([P, HEADS, DH]), ALU.mult)\
                         .then_inc(S("c_mixed"), 1)
                if 2 <= s < len(UNITS) + 2 and s % 2 == 1:
                    u = s - 2
                    n = width(*UNITS[u][:2])
                    dve.wait_ge(S("pT_ps"), u + 1)
                    if u >= 3:
                        dve.wait_ge(S("pv_done"), u - 2)
                        dve.wait_ge(S("pt_done0"), (u - 3) // 2 + 1)
                    V.tensor_copy(pt[u % 3][:, 0:n], bank[4][:, 0:n]).then_inc(S("pt_done1"), 1)
                if in_qb == HEADS and qb < TB:
                    dve.wait_ge(S("max_done"), s)
                    V.tensor_tensor(es_in[:, qb], sinks, nmax[:, qb * STEP_QB:qb * STEP_QB + HEADS], ALU.add)\
                     .then_inc(S("es_in_done"), 1)
                if s >= 12 and (s - 12) % HEADS == 0 and (s - 12) // HEADS < 3 * TB:
                    finish((s - 12) // HEADS)
            V.tensor_copy(nt[:, 0:1], mixed[:, TB - 1, D - 1:D]).then_inc(S("mixed_done"), 1)
            evac_lo(1, None)
            split_w(5)
            for n in range(2 * TB):
                half, b = divmod(n, TB)
                dve.wait_ge(S("wo_ps"), n + 1)
                o = xt[:, b, half * COLS:(half + 1) * COLS]
                V.tensor_tensor(o, o, bank[n % 4][:], ALU.add).then_inc(S("x1_done"), 1)
                if n >= TB:
                    scale_rows(1, n - TB)
            evac_lo(2, g_ffn)

            LOW = -3.0e38

            def keys_of(hd):
                r = hd % 2
                for s in range(2):
                    dve.wait_ge(S("hit_done"), 2 * hd + s + 1)
                    V.tensor_reduce(key[s][:, :, hd], hit[r][s][:], X_AXIS, ALU.add).then_inc(S("key_done"), 1)

            def top16(vals, idx, src, tmp):
                for b in range(TB):
                    V.max(vals[b][:, 0:8], src[b]).then_inc(S("top_a"), 1)
                top_count[0] += TB
                for b in range(TB):
                    dve.wait_ge(S("top_a"), top_count[0] - TB + b + 1)
                    V.max_index(idx[b][:, 0:8], vals[b][:, 0:8], src[b])
                    V.match_replace(tmp[b], vals[b][:, 0:8], src[b], LOW).then_inc(S("top_b"), 1)
                for b in range(TB):
                    dve.wait_ge(S("top_b"), top_count[0] - TB + b + 1)
                    V.max(vals[b][:, 8:16], tmp[b]).then_inc(S("top_c"), 1)
                for b in range(TB):
                    dve.wait_ge(S("top_c"), top_count[0] - TB + b + 1)
                    last = V.max_index(idx[b][:, 8:16], vals[b][:, 8:16], tmp[b])
                return last

            top_count = [0]
            for hd in range(PH):
                r = hd % 2
                for s in range(2):
                    v = 2 * hd + s
                    dve.wait_ge(S("s_ps"), v + 1)
                    src = bank[2 + v % 4]
                    if v >= 2:
                        dve.wait_ge(S("s_free"), v - 1)
                    if hd >= 2:
                        dve.wait_ge(S("hit_done"), 2 * (hd - 2) + s + 1)
                    top16([tv[r][s][:, b] for b in range(TB)], [ti[r][s][:, b] for b in range(TB)],
                          [src[:, b * NK:(b + 1) * NK] for b in range(TB)],
                          [work[s][:, b] for b in range(TB)]).then_inc(S("s_free"), 1)
                dve.wait_ge(S("s_free"), 2 * hd + 2)
                for b in range(TB):
                    V.tensor_tensor(cand[:, b], tv[r][0][:, b].unsqueeze(2).broadcast_to([P, TOPK, TOPK]),
                                    tv[r][1][:, b].unsqueeze(1).broadcast_to([P, TOPK, TOPK]), ALU.add)\
                     .then_inc(S("cand_done"), 1)
                dve.wait_ge(S("cand_done"), TB * (hd + 1))
                link(top16([score[:, b, hd] for b in range(TB)], [posn[:, b] for b in range(TB)],
                           [cand[:, b].rearrange("p i j -> p (i j)") for b in range(TB)],
                           [candw[:, b] for b in range(TB)]))
                V.tensor_copy(tif[r][0][:], ti[r][0][:])
                V.tensor_copy(tif[r][1][:], ti[r][1][:])
                V.tensor_scalar(pab[r][0][:], posn[:], 4, None, ALU.logical_shift_right)
                link(V.tensor_scalar(pab[r][1][:], posn[:], TOPK - 1, None, ALU.bitwise_and))
                if hd >= 2:
                    dve.wait_ge(S("key_done"), 2 * (hd - 1))
                for s in range(2):
                    V.tensor_tensor(hit[r][s][:].rearrange("p b k r -> p (b k) r"),
                                    pab[r][s][:].rearrange("p b k -> p (b k)").unsqueeze(2)
                                    .broadcast_to([P, TB * TOPK, TOPK]),
                                    iota16.unsqueeze(1).broadcast_to([P, TB * TOPK, TOPK]), ALU.is_equal)\
                     .then_inc(S("hit_eq"), 1)
                if hd >= 1:
                    keys_of(hd - 1)
            link(V.tensor_copy(g_sum[:], score[:, :, :, 0]))
            sv = score[:].rearrange("p b h k -> p (b h) k")
            gv = g_sum[:].rearrange("p b h -> p (b h)").unsqueeze(2).broadcast_to([P, TB * PH, TOPK])
            V.tensor_tensor(sv, sv, gv, ALU.subtract).then_inc(S("score_shift"), 1)
            keys_of(PH - 1)
            dve.wait_ge(S("score_exp"), 1)
            link(V.tensor_reduce(g_sum[:].rearrange("p b h -> p (b h)"), sv, X_AXIS, ALU.add))
            link(V.reciprocal(g_sum[:], g_sum[:]))
            V.tensor_tensor(sv, sv, gv, ALU.mult).then_inc(S("gate_done"), 1)
            dve.wait_ge(S("slot_ps"), 3)
            V.tensor_copy(sl_key[0][:], bank[1][:]).then_inc(S("slot_done"), 1)
            V.tensor_copy(sl_key[1][:], bank[2][:]).then_inc(S("slot_done"), 1)
            link(V.tensor_copy(sl_g[0][:], bank[0][:]))
            link(V.tensor_tensor(sl_r[0][:], bank[0][:], sl_g[0][:], ALU.subtract))
            link(V.tensor_copy(sl_g[1][:], sl_r[0][:]))
            link(V.tensor_tensor(sl_r[1][:], sl_r[0][:], sl_g[1][:], ALU.subtract))
            link(V.tensor_copy(sl_g[2][:], sl_r[1][:]))
            dve.wait_ge(S("iota_loaded"), 16)

            def one_hots(i, r):
                if not (isinstance(i, int) and i < 2):
                    dve.wait_ge(S("gate_mm"), (i - 1) * (TG // PSTEP))
                tok = bass.ts(i, TG)
                cols = lambda t: t[:, tok].unsqueeze(1).broadcast_to([P, NK, TG])
                V.tensor_tensor(oh[r][0][:], iota_k[:], cols(sl_key[0]), ALU.is_equal).then_inc(S("oh_a"), 1)
                V.tensor_tensor(oh[r][1][:], iota_k[:], cols(sl_key[1]), ALU.is_equal)
                dve.wait_ge(S("oh_a"), i + 1)
                for j in range(3):
                    ins = V.tensor_tensor(gp[r][j][:], oh[r][0][:], cols(sl_g[j]), ALU.mult)
                ins.then_inc(S("oh_done"), 1)

            for i in range(2):
                one_hots(i, i)
            with dve.Fori(1, NTG // 2) as o:
                for r in range(2):
                    one_hots(o * 2 + r, r)

            def accumulate(before, n):
                dve.wait_ge(S("pu_done"), before + n + 1)
                o = xt[:, n // 2, (n % 2) * COLS:(n % 2 + 1) * COLS]
                V.tensor_tensor(o, o, bank[4 + n % 4][:], ALU.add).then_inc(S("acc_done"), 1)

            def early_u_low(n, c):
                e, j = n * GB + c, n % 2 * GB + c
                dve.wait_ge(S("u_hi_done"), e + 1)
                V.tensor_tensor(u_lo[:, j], u_raw[:, c], f32(u_hi[:, j]), ALU.subtract).then_inc(S("u_lo_done"), 1)

            def early_weights(n, c):
                e, j = n * GB + c, n % 2 * GB + c
                dve.wait_ge(S("gs_loaded"), 16 * (n + 1))
                dve.wait_ge(S(f"as_loaded{n % 2}"), 16 * (n // 2 + 1))
                V.tensor_tensor(a_early[:, j], a_early[:, j], g_early[:, :, c], ALU.mult).then_inc(S("w_step"), 1)
                dve.wait_ge(S("w_step"), 2 * e + 1)
                V.tensor_copy(w_e_hi[:, j], a_early[:, j]).then_inc(S("w_step"), 1)
                dve.wait_ge(S("w_step"), 2 * e + 2)
                V.tensor_tensor(w_e_lo[:, j], a_early[:, j], f32(w_e_hi[:, j]), ALU.subtract).then_inc(S("w_done"), 1)

            def d_low(g, c):
                e = (g - G0) * GC + c
                dve.wait_ge(S("d_hi_done"), e + 1)
                V.tensor_tensor(d_lo[:, c % DR], d_raw[:, c % DR], f32(d_hi[:, c % 2]), ALU.subtract)\
                 .then_inc(S("d_lo_done"), 1)

            def group(g, last):
                for c in range(GC):
                    e, b = g * GC + c, c // GB
                    dve.wait_ge(S("u_hi_done"), e + 1)
                    V.tensor_tensor(u_lo[:, c], u_raw[:, c % DR], f32(u_hi[:, c]), ALU.subtract)\
                     .then_inc(S("u_lo_done"), 1)
                    dve.wait_ge(S("gelu_done"), e - NE + 1)
                    if c % GB == 0:
                        dve.wait_ge(S(f"g_loaded{b}"), 16 * (g - G0) + 16)
                    V.tensor_tensor(a_sb[:, c % 2], a_sb[:, c % 2], g_sb[:, b, :, c % GB], ALU.mult)\
                     .then_inc(S("w_step"), 1)
                    dve.wait_ge(S("w_step"), 2 * e + 1)
                    V.tensor_copy(w_e_hi[:, c], a_sb[:, c % 2]).then_inc(S("w_step"), 1)
                    dve.wait_ge(S("w_step"), 2 * e + 2)
                    V.tensor_tensor(w_e_lo[:, c], a_sb[:, c % 2], f32(w_e_hi[:, c]), ALU.subtract)\
                     .then_inc(S("w_done"), 1)
                    if c < GC - 2:
                        d_low(g, c + 2)
                    elif not last:
                        d_low(g + 1, c + 2 - GC)
                for n in range(8):
                    accumulate(banks_before(g), n)
                    if last and n % 2 == 1:
                        final_rows(n // 2)

            for c in range(GB):
                early_u_low(0, c)
            for c in range(GB):
                early_weights(0, c)
            for n in range(NSUB):
                for c in range(GB):
                    if n + 1 < NSUB:
                        early_u_low(n + 1, c)
                if n == 0:
                    dve.wait_ge(S("f_gelu"), NE)
                for c in range(GB):
                    if n + 1 < NSUB:
                        early_weights(n + 1, c)
                    elif c < 2:
                        d_low(G0, c)
                    accumulate(8 * n, 2 * c)
                    accumulate(8 * n, 2 * c + 1)
            group(G0, False)
            with dve.Fori(G0 + 1, NG - 1) as g:
                group(g, False)
            group(NG - 1, True)

        @block.tensor
        def _(pe):
            def transposes(rep, src):
                for b in range(TB):
                    if rep != 1:
                        pe.wait_ge(S("xs_done"), (rep // 2) * TB + b + 1)
                    for k in range(KC):
                        t = nc.tensor.transpose(bank[k][:, b * P:(b + 1) * P], src[:, b, k * P:(k + 1) * P], ident)
                        if b == TB - 1:
                            t.then_inc(S("hT_ps"), 1)

            def mm3(out, a_hi, a_lo, b_hi, b_lo, n, last):
                for j, (a, b) in enumerate(((a_hi, b_hi), (a_hi, b_lo), (a_lo, b_hi))):
                    m = nc.tensor.matmul(out, a, b, start=(n == 0 and j == 0), stop=(n == last and j == 2))
                return m

            pe.wait_ge(S("cst_loaded"), 16)
            transposes(0, xs)

            def rope_T(u):
                pe.wait_ge(S("rope_done"), u + 1)
                if u >= 2:
                    pe.wait_ge(S("evT"), u - 1)
                for j in range(4):
                    t = nc.tensor.transpose(bank[4 + u % 2][:, j * P:(j + 1) * P],
                                            roped[u % 2][:, j * P:(j + 1) * P], ident)
                t.then_inc(S("tT_done"), 1)

            for u in range(16):
                n, b = divmod(u, TB)
                if b == 0 and n > 0:
                    pe.wait_ge(S("w_lo_done"), n + 1)
                if u >= 4:
                    pe.wait_ge(S("pj_free"), u - 3)
                tok = slice(b * P, (b + 1) * P)
                for k in range(KC):
                    if u == 0:
                        pe.wait_ge(S("h_lo_done"), k + 1)
                        if k == 0:
                            pe.wait_ge(S("w0_lo_done"), 1)
                        if k == KC // 2:
                            pe.wait_ge(S("w_lo_done"), 1)
                    m = mm3(bank[u % 4][:], h_hi[:, k, tok], h_lo[:, k, tok],
                            w_hi[n % 2][:, k], w_lo[n % 2][:, k], k, KC - 1)
                m.then_inc(S("pj_done"), 1)
                if 1 <= u <= 12:
                    rope_T(u - 1)
            pe.wait_ge(S("v_done"), 1)
            pe.wait_ge(S("wg_lo_done"), 1)
            for k in range(KC):
                m = mm3(bank[0][0:N_GATES], wg_hi[:, k], wg_lo[:, k], h_hi[:, k], h_lo[:, k], k, KC - 1)
            m.then_inc(S("pj_done"), 1)
            pe.wait_ge(S("v_done"), TB)
            pe.wait_ge(S("evT"), 11)
            for b in range(TB):
                t = nc.tensor.transpose(bank[4][:, b * P:(b + 1) * P], vnat[:, b, P:2 * P], ident)
            t.then_inc(S("tT_done"), 1)

            pe.wait_ge(S("gexp_done"), 1)
            for b in range(TB):
                t = nc.tensor.transpose(bank[1][:, b * N_GATES:(b + 1) * N_GATES], gexp_T[:, b * P:(b + 1) * P],
                                        ident[0:N_GATES, 0:N_GATES])
            t.then_inc(S("gates_T"), 1)

            for kv in range(2):
                pe.wait_ge(S("cx_done"), 8 * (kv + 1))
                pe.wait_ge(S("w1v_loaded" if kv else "w1k_loaded"), 16)
                for l in range(LP):
                    m = nc.tensor.matmul(bank[6 + kv][0:GROUPS * NC, 0:CMP_HIDDEN],
                                         cx[kv][:, l].rearrange("p g c -> p (g c)"), w1_sb[kv][:, l],
                                         start=(l == 0), stop=(l == LP - 1))
                m.then_inc(S("hid_done"), 1)
            for kv in range(2):
                pe.wait_ge(S("hid_act"), kv + 1)
                for hh in range(2):
                    t = nc.tensor.transpose(bank[2 + kv][:, hh * GROUPS * NC:(hh + 1) * GROUPS * NC],
                                            hid_T[kv][:, hh * P:(hh + 1) * P], ident[0:GROUPS * NC, 0:GROUPS * NC])
                t.then_inc(S("hid_ps"), 1)
            pe.wait_ge(S("hid_T_done"), 1)
            pe.wait_ge(S("w2_loaded"), 16)
            pe.wait_ge(S("evT"), 13)
            for g in range(GROUPS):
                for hh in range(2):
                    m = nc.tensor.matmul(bank[4][DH * g:DH * g + DH, 0:NC], w2_sb[:, 0, hh],
                                         hid[:, hh * 2 + g, 0:NC], start=(hh == 0), stop=(hh == 1))
            m.then_inc(S("cmp_ps"), 1)
            pe.wait_ge(S("hrep_done"), 1)
            for g in range(GROUPS):
                for hh in range(2):
                    m = nc.tensor.matmul(bank[5][:, g * DH:(g + 1) * DH],
                                         hrep[:, hh * 2 + g].rearrange("p j c -> p (j c)"),
                                         w2_sb[:, 1, hh], start=(hh == 0), stop=(hh == 1))
            m.then_inc(S("cmp_ps"), 1)

            pe.wait_ge(S("kc_done"), GROUPS)
            pe.wait_ge(S("vbd_done"), 8)
            pe.wait_ge(S("gates_ready"), 1)
            for qb in range(TB):
                for j in range(HPG):
                    c0 = (qb % 2 * HPG + j) * GROUPS * CP
                    m = nc.tensor.matmul(bank[6 + qb // 2][:, c0:c0 + GROUPS * CP],
                                         qT[:, 1, j, qb * P:(qb + 1) * P],
                                         kcT[:].rearrange("p g c -> p (g c)"), start=True, stop=True)
            m.then_inc(S("c_s"), 1)
            pe.wait_ge(S("q_moved"), 1)
            pe.wait_ge(S("q_zeroed"), 2)
            q_of = (qT, q_g1)
            for s in range(len(UNITS) + 12):
                qb, in_qb = divmod(s, STEP_QB)
                if s < len(UNITS):
                    _, br, h = UNITS[s]
                    g, j = divmod(h, HPG)
                    if s == HEADS:
                        pe.wait_ge(S("q_zeroed"), 3)
                    n = width(qb, br)
                    k0 = (qb + 1) * P - n
                    if s >= 3:
                        pe.wait_ge(S("exp_done"), s - 2)
                    nc.tensor.matmul(bank[s % 3][:, 0:n], q_of[g][:, 0 if br == SWA else 1, j, qb * P:(qb + 1) * P],
                                     kT[:, K_OF[br], k0:k0 + n], start=True, stop=False)
                    mw = n if br == SWA else P
                    nc.tensor.matmul(bank[s % 3][:, n - mw:n], ident_b, mask_b[:, 2 * P - mw:2 * P],
                                     start=False, stop=True).then_inc(S("s_done"), 1)
                if 2 <= s < len(UNITS) + 2:
                    u = s - 2
                    n = width(*UNITS[u][:2])
                    pe.wait_ge(S("exp_done"), u + 1)
                    if u >= 2:
                        pe.wait_ge(S(f"pt_done{u % 2}"), u // 2)
                    for kb in range(n // P):
                        t = nc.tensor.transpose(bank[3 + u % 2][:, kb * P:(kb + 1) * P],
                                                pr[u % 3][:, kb * P:(kb + 1) * P], ident)
                    t.then_inc(S("pT_ps"), 1)
                if 4 <= s < len(UNITS) + 4:
                    u = s - 4
                    uq, ub, uh = UNITS[u]
                    n = width(uq, ub)
                    gi = u // HEADS
                    if uh == 0 and gi >= 2:
                        pe.wait_ge(S("o_free"), gi - 1)
                    pe.wait_ge(S(f"pt_done{u % 2}"), u // 2 + 1)
                    v0 = K_OF[ub] * P + (uh // HPG) * DH
                    for kb in range(n // P):
                        tb = uq + 1 - n // P + kb
                        m = nc.tensor.matmul(bank[5 + gi % 2][:, uh * DH:(uh + 1) * DH],
                                             pt[u % 3][:, kb * P:(kb + 1) * P], vnat[:, tb, v0:v0 + DH],
                                             start=(kb == 0), stop=(kb == n // P - 1))
                    m.then_inc(S("pv_done"), 1)
                if s < len(UNITS) and in_qb == 10:
                    pe.wait_ge(S("c_p"), TB)
                    if qb >= 1:
                        pe.wait_ge(S("c_mixed"), qb)
                    for g in range(GROUPS):
                        t = nc.tensor.transpose(bank[7][:, 256 + g * P:256 + (g + 1) * P],
                                                c_sc[:, qb, g * HPG:(g + 1) * HPG].rearrange("p h c -> p (h c)"), ident)
                    t.then_inc(S("c_T"), 1)
                if s < len(UNITS) and in_qb == 13:
                    pe.wait_ge(S("c_pT_done"), qb + 1)
                    for g in range(GROUPS):
                        m = nc.tensor.matmul(bank[7][:, g * 256:(g + 1) * 256], c_pT[:, g],
                                             vbd[:, g].rearrange("p j d -> p (j d)"), start=True, stop=True)
                    m.then_inc(S("c_o"), 1)

            pe.wait_ge(S("mixed_done"), 1)
            transposes(1, mixed)
            for n in range(2 * TB):
                half, b = divmod(n, TB)
                i = TILES_IN + half
                if b == 0:
                    pe.wait_ge(S("w_lo_done"), i + 1)
                if n >= 4:
                    pe.wait_ge(S("x1_done"), n - 3)
                tok = slice(b * P, (b + 1) * P)
                for k in range(KC):
                    if n == 0:
                        pe.wait_ge(S("h_lo_done"), KC + k + 1)
                    m = mm3(bank[n % 4][:], h_hi[:, k, tok], h_lo[:, k, tok],
                            w_hi[i % 2][:, k], w_lo[i % 2][:, k], k, KC - 1)
                m.then_inc(S("wo_ps"), 1)
            pe.wait_ge(S("x1_done"), 2 * TB)
            transposes(2, xs)

            pe.wait_ge(S("sk_loaded"), 16)

            def early_score(f, r):
                pe.wait_ge(S("f_lo_done"), f + 1)
                if not (isinstance(f, int) and f < 2):
                    pe.wait_ge(S("f_gelu"), f - 1)
                for k in range(KC):
                    m = mm3(bank[6 + r][:], f_hi[r][:, k], f_lo[r][:, k], h_hi[:, k], h_lo[:, k], k, KC - 1)
                m.then_inc(S("f_ps"), 1)

            def key_scores(v):
                if v >= 4:
                    pe.wait_ge(S("s_free"), v - 3)
                pe.wait_ge(S("q_done"), v + 1)
                for b in range(TB):
                    m = nc.tensor.matmul(bank[2 + v % 4][:, b * NK:(b + 1) * NK],
                                         q_sb[v % 2][:, b * P:(b + 1) * P], sk[:, v % 2], start=True, stop=True)
                m.then_inc(S("s_ps"), 1)

            for v in range(2 * PH):
                i = TILES_IN + TILES_OUT + v // 4
                if v % 4 == 0:
                    pe.wait_ge(S("w_part_lo"), 3 * (v // 4 + 1))
                if v >= 2:
                    pe.wait_ge(S("q_done"), v - 1)
                for k in range(KC):
                    if v == 0:
                        pe.wait_ge(S("h_lo_done"), 2 * KC + k + 1)
                    c = slice((v % 4) * P, (v % 4 + 1) * P)
                    m = mm3(bank[v % 2][:], w_hi[i % 2][:, k, c], w_lo[i % 2][:, k, c],
                            h_hi[:, k], h_lo[:, k], k, KC - 1)
                m.then_inc(S("q_ps"), 1)
                if v >= 1:
                    key_scores(v - 1)
                early_score(v, v % 2)
            key_scores(2 * PH - 1)
            for f in range(E_REST, E_GATES):
                early_score(f, f % 2)
                if f == E_SLOTS:
                    pe.wait_ge(S("gate_done"), 1)
                    pe.wait_ge(S("key_done"), 2 * PH)
                    for n, src in enumerate((score, key[0], key[1])):
                        for b in range(TB):
                            t = nc.tensor.transpose(bank[n][:, b * P:(b + 1) * P],
                                                    src[:, b].rearrange("p h k -> p (h k)"), ident)
                        t.then_inc(S("slot_ps"), 1)


            def gate_rows(i, r):
                pe.wait_ge(S("oh_done"), i + 1)
                for q in range(TG // PSTEP):
                    n = i * (TG // PSTEP) + q
                    if not (isinstance(n, int) and n < 4):
                        pe.wait_ge(S("ev_full"), n - 3)
                    for tt in range(PSTEP):
                        t = q * PSTEP + tt
                        for j in range(3):
                            m = nc.tensor.matmul(bank[2 + q % 4][:, tt * NK:(tt + 1) * NK], oh[r][1][:, :, t],
                                                 gp[r][j][:, :, t], start=(j == 0), stop=(j == 2))
                    m.then_inc(S("gate_mm"), 1)

            for i in range(2):
                gate_rows(i, i)
                early_score(i + E_GATES, i)
            with pe.Fori(1, NTG // 2) as o:
                for r in range(2):
                    gate_rows(o * 2 + r, r)
                    early_score(o * 2 + r + E_GATES, r)
            for f in range(E_LAST, NE):
                early_score(f, f % 2)

            pe.wait_ge(S("ev_full"), NTG * (TG // PSTEP))

            def early_group(n, half):
                for j in range(8):
                    b, side = divmod(j, 2)
                    if not (isinstance(n, int) and n == 0 and j < 4):
                        pe.wait_ge(S("acc_done"), n * 8 + j - 3)
                    elif j == 2:
                        pe.wait_ge(S("f_gelu"), NE)
                    tok, cols = slice(b * P, (b + 1) * P), slice(side * COLS, (side + 1) * COLS)
                    for c in range(GB):
                        if j == 0:
                            pe.wait_ge(S("w_done"), n * GB + c + 1)
                        e = half * GB + c
                        m = mm3(bank[4 + j % 4][:], w_e_hi[:, e, tok], w_e_lo[:, e, tok],
                                u_hi[:, e, cols], u_lo[:, e, cols], c, GB - 1)
                    m.then_inc(S("pu_done"), 1)

            for n in range(2):
                early_group(n, n)
            with pe.Fori(1, NSUB // 2) as o:
                for r in range(2):
                    early_group(o * 2 + r, r)

            def group(g):
                first = isinstance(g, int) and g == G0
                for c in range(GC):
                    e = (g - G0) * GC + c
                    pe.wait_ge(S("d_lo_done"), e + 1)
                    if not (first and c < 2):
                        pe.wait_ge(S("gelu_done"), e - 1)
                    for k in range(KC):
                        m = mm3(bank[c % 2][:], d_hi[:, c % 2, k], d_lo[:, c % DR, k],
                                h_hi[:, k], h_lo[:, k], k, KC - 1)
                    m.then_inc(S("pd_done"), 1)
                for n in range(8):
                    b, half = divmod(n, 2)
                    pe.wait_ge(S("acc_done"), banks_before(g) + n - 3)
                    tok, cols = slice(b * P, (b + 1) * P), slice(half * COLS, (half + 1) * COLS)
                    for c in range(GC):
                        if n == 0:
                            pe.wait_ge(S("u_lo_done"), g * GC + c + 1)
                            pe.wait_ge(S("w_done"), g * GC + c + 1)
                        m = mm3(bank[4 + n % 4][:], w_e_hi[:, c, tok], w_e_lo[:, c, tok],
                                u_hi[:, c, cols], u_lo[:, c, cols], c, GC - 1)
                    m.then_inc(S("pu_done"), 1)

            group(G0)
            with pe.Fori(G0 + 1, NG) as g:
                group(g)


def constants():
    c = np.zeros((P, 432), np.float32)
    c[:, 0:P] = np.eye(P)
    t = np.arange(T).reshape(TB, P).T
    vis = np.zeros((P, TB, CP), np.float32)
    vis[:, :, :NC] = (np.arange(NC) * CMP_STRIDE + CMP_LEN - 1)[None, None] <= t[:, :, None]
    c[:, 128:256] = np.where(vis > 0, 0.0, NEG).reshape(P, -1)
    c[:, 256:384] = vis.reshape(P, -1)
    c[:, 384:416] = np.float32(10000.0) ** (-np.arange(HALF, dtype=np.float32) / np.float32(HALF))
    c[:, 416:432] = np.arange(TOPK)
    b = np.zeros((P, 384 + NK * TG), np.dtype("bfloat16"))
    b[:, 0:P] = np.eye(P)
    q, k = np.arange(P)[:, None], np.arange(P)[None]
    b[:, P:2 * P] = np.where(k > q, 0.0, NEG)
    b[:, 2 * P:3 * P] = np.where(k <= q, 0.0, NEG)
    b[:, 384:] = np.repeat(np.arange(NK), TG)[None]
    return c, b


def kernel(x, positions, norm_attn, w_in, attn_sinks, cmp_k_pos, cmp_k_w1, cmp_k_w2, cmp_v_pos, cmp_v_w1,
           cmp_v_w2, w_out, norm_ffn, peer_w_query, peer_sub_keys_1, peer_sub_keys_2, peer_expert_down,
           peer_expert_up, norm_f):
    import concourse.bacc as bacc
    from concourse.bass_utils import run_bass_kernel_spmd

    a = lambda v: np.asarray(v)[0]
    kw = HEADS // HPG * DH
    w = a(w_in)
    sizes = [HEADS * DH, kw, kw, HEADS * DH] + [kw] * 6 + [N_GATES]
    qa, ka, va, qb, kc, vc, ks, vs, kw_, vw, gl = np.split(w, np.cumsum(sizes)[:-1], axis=1)
    pairs = lambda q: q.reshape(D, GROUPS, HPG, DH).transpose(0, 2, 1, 3).reshape(D, HEADS * DH)
    tiles = [pairs(qa), pairs(qb), np.concatenate([ka, kc, ks, kw_], 1), np.concatenate([va, vc, vs, vw], 1)]
    for m in (a(w_out), a(peer_w_query)):
        tiles += [m[:, c:c + COLS] for c in range(0, m.shape[1], COLS)]
    chunked = lambda m: m.reshape(KC, P, -1).transpose(1, 0, 2).reshape(P, -1)
    params = np.zeros((P, 96), np.float32)
    params[:, 0:8] = a(norm_attn).reshape(KC, P).T
    params[:, 8:16] = a(norm_ffn).reshape(KC, P).T
    params[:, 16:24] = a(attn_sinks)[None]
    for n, e in enumerate((a(cmp_k_pos), a(cmp_v_pos))):
        params[:, 32 + 32 * n:64 + 32 * n] = np.concatenate([e.T, e.T], 0)
    w1 = lambda m: a(m).reshape(LP, P, CMP_HIDDEN).transpose(1, 0, 2).reshape(P, -1)
    w2 = lambda m: a(m).reshape(2, P, DH).transpose(1, 0, 2).reshape(P, -1)
    c, b = constants()
    arrays = {
        "x_in": a(x), "pos": np.asarray(positions)[0].reshape(TB, P).T, "params": params, "consts": c, "consts_b": b,
        "wts": np.stack([chunked(t) for t in tiles]), "wgate": chunked(gl),
        "w1": np.stack([w1(cmp_k_w1), w1(cmp_v_w1)]), "w2": np.concatenate([w2(cmp_k_w2), w2(cmp_v_w2)], 1),
        "subkeys": np.concatenate([a(peer_sub_keys_1).T, a(peer_sub_keys_2).T], 1),
        "normf": np.asarray(norm_f).reshape(1, D),
        "down": a(peer_expert_down).reshape(NK, P, KC, P).transpose(0, 3, 2, 1).reshape(NK, P, KC * P),
        "up": a(peer_expert_up).reshape(NK, P, D),
    }
    arrays = {k: np.ascontiguousarray(v) for k, v in arrays.items()}
    nc = bacc.Bacc("TRN2", target_bir_lowering=False, num_devices=1)
    ins = [nc.dram_tensor(k, v.shape, mybir.dt.from_np(v.dtype), kind="ExternalInput").ap() for k, v in arrays.items()]
    y = nc.dram_tensor("y", (T, D), F32, kind="ExternalOutput").ap()
    build(nc, *ins, y)
    r = run_bass_kernel_spmd(nc, [arrays], core_ids=[0])
    return r.results[0]["y"].reshape(1, T, D)
```
